# Optimizing a Trainium2 kernel written in Bass

```python
import math
import jax
import jax.numpy as jnp
from jax import lax
import numpy as np

D_MODEL = 1024
BATCH = 1
SEQ = 2048
DEPTH = 1

N_MIXERS = 4
NORM_EPS = 1e-6

SSM_EXPAND = 2
SSM_D_INNER = SSM_EXPAND * D_MODEL
SSM_HEAD_DIM = 64
SSM_N_HEADS = SSM_D_INNER // SSM_HEAD_DIM
SSM_N_GROUPS = 8
SSM_HEADS_PER_GROUP = SSM_N_HEADS // SSM_N_GROUPS
SSM_D_STATE = 128
SSM_CONV = 4
SSM_CHUNK = 128
SSM_CONV_DIM = SSM_D_INNER + 2 * SSM_N_GROUPS * SSM_D_STATE
SSM_IN_DIM = SSM_D_INNER + SSM_CONV_DIM + SSM_N_HEADS

RWKV_HEAD_DIM = 64
RWKV_N_HEADS = D_MODEL // RWKV_HEAD_DIM
RWKV_DECAY_LORA = 64
RWKV_AAA_LORA = 64
RWKV_GATE_LORA = 160
RWKV_LN_EPS = 64e-5

RET_N_HEADS = 4
RET_QK_DIM = D_MODEL // RET_N_HEADS
RET_V_DIM = 2 * D_MODEL // RET_N_HEADS
RET_CHUNK = 128
RET_IN_DIM = 2 * D_MODEL + 4 * D_MODEL

ATT_GROUPS = ((128, 1), (512, 4), (2048, 16))
ATT_HEADS_PER_GROUP = 8
ATT_HEAD_DIM = 128
ATT_BLOCK = 128
ATT_N_HEADS = len(ATT_GROUPS) * ATT_HEADS_PER_GROUP
ATT_IN_DIM = 3 * ATT_N_HEADS * ATT_HEAD_DIM
ATT_OUT_DIM = ATT_HEADS_PER_GROUP * ATT_HEAD_DIM

MOE_GROUPS = 4
MOE_EXPERTS_PER_GROUP = 8
MOE_EXPERTS = MOE_GROUPS * MOE_EXPERTS_PER_GROUP
MOE_TOP_K = 2
MOE_D_FF = 512
MOE_BLOCK = 128

kernel_name = "hybrid_ssd_rwkv7_retnet_dilated_hmoe"

def rms_norm(x, w):
    xf = x.astype(jnp.float32)
    y = xf * lax.rsqrt(jnp.mean(xf * xf, axis=-1, keepdims=True) + NORM_EPS)
    return (y * w.astype(jnp.float32)).astype(x.dtype)

def modulate(h, shift, scale):
    return h * (1 + scale[:, None, :]) + shift[:, None, :]

def alibi_slopes(n):
    return jnp.exp2(-8.0 * jnp.arange(1, n + 1, dtype=jnp.float32) / n)

def mamba2_ssd(h, in_w, conv_w, conv_b, dt_bias, a_log, d_skip, norm_w, out_w):
    B, T, _ = h.shape
    G, HG, P, N, Q = SSM_N_GROUPS, SSM_HEADS_PER_GROUP, SSM_HEAD_DIM, SSM_D_STATE, SSM_CHUNK
    nc = T // Q
    f32 = jnp.float32
    z, xbc, dt = jnp.split(h @ in_w, [SSM_D_INNER, SSM_D_INNER + SSM_CONV_DIM], axis=-1)
    xbc = lax.conv_general_dilated(xbc, conv_w[:, None, :], window_strides=(1,),
                                   padding=[(SSM_CONV - 1, 0)],
                                   dimension_numbers=("NWC", "WIO", "NWC"),
                                   feature_group_count=SSM_CONV_DIM)
    xbc = jax.nn.silu(xbc + conv_b)
    xs, bm, cm = jnp.split(xbc, [SSM_D_INNER, SSM_D_INNER + G * N], axis=-1)
    xs = xs.astype(f32).reshape(B, nc, Q, G, HG, P)
    bm = bm.astype(f32).reshape(B, nc, Q, G, N)
    cm = cm.astype(f32).reshape(B, nc, Q, G, N)
    dt = jax.nn.softplus(dt.astype(f32) + dt_bias.astype(f32)).reshape(B, nc, Q, G, HG)
    a = -jnp.exp(a_log.astype(f32)).reshape(G, HG)
    acum = jnp.cumsum(dt * a, axis=2)
    xdt = xs * dt[..., None]
    causal = jnp.tril(jnp.ones((Q, Q), bool))[:, :, None, None]
    seg = acum[:, :, :, None] - acum[:, :, None, :]
    lmat = jnp.exp(jnp.where(causal, seg, -jnp.inf))
    cb = jnp.einsum("bcign,bcjgn->bcijg", cm, bm)
    y_diag = jnp.einsum("bcijg,bcijgh,bcjghp->bcighp", cb, lmat, xdt)
    decay_end = jnp.exp(acum[:, :, -1:] - acum)
    states = jnp.einsum("bcjgn,bcjgh,bcjghp->bcghpn", bm, decay_end, xdt)
    chunk_decay = jnp.exp(acum[:, :, -1])

    def step(state, inp):
        st, cdec, c_c, eacum = inp
        y = jnp.einsum("bign,bghpn,bigh->bighp", c_c, state, eacum)
        return state * cdec[..., None, None] + st, y

    init = jnp.zeros((B, G, HG, P, N), f32)
    _, y_off = lax.scan(step, init, (jnp.moveaxis(states, 1, 0), jnp.moveaxis(chunk_decay, 1, 0),
                                     jnp.moveaxis(cm, 1, 0), jnp.moveaxis(jnp.exp(acum), 1, 0)))
    y = y_diag + jnp.moveaxis(y_off, 0, 1) + xs * d_skip.astype(f32).reshape(G, HG, 1)
    gsz = SSM_D_INNER // G
    y = y.reshape(B, T, G, gsz) * jax.nn.silu(z.astype(f32)).reshape(B, T, G, gsz)
    y = y * lax.rsqrt(jnp.mean(y * y, axis=-1, keepdims=True) + NORM_EPS)
    y = y.reshape(B, T, SSM_D_INNER) * norm_w.astype(f32)
    return y.astype(h.dtype) @ out_w

def rwkv7_time_mix(h, mix, rkv_w, w0, w1, w2, a0, a1, a2, g1, g2, k_k, k_a, r_k, ln_w, ln_b, out_w):
    B, T, D = h.shape
    H, N = RWKV_N_HEADS, RWKV_HEAD_DIM
    f32 = jnp.float32
    xx = jnp.pad(h, ((0, 0), (1, 0), (0, 0)))[:, :-1] - h
    xr, xw, xk, xv, xa, xg = [h + xx * mix[j] for j in range(6)]
    r, k, v = jnp.einsum("jbtd,jde->jbte", jnp.stack([xr, xk, xv]), rkv_w)
    w_log = -jax.nn.softplus(-(w0 + jnp.tanh(xw @ w1) @ w2)) - 0.5
    decay = jnp.exp(-jnp.exp(w_log.astype(f32)))
    a = jax.nn.sigmoid(a0 + (xa @ a1) @ a2)
    g = jax.nn.sigmoid(xg @ g1) @ g2
    kk = (k * k_k).astype(f32).reshape(B, T, H, N)
    kk = kk / jnp.maximum(jnp.sqrt(jnp.sum(kk * kk, -1, keepdims=True)), 1e-12)
    k = k * (1 + (a - 1) * k_a)
    r4 = r.astype(f32).reshape(B, T, H, N)
    k4 = k.astype(f32).reshape(B, T, H, N)
    v4 = v.astype(f32).reshape(B, T, H, N)
    a4 = a.astype(f32).reshape(B, T, H, N)
    w4 = decay.reshape(B, T, H, N)
    a_in = -kk
    b_in = kk * a4

    def step(S, inp):
        r_t, w_t, k_t, v_t, a_t, b_t = inp
        sa = jnp.einsum("bhvk,bhk->bhv", S, a_t)
        S = S * w_t[:, :, None, :] + sa[..., None] * b_t[:, :, None, :] + v_t[..., None] * k_t[:, :, None, :]
        return S, jnp.einsum("bhvk,bhk->bhv", S, r_t)

    tm = lambda t: jnp.moveaxis(t, 1, 0)
    _, o = lax.scan(step, jnp.zeros((B, H, N, N), f32),
                    (tm(r4), tm(w4), tm(k4), tm(v4), tm(a_in), tm(b_in)))
    o = jnp.moveaxis(o, 0, 1)
    mu = jnp.mean(o, -1, keepdims=True)
    var = jnp.mean((o - mu) ** 2, -1, keepdims=True)
    o = ((o - mu) * lax.rsqrt(var + RWKV_LN_EPS)).reshape(B, T, D) * ln_w.astype(f32) + ln_b.astype(f32)
    bonus = jnp.sum(r4 * k4 * r_k.astype(f32), -1, keepdims=True) * v4
    o = o + bonus.reshape(B, T, D)
    return (o.astype(h.dtype) * g) @ out_w

def multiscale_retention(h, in_w, out_w):
    B, T, D = h.shape
    H, DK, DV, Q = RET_N_HEADS, RET_QK_DIM, RET_V_DIM, RET_CHUNK
    nc = T // Q
    f32 = jnp.float32
    q, k, v, g = jnp.split(h @ in_w, [D, 2 * D, 4 * D], axis=-1)
    q = q.astype(f32).reshape(B, nc, Q, H, DK)
    k = (k.astype(f32) * DK ** -0.5).reshape(B, nc, Q, H, DK)
    v = v.astype(f32).reshape(B, nc, Q, H, DV)
    log_gamma = jnp.log(1 - jnp.exp2(-5.0 - jnp.arange(H, dtype=f32)))
    idx = jnp.arange(Q)
    rel = idx[:, None] - idx[None, :]
    inner_decay = jnp.where(rel >= 0, jnp.exp(jnp.maximum(rel, 0).astype(f32) * log_gamma[:, None, None]), 0.0)
    scores = jnp.einsum("bcihd,bcjhd->bchij", q, k) * inner_decay
    inner = jnp.einsum("bchij,bcjhe->bcihe", scores, v)
    q_decay = jnp.exp((idx + 1).astype(f32)[:, None] * log_gamma)
    k_decay = jnp.exp((Q - 1 - idx).astype(f32)[:, None] * log_gamma)
    chunk_decay = jnp.exp(Q * log_gamma)

    def step(R, inp):
        qc, kc, vc = inp
        cross = jnp.einsum("bihd,bhde->bihe", qc * q_decay[:, :, None], R)
        R = R * chunk_decay[:, None, None] + jnp.einsum("bjhd,bjhe->bhde", kc * k_decay[:, :, None], vc)
        return R, cross

    _, cross = lax.scan(step, jnp.zeros((B, H, DK, DV), f32),
                        (jnp.moveaxis(q, 1, 0), jnp.moveaxis(k, 1, 0), jnp.moveaxis(v, 1, 0)))
    o = (inner + jnp.moveaxis(cross, 0, 1)).reshape(B, T, H, DV)
    o = o * lax.rsqrt(jnp.mean(o * o, -1, keepdims=True) + NORM_EPS)
    o = jax.nn.silu(g.astype(f32)) * o.reshape(B, T, H * DV)
    return o.astype(h.dtype) @ out_w

def dilated_group_attention(q, k, v, window, dil, slopes):
    B, T, H, E = q.shape
    W = ATT_BLOCK
    span = window // dil
    Ls = T // dil
    nb = -(-Ls // W)
    Lp = nb * W
    f32 = jnp.float32

    def to_blocks(a):
        a = a.reshape(B, Ls, dil, H, E).transpose(0, 2, 1, 3, 4)
        a = jnp.pad(a, ((0, 0), (0, 0), (0, Lp - Ls), (0, 0), (0, 0)))
        return a.astype(f32).reshape(B, dil, nb, W, H, E)

    def with_prev(a):
        prev = jnp.pad(a, ((0, 0), (0, 0), (1, 0), (0, 0), (0, 0), (0, 0)))[:, :, :-1]
        return jnp.concatenate([prev, a], axis=3)

    qb = to_blocks(q)
    kw = with_prev(to_blocks(k))
    vw = with_prev(to_blocks(v))
    s = jnp.einsum("brnqhe,brnkhe->brnhqk", qb, kw) * E ** -0.5
    delta = W + jnp.arange(W)[:, None] - jnp.arange(2 * W)[None, :]
    band = (delta >= 0) & (delta <= span)
    key_exists = (jnp.arange(nb)[:, None] > 0) | (jnp.arange(2 * W)[None, :] >= W)
    mask = band[None, :, :] & key_exists[:, None, :]
    bias = -slopes[:, None, None] * (dil * delta).astype(f32)
    s = jnp.where(mask[:, None], s + bias, -jnp.inf)
    m = jnp.max(s, axis=-1, keepdims=True)
    e = jnp.exp(s - m)
    den = jnp.sum(e, axis=-1, keepdims=True)
    o = jnp.einsum("brnhqk,brnkhe->brnqhe", e / den, vw)
    lse = jnp.moveaxis((m + jnp.log(den))[..., 0], 3, 4)
    o = o.reshape(B, dil, Lp, H, E)[:, :, :Ls].transpose(0, 2, 1, 3, 4).reshape(B, T, H, E)
    lse = lse.reshape(B, dil, Lp, H)[:, :, :Ls].transpose(0, 2, 1, 3).reshape(B, T, H)
    return o, lse

def dilated_attention(h, in_w, out_w):
    B, T, _ = h.shape
    G, HG, E = len(ATT_GROUPS), ATT_HEADS_PER_GROUP, ATT_HEAD_DIM
    qkv = (h @ in_w).reshape(B, T, 3, G, HG, E)
    slopes = alibi_slopes(G * HG).reshape(G, HG)
    outs, lses = [], []
    for gi, (window, dil) in enumerate(ATT_GROUPS):
        o, lse = dilated_group_attention(qkv[:, :, 0, gi], qkv[:, :, 1, gi], qkv[:, :, 2, gi],
                                         window, dil, slopes[gi])
        outs.append(o)
        lses.append(lse)
    wts = jax.nn.softmax(jnp.stack(lses), axis=0)
    o = jnp.sum(wts[..., None] * jnp.stack(outs), axis=0).reshape(B, T, HG * E)
    return o.astype(h.dtype) @ out_w

def hierarchical_moe(h, group_w, group_b, expert_w, expert_b, w1, w3, w2):
    B, T, D = h.shape
    N = B * T
    E, EPG, K, BLK = MOE_EXPERTS, MOE_EXPERTS_PER_GROUP, MOE_TOP_K, MOE_BLOCK
    f32 = jnp.float32
    xt = h.reshape(N, D)
    g_logits = (xt @ group_w + group_b).astype(f32)
    g_prob = jax.nn.softmax(g_logits, axis=-1)
    g_idx = jnp.argmax(g_logits, axis=-1)
    g_top = jnp.take_along_axis(g_prob, g_idx[:, None], axis=-1)
    e_logits = (xt @ expert_w + expert_b).astype(f32).reshape(N, MOE_GROUPS, EPG)
    e_in_group = jnp.take_along_axis(e_logits, g_idx[:, None, None], axis=1)[:, 0]
    top_vals, top_idx = lax.top_k(e_in_group, K)
    gate = g_top * jax.nn.softmax(top_vals, axis=-1)
    flat_e = (g_idx[:, None] * EPG + top_idx).reshape(-1)
    flat_gate = gate.reshape(-1)
    flat_tok = jnp.repeat(jnp.arange(N), K)
    S = N * K
    order = jnp.argsort(flat_e)
    se = flat_e[order]
    counts = jnp.bincount(flat_e, length=E)
    starts = jnp.cumsum(counts) - counts
    padded = (counts + BLK - 1) // BLK * BLK
    pends = jnp.cumsum(padded)
    pstarts = pends - padded
    dest = pstarts[se] + jnp.arange(S) - starts[se]
    R = -(-S // BLK) * BLK + E * BLK
    row_tok = jnp.full((R,), N, jnp.int32).at[dest].set(flat_tok[order].astype(jnp.int32))
    row_gate = jnp.zeros((R,), f32).at[dest].set(flat_gate[order])
    nblk = R // BLK
    blk_e = jnp.minimum(jnp.searchsorted(pends, jnp.arange(nblk) * BLK, side="right"), E - 1)
    xpad = jnp.concatenate([xt, jnp.zeros((1, D), xt.dtype)], axis=0)
    xb = xpad[row_tok].reshape(nblk, BLK, D)

    def expert_block(args):
        xblk, e = args
        return (jax.nn.silu(xblk @ w1[e]) * (xblk @ w3[e])) @ w2[e]

    yb = lax.map(expert_block, (xb, blk_e)).reshape(R, D)
    y = yb * row_gate[:, None].astype(yb.dtype)
    out = jnp.zeros((N + 1, D), y.dtype).at[row_tok].add(y)[:N]
    return out.reshape(B, T, D)

def setup_inputs(seed: int = 0) -> dict:
    key = jax.random.key(seed)
    ks = iter(jax.random.split(key, 64))
    D = D_MODEL

    def nrm(shape, scale):
        return jax.random.normal(next(ks), shape, jnp.float32) * scale

    def unif(shape, lo, hi):
        return jax.random.uniform(next(ks), shape, jnp.float32, lo, hi)

    n_a, n_b, n_c, n_d = [len(range(m, DEPTH, N_MIXERS)) for m in range(N_MIXERS)]
    dt0 = jnp.exp(unif((n_a, SSM_N_HEADS), math.log(1e-3), math.log(1e-1)))
    return {
        "x": nrm((BATCH, SEQ, D), 1.0),
        "c": nrm((BATCH, D), 1.0),
        "ada_w": nrm((DEPTH, D, 6 * D), 0.5 * D ** -0.5),
        "ada_b": nrm((DEPTH, 6 * D), 0.02),
        "norm_mix_w": 1.0 + nrm((DEPTH, D), 0.02),
        "norm_ffn_w": 1.0 + nrm((DEPTH, D), 0.02),
        "ssm_in_w": nrm((n_a, D, SSM_IN_DIM), D ** -0.5),
        "ssm_conv_w": nrm((n_a, SSM_CONV, SSM_CONV_DIM), SSM_CONV ** -0.5),
        "ssm_conv_b": nrm((n_a, SSM_CONV_DIM), 0.02),
        "ssm_dt_bias": dt0 + jnp.log(-jnp.expm1(-dt0)),
        "ssm_a_log": jnp.log(unif((n_a, SSM_N_HEADS), 1.0, 16.0)),
        "ssm_d": 1.0 + nrm((n_a, SSM_N_HEADS), 0.1),
        "ssm_norm_w": 1.0 + nrm((n_a, SSM_D_INNER), 0.02),
        "ssm_out_w": nrm((n_a, SSM_D_INNER, D), SSM_D_INNER ** -0.5),
        "rwkv_mix": unif((n_b, 6, D), 0.0, 1.0),
        "rwkv_rkv_w": nrm((n_b, 3, D, D), D ** -0.5),
        "rwkv_w0": unif((n_b, D), -6.0, -1.0),
        "rwkv_w1": nrm((n_b, D, RWKV_DECAY_LORA), D ** -0.5),
        "rwkv_w2": nrm((n_b, RWKV_DECAY_LORA, D), 0.1 * RWKV_DECAY_LORA ** -0.5),
        "rwkv_a0": nrm((n_b, D), 0.1),
        "rwkv_a1": nrm((n_b, D, RWKV_AAA_LORA), D ** -0.5),
        "rwkv_a2": nrm((n_b, RWKV_AAA_LORA, D), 0.1 * RWKV_AAA_LORA ** -0.5),
        "rwkv_g1": nrm((n_b, D, RWKV_GATE_LORA), D ** -0.5),
        "rwkv_g2": nrm((n_b, RWKV_GATE_LORA, D), RWKV_GATE_LORA ** -0.5),
        "rwkv_k_k": 0.85 + nrm((n_b, D), 0.05),
        "rwkv_k_a": 1.0 + nrm((n_b, D), 0.05),
        "rwkv_r_k": nrm((n_b, RWKV_N_HEADS, RWKV_HEAD_DIM), 0.1),
        "rwkv_ln_w": 1.0 + nrm((n_b, D), 0.02),
        "rwkv_ln_b": nrm((n_b, D), 0.02),
        "rwkv_out_w": nrm((n_b, D, D), D ** -0.5),
        "ret_in_w": nrm((n_c, D, RET_IN_DIM), D ** -0.5),
        "ret_out_w": nrm((n_c, 2 * D, D), (2 * D) ** -0.5),
        "att_in_w": nrm((n_d, D, ATT_IN_DIM), D ** -0.5),
        "att_out_w": nrm((n_d, ATT_OUT_DIM, D), ATT_OUT_DIM ** -0.5),
        "moe_group_w": nrm((DEPTH, D, MOE_GROUPS), D ** -0.5),
        "moe_group_b": nrm((DEPTH, MOE_GROUPS), 0.01),
        "moe_expert_w": nrm((DEPTH, D, MOE_EXPERTS), D ** -0.5),
        "moe_expert_b": nrm((DEPTH, MOE_EXPERTS), 0.01),
        "moe_w1": nrm((DEPTH, MOE_EXPERTS, D, MOE_D_FF), D ** -0.5),
        "moe_w3": nrm((DEPTH, MOE_EXPERTS, D, MOE_D_FF), D ** -0.5),
        "moe_w2": nrm((DEPTH, MOE_EXPERTS, MOE_D_FF, D), MOE_D_FF ** -0.5),
        "final_norm_w": 1.0 + nrm((D,), 0.02),
    }

def reference(x, c, ada_w, ada_b, norm_mix_w, norm_ffn_w,
              ssm_in_w, ssm_conv_w, ssm_conv_b, ssm_dt_bias, ssm_a_log, ssm_d, ssm_norm_w, ssm_out_w,
              rwkv_mix, rwkv_rkv_w, rwkv_w0, rwkv_w1, rwkv_w2, rwkv_a0, rwkv_a1, rwkv_a2,
              rwkv_g1, rwkv_g2, rwkv_k_k, rwkv_k_a, rwkv_r_k, rwkv_ln_w, rwkv_ln_b, rwkv_out_w,
              ret_in_w, ret_out_w, att_in_w, att_out_w,
              moe_group_w, moe_group_b, moe_expert_w, moe_expert_b, moe_w1, moe_w3, moe_w2,
              final_norm_w):
    cs = jax.nn.silu(c)
    for i in range(DEPTH):
        mod = cs @ ada_w[i] + ada_b[i]
        sh1, sc1, gt1, sh2, sc2, gt2 = jnp.split(mod, 6, axis=-1)
        hm = modulate(rms_norm(x, norm_mix_w[i]), sh1, sc1)
        kind, j = i % N_MIXERS, i // N_MIXERS
        if kind == 0:
            y = mamba2_ssd(hm, ssm_in_w[j], ssm_conv_w[j], ssm_conv_b[j], ssm_dt_bias[j],
                           ssm_a_log[j], ssm_d[j], ssm_norm_w[j], ssm_out_w[j])
        elif kind == 1:
            y = rwkv7_time_mix(hm, rwkv_mix[j], rwkv_rkv_w[j], rwkv_w0[j], rwkv_w1[j], rwkv_w2[j],
                               rwkv_a0[j], rwkv_a1[j], rwkv_a2[j], rwkv_g1[j], rwkv_g2[j],
                               rwkv_k_k[j], rwkv_k_a[j], rwkv_r_k[j], rwkv_ln_w[j], rwkv_ln_b[j],
                               rwkv_out_w[j])
        elif kind == 2:
            y = multiscale_retention(hm, ret_in_w[j], ret_out_w[j])
        else:
            y = dilated_attention(hm, att_in_w[j], att_out_w[j])
        x = x + gt1[:, None, :] * y
        hf = modulate(rms_norm(x, norm_ffn_w[i]), sh2, sc2)
        x = x + gt2[:, None, :] * hierarchical_moe(hf, moe_group_w[i], moe_group_b[i], moe_expert_w[i],
                                                    moe_expert_b[i], moe_w1[i], moe_w3[i], moe_w2[i])
    return rms_norm(x, final_norm_w)


_drawn_inputs = setup_inputs


def setup_inputs(seed=0):
    import zlib

    import numpy as np

    out = dict(_drawn_inputs(seed))
    spreads = {}
    factors = {'norm_mix_w': 5.058,
     'norm_ffn_w': 4.535,
     'ssm_conv_b': 5.113,
     'ssm_d': 10.737,
     'ssm_norm_w': 6.719,
     'moe_group_b': 8.0,
     'moe_expert_b': 8.0,
     'final_norm_w': 8.149}
    for name, (base, spread) in spreads.items():
        noise = np.random.default_rng([zlib.crc32(name.encode()), seed]).standard_normal(out[name].shape)
        drawn = base * np.exp(spread * noise) if base else spread * noise
        out[name] = jnp.asarray(drawn.astype(out[name].dtype))
    for name, factor in factors.items():
        out[name] = (out[name] * factor).astype(out[name].dtype)
    return out
```

```python
from contextlib import ExitStack

import concourse.bass as bass
from concourse import mybir

F32 = mybir.dt.float32
F32R = mybir.dt.float32r
BF16 = mybir.dt.bfloat16
I32 = mybir.dt.int32
U32 = mybir.dt.uint32
ALU = mybir.AluOpType
ACT = mybir.ActivationFunctionType
AX = mybir.AxisListType.X

P = 128
D = 1024
KD = D // P
SEQ = 2048
TILES = SEQ // P
HALVES = 2
HT = TILES // HALVES
HTOK = HT * P
EPS = 1e-6

DI = 2048
G = 8
GW = DI // G
HG = 4
HEADS = G * HG
PD = 64
N = 128
CONV_DIM = DI + 2 * G * N
CB = CONV_DIM // P
TAPS = 4
KI = DI // P
SUP = 512
CS = SUP // P
PIECES = 6

GROUPS = 4
EPG = 8
EXPERTS = GROUPS * EPG
FF = 512
KF = FF // P
REGION = SEQ
BIG = 1e30


def semaphores(nc, ctx, phase):
    taken = []

    def take(name):
        taken.append(nc.alloc_semaphore(phase + name))
        return taken[-1]

    def give_back():
        nc.clear_and_free_semaphores(taken)
        nc.all_engine_barrier()

    ctx.callback(give_back)
    return take


class Steps:

    def __init__(self, eng, sem, base=0):
        self.eng, self.sem, self.base, self.n = eng, sem, base, 0

    def add(self, ins):
        ins.then_inc(self.sem, 1)
        self.n += 1

    def settle(self):
        self.eng.wait_ge(self.sem, self.base + self.n)


def mod_phase(nc, c, ada_w, ada_b, norm_mix_w, norm_ffn_w, conv_w, conv_b, xs, K):
    NV = KD + 6 * KD + 2 * KD + CB
    with ExitStack() as ctx:
        sb = lambda n, s, d=F32: ctx.enter_context(nc.sbuf_tensor(n, s, d))
        sem = semaphores(nc, ctx, "mod_")
        W = [sb(f"ada_w{i}", [P, KD, D]) for i in range(2)]
        vrows = sb("vrows", [NV, P])
        trows = sb("trows", [P, P])
        vcols = sb("vcols", [P, NV])
        cs = sb("cs", [P, KD])
        zero = sb("zero", [P, D])
        ps = ctx.enter_context(nc.psum_tensor("ps_mod", [P, 512], F32))
        pv = ctx.enter_context(nc.psum_tensor("ps_vec", [P, 512], F32))
        rows_loaded, w_loaded = sem("rows_loaded"), [sem("w_loaded0"), sem("w_loaded1")]
        turned, cols_ready, cs_ready = sem("turned"), sem("cols_ready"), sem("cs_ready")
        mod_done, consts_ready, psteps, vsteps = sem("mod_done"), sem("consts_ready"), sem("psteps"), sem("vsteps")
        zero_ready, zero_stored = sem("zero_ready"), sem("zero_stored")
        ident, upper = K["ident"], K["upper"]
        mod = K["mod"]
        block = ctx.enter_context(nc.Block())

        @block.sync
        def _(sp):
            r = 0
            for src in (c, ada_b, norm_mix_w, norm_ffn_w, conv_b):
                src = src.rearrange("o (k p) -> (o k) p", p=P)
                sp.dma_start(vrows[r:r + src.shape[0], :], src).then_inc(rows_loaded, 16)
                r += src.shape[0]
            sp.dma_start(trows[:], conv_w[0].rearrange("t (b p) -> (t b) p", p=P)).then_inc(rows_loaded, 16)
            for j in range(6):
                if j >= 2:
                    sp.wait_ge(mod_done, j - 1)
                sp.dma_start(W[j % 2][:], ada_w[0, :, j * D:(j + 1) * D].rearrange("(k p) n -> p k n", p=P)
                             ).then_inc(w_loaded[j % 2], 16)
            sp.wait_ge(zero_ready, 1)
            with sp.Fori(0, EXPERTS) as e:
                sp.dma_start(xs[bass.ds(e * REGION, P), :], zero[:]).then_inc(zero_stored, 16)
            sp.wait_ge(zero_stored, 16 * EXPERTS)

        @block.gpsimd
        def _(pool):
            own = Steps(pool, psteps)
            own.add(nc.gpsimd.memset(ident[:], 0.0))
            own.add(nc.gpsimd.memset(upper[:], 1.0))
            own.add(nc.gpsimd.memset(K["ones"][:], 1.0))
            own.add(nc.gpsimd.memset(K["mask"][:], 0.0))
            own.settle()
            own.add(nc.gpsimd.affine_select(out=ident[:], in_=ident[:], compare_op=ALU.not_equal, fill=1.0,
                                            base=0, pattern=[[-1, P]], channel_multiplier=1))
            own.add(nc.gpsimd.affine_select(out=upper[:], in_=upper[:], compare_op=ALU.is_ge, fill=0.0,
                                            base=0, pattern=[[1, P]], channel_multiplier=-1))
            own.add(nc.gpsimd.affine_select(out=K["mask"][:], in_=K["mask"][:], compare_op=ALU.is_ge, fill=-BIG,
                                            base=0, pattern=[[1, P]], channel_multiplier=-1))
            own.settle()
            own.add(nc.gpsimd.tensor_copy(K["identb"][:], ident[:]))
            own.add(nc.gpsimd.tensor_copy(K["maskb"][:], K["mask"][:]))
            own.add(nc.gpsimd.tensor_tensor(K["strictb"][:], upper[:], ident[:], ALU.subtract))
            own.add(nc.gpsimd.tensor_copy(K["onesb"][:], K["ones"][:]))
            nc.gpsimd.memset(zero[:], 0.0).then_inc(zero_ready, 1)
            own.settle()
            nc.gpsimd.memset(K["scratch"][:], 0.0).then_inc(consts_ready, 1)

        @block.scalar
        def _(act):
            act.wait_ge(cols_ready, 2)
            nc.scalar.activation(cs[:], vcols[:, 0:KD], ACT.Silu).then_inc(cs_ready, 1)

        @block.tensor
        def _(pe):
            pe.wait_ge(consts_ready, 1)
            pe.wait_ge(rows_loaded, 6 * 16)
            nc.tensor.transpose(pv[:, 0:NV], vrows[:], ident[0:NV, 0:NV]).then_inc(turned, 1)
            nc.tensor.transpose(pv[:, P:2 * P], trows[:], ident[:]).then_inc(turned, 1)
            pe.wait_ge(cs_ready, 1)
            for j in range(6):
                pe.wait_ge(w_loaded[j % 2], 16 * (j // 2 + 1))
                for m in range(KD):
                    for k in range(KD):
                        mm = nc.tensor.matmul(ps[:, j * KD + m:j * KD + m + 1], W[j % 2][:, k, m * P:(m + 1) * P],
                                              cs[:, k:k + 1], start=(k == 0), stop=(k == KD - 1))
                mm.then_inc(mod_done, 1)

        @block.vector
        def _(dve):
            own = Steps(dve, vsteps)
            dve.wait_ge(turned, 2)
            nc.vector.tensor_copy(vcols[:], pv[:, 0:NV]).then_inc(cols_ready, 1)
            nc.vector.tensor_copy(K["conv"][:, 0:TAPS, :], pv[:, P:2 * P].rearrange("p (t b) -> p t b", t=TAPS)
                                  ).then_inc(cols_ready, 1)
            dve.wait_ge(cols_ready, 2)
            own.add(nc.vector.tensor_copy(K["conv"][:, TAPS, :], vcols[:, 9 * KD:9 * KD + CB]))
            dve.wait_ge(mod_done, 6)
            own.add(nc.vector.tensor_tensor(mod[:], ps[:, 0:6 * KD], vcols[:, KD:7 * KD], ALU.add))
            own.settle()
            own.add(nc.vector.scalar_tensor_tensor(K["a1"][:], mod[:, KD:2 * KD], 1.0, vcols[:, 7 * KD:8 * KD],
                                                   ALU.add, ALU.mult))
            own.add(nc.vector.scalar_tensor_tensor(K["a2"][:], mod[:, 4 * KD:5 * KD], 1.0, vcols[:, 8 * KD:9 * KD],
                                                   ALU.add, ALU.mult))


def mixer_phase(nc, x, in_w, dt_bias, a_log, d_skip, norm_w, ydram, K):
    with ExitStack() as ctx:
        sb = lambda n, s, d=F32: ctx.enter_context(nc.sbuf_tensor(n, s, d))
        psum = lambda n: ctx.enter_context(nc.psum_tensor(n, [P, 512], F32))
        sem = semaphores(nc, ctx, "mixer_")
        ident, upper, ones, maskb, identb = (K[x] for x in ("ident", "upper", "ones", "maskb", "identb"))
        hT = [sb(f"hT{i}", [P, KD, HTOK], F32R) for i in range(2)]
        wfm = [sb(f"wfm{i}", [P, 4, KD, P], F32R) for i in range(2)]
        wz = [sb(f"wz{i}", [P, KD, GW], F32R) for i in range(2)]
        wraw = sb("wraw", [P, 3, KD * P])
        raw = sb("raw", [P, 2, 3 + SUP])
        cv = sb("cv", [P, 2, SUP])
        fm = [sb(f"fm{i}", [P, 4, SUP]) for i in range(2)]
        zs = [sb(f"zs{i}", [P, CS, GW]) for i in range(2)]
        tok = [sb(f"tok{i}", [P, 3 * P]) for i in range(2)]
        gm = [sb(f"gm{i}", [P, HG, P]) for i in range(2)]
        xdt = [sb(f"xdt{i}", [P, HG, PD]) for i in range(2)]
        xde = [sb(f"xde{i}", [P, HG, PD]) for i in range(2)]
        xd = [sb(f"xd{i}", [P, HG, PD]) for i in range(2)]
        yt = [sb(f"yt{i}", [P, HG, PD]) for i in range(2)]
        ysq = sb("ysq", [P, GW])
        yo = [sb(f"yo{i}", [P, GW]) for i in range(2)]
        ssq = sb("ssq", [P, 6])
        state = sb("state", [P, HG, PD])
        states = sb("states", [P, G, HG * PD])
        hist = sb("hist", [P, 12, G])
        histg = sb("histg", [P, 2, 4, 3])
        nw = sb("nw", [P, DI])
        vecg = sb("vecg", [P, TAPS + 1, 4])
        dbias = sb("dbias", [P, HEADS])
        aneg = sb("aneg", [P, HEADS])
        W8 = HT * HEADS
        pk = sb("pk", [P, 5 * HT + 1, HEADS])
        pkg = sb("pkg", [P, 5 * HT + 1, HG])
        da = [sb(f"da{i}", [P, HT, HEADS], F32R) for i in range(2)]
        dag = [sb(f"dag{i}", [P, HT, HG], F32R) for i in range(2)]
        wdt = sb("wdt", [P, KD, HEADS])
        wdts = [sb(f"wdts{i}", [P, KD, HEADS], F32R) for i in range(2)]
        upr = sb("upr", [P, P], F32R)
        tss = sb("tss", [P, 4])
        minus_half = sb("minus_half", [P, 1])
        eps = sb("eps", [P, 1])
        flat = lambda a: a.rearrange("p a b -> p (a b)")
        xt = [flat(fm[i][:, 0:2, :]) for i in range(2)]
        xsq = flat(fm[0][:, 2:4, :])
        v = flat(fm[1][:, 2:4, :]).rearrange("p (k n) -> p k n", k=KD)
        T = [cv[:, i // 2, (i % 2) * W8:(i % 2 + 1) * W8] for i in range(4)]
        T += [zs[0][:, i, :] for i in range(4)]
        row = lambda i: flat(pk[:, i * HT:(i + 1) * HT, :])
        DT, NAC, EAC, DTE, CDEC = range(5)
        dtcol = lambda q, c: pkg[:, q * HT + c, :]

        psF = [psum("psF0"), psum("psF1")]
        psZ = psum("psZ")
        psT = [psum("psT0"), psum("psT1")]
        psS = [psum("psS0"), psum("psS1")]
        psY = psum("psY")
        NAMES = ("vec_loaded", "x_sq", "x_scaled", "x_turned", "v_ready", "v_high", "h_ready", "wdt_ready",
                 "dt_done", "dt_low", "dt_exp", "dt_ln", "dt_ready", "cum_done", "cum_sub", "cum_exp", "aneg_ready",
                 "w_high", "w_low", "fm_done", "fm_out", "conv_done", "fm_ready", "z_done", "z_ready",
                 "turned", "seg_done", "tok_ready", "decay_ready", "gm_ready", "x_parts", "scan_done",
                 "state_ready", "y_read", "y_gated", "y_squared", "y_ready", "group_ready",
                 "vsteps", "asteps", "psteps", "zeroed", "passed", "x_mean", "x_rstd", "y_mean", "y_rstd", "w_order", "half_ready", "hist_in")
        S = {n: sem(n) for n in NAMES}
        x_loaded = [sem(f"x_loaded{i}") for i in range(2)]
        raw_loaded = [sem(f"raw_loaded{i}") for i in range(3)]
        y_stored = [sem(f"y_stored{i}") for i in range(2)]
        block = ctx.enter_context(nc.Block())

        @block.sync
        def _(sp):
            sp.dma_start(dbias[:], dt_bias.broadcast_to([P, HEADS])).then_inc(S["vec_loaded"], 16)
            sp.dma_start(aneg[:], a_log.broadcast_to([P, HEADS])).then_inc(S["vec_loaded"], 16)
            sp.dma_start(pk[:, 5 * HT, :], d_skip.broadcast_to([P, HEADS])).then_inc(S["vec_loaded"], 16)
            sp.dma_start(nw[:], norm_w.broadcast_to([P, DI])).then_inc(S["vec_loaded"], 16)
            sp.dma_start(wdt[:], in_w[0, :, DI + CONV_DIM:].rearrange("(k p) n -> p k n", p=P)
                         ).then_inc(S["vec_loaded"], 16)

            def load_x(h):
                for t in range(HT):
                    if t >= 2:
                        sp.wait_ge(S["x_turned"], h * HT + t - 1)
                    elif h:
                        sp.wait_ge(S["y_ready"], h * G * HT)
                    sp.dma_start(xt[t % 2], x[0, h * HTOK + t * P:h * HTOK + (t + 1) * P, :]
                                 ).then_inc(x_loaded[t % 2], 16)

            def load_weights(it, g, part):
                for m in range(3 * part, 3 * part + 3):
                    if m >= 3:
                        sp.wait_ge(S["w_low"], it * PIECES + (m - 2))
                    else:
                        sp.wait_ge(S["w_low"], it * PIECES)
                    sp.sem_inc(S["passed"], 1)
                    if m < 2:
                        src = in_w[0, :, bass.ds(DI + g * GW + m * P, P)].rearrange("(k p) n -> p k n", p=P)
                    elif m < 4:
                        src = in_w[0, :, bass.ds(2 * DI + (m - 2) * G * N + g * N, P)].rearrange("(k p) n -> p k n", p=P)
                    else:
                        src = in_w[0, (m - 4) * 4 * P:(m - 3) * 4 * P, bass.ds(g * GW, GW)].rearrange(
                            "(k p) n -> p k n", p=P)
                    dst = wraw[:, m % 3, :].rearrange("p (k n) -> p k n", k=src.shape[1])
                    sp.dma_start(dst, src).then_inc(raw_loaded[m % 3], 16)

            def store_y(h, it, g):
                for c in range(HT):
                    sp.wait_ge(S["y_ready"], it * HT + (c + 1))
                    sp.dma_start(ydram[h * HTOK + c * P:h * HTOK + (c + 1) * P, bass.ds(g * GW, GW)], yo[c % 2][:]
                                 ).then_inc(y_stored[c % 2], 16)

            for h in range(HALVES):
                load_weights(h * G, 0, 0)
                if h:
                    store_y(h - 1, h * G - 1, G - 1)
                load_x(h)
                load_weights(h * G, 0, 1)
                with sp.Fori(1, G) as g:
                    load_weights(g + h * G, g, 0)
                    store_y(h, g + (h * G - 1), g - 1)
                    load_weights(g + h * G, g, 1)
            store_y(HALVES - 1, HALVES * G - 1, G - 1)
            for q in y_stored:
                sp.wait_ge(q, 16 * (HALVES * G * HT // 2 + 1))

        @block.gpsimd
        def _(pool):
            nc.gpsimd.memset(states[:], 0.0).then_inc(S["zeroed"], 1)
            nc.gpsimd.memset(hist[:], 0.0).then_inc(S["zeroed"], 1)
            nc.gpsimd.memset(minus_half[:], -0.5).then_inc(S["zeroed"], 1)
            nc.gpsimd.memset(eps[:], EPS).then_inc(S["zeroed"], 1)
            pool.wait_ge(S["zeroed"], 4)

            def half(h):
                for t in range(HT):
                    pool.wait_ge(S["x_sq"], h * HT + (t + 1))
                    nc.gpsimd.tensor_tensor(tss[:, 1:2], tss[:, 0:1], eps[:], ALU.add).then_inc(S["x_mean"], 1)
                    pool.wait_ge(S["x_mean"], h * HT + (t + 1))
                    if t >= 1:
                        pool.wait_ge(S["x_scaled"], h * HT + t)
                    nc.gpsimd.tensor_tensor(tss[:, 2:3], tss[:, 1:2], minus_half[:], ALU.pow).then_inc(S["x_rstd"], 1)

            def group(it):
                n8 = pool.snap(it * HT)
                n6 = pool.snap(it * PIECES)
                for m in range(PIECES):
                    pool.wait_ge(S["w_high"], n6 + (m + 1))
                    hi, lo = (flat(wfm[i][:, m]) if m < 4 else flat(wz[i][:, (m - 4) * 4:(m - 3) * 4]) for i in range(2))
                    nc.gpsimd.tensor_tensor(lo, wraw[:, m % 3, :], hi.bitcast(F32), ALU.subtract
                                            ).then_inc(S["w_low"], 1)
                pool.wait_ge(S["group_ready"], it + 1)
                for c in range(HT):
                    pool.wait_ge(S["tok_ready"], n8 + (c + 1))
                    if c >= 2:
                        pool.wait_ge(S["y_gated"], n8 + (c - 1))
                    xv = tok[c % 2][:, 0:GW].rearrange("p (h d) -> p h d", h=HG)
                    by = lambda col: col.unsqueeze(2).broadcast_to([P, HG, PD])
                    nc.gpsimd.tensor_tensor(xdt[c % 2][:], xv, by(dtcol(DT, c)), ALU.mult)
                    nc.gpsimd.tensor_tensor(xde[c % 2][:], xv, by(dtcol(DTE, c)), ALU.mult)
                    nc.gpsimd.tensor_tensor(xd[c % 2][:], xv, by(pkg[:, 5 * HT, :]), ALU.mult
                                            ).then_inc(S["x_parts"], 1)
                    if c >= 1:
                        rstd(c - 1, n8)
                rstd(HT - 1, n8)

            def rstd(c, n8):
                b = c % 2
                pool.wait_ge(S["y_squared"], n8 + (c + 1))
                nc.gpsimd.tensor_tensor(ssq[:, 2 + b:3 + b], ssq[:, b:b + 1], eps[:], ALU.add).then_inc(S["y_mean"], 1)
                pool.wait_ge(S["y_mean"], n8 + (c + 1))
                nc.gpsimd.tensor_tensor(ssq[:, 4 + b:5 + b], ssq[:, 2 + b:3 + b], minus_half[:], ALU.pow
                                        ).then_inc(S["y_rstd"], 1)

            with pool.Fori(0, HALVES) as h:
                half(h)
                with pool.Fori(0, G) as g:
                    group(pool.snap(h * G + g))

        @block.scalar
        def _(act):
            act.wait_ge(S["vec_loaded"], 5 * 16)
            nc.scalar.activation(aneg[:], aneg[:], ACT.Exp).then_inc(S["aneg_ready"], 1)

            def half(h):
                for t in range(HT):
                    act.wait_ge(x_loaded[t % 2], h * (HT // 2 * 16) + 16 * (t // 2 + 1))
                    if t >= 1:
                        act.wait_ge(S["x_scaled"], h * HT + t)
                    nc.scalar.activation(xsq, xt[t % 2], ACT.Square, scale=D ** -0.5, accum_out=tss[:, 0:1]).then_inc(S["x_sq"], 1)
                    act.wait_ge(S["x_turned"], h * HT + (t + 1))
                    if t >= 1:
                        act.wait_ge(S["h_ready"], h * HT + t)
                    for k in range(KD):
                        last = nc.scalar.activation(v[:, k, :], psF[k // 4][:, (k % 4) * P:(k % 4 + 1) * P],
                                                    ACT.Identity, bias=K["mod"][:, k:k + 1], scale=K["a1"][:, k:k + 1])
                    last.then_inc(S["v_ready"], 1)
                    act.wait_ge(S["v_ready"], h * HT + (t + 1))
                    nc.scalar.copy(hT[0][:, :, t * P:(t + 1) * P], v).then_inc(S["v_high"], 1)
                act.wait_ge(S["dt_low"], h + 1)
                nc.scalar.activation(T[2], T[1], ACT.Exp).then_inc(S["dt_exp"], 1)
                act.wait_ge(S["dt_exp"], h + 1)
                nc.scalar.activation(T[4], T[2], ACT.Ln, bias=1.0).then_inc(S["dt_ln"], 1)
                act.wait_ge(S["cum_sub"], h + 1)
                nc.scalar.activation(row(EAC), row(NAC), ACT.Exp, scale=-1.0)
                nc.scalar.activation(row(CDEC), psS[1][:, W8:2 * W8], ACT.Exp)
                nc.scalar.activation(T[5], T[6], ACT.Exp).then_inc(S["cum_exp"], 1)

            def group(it):
                n8 = act.snap(it * HT)
                n6 = act.snap(it * PIECES)
                half6 = act.snap(it * 32)
                for m in range(PIECES):
                    act.wait_ge(raw_loaded[m % 3], half6 + 16 * (m // 3 + 1))
                    hi = flat(wfm[0][:, m]) if m < 4 else flat(wz[0][:, (m - 4) * 4:(m - 3) * 4])
                    nc.scalar.copy(hi, wraw[:, m % 3, :]).then_inc(S["w_high"], 1)
                act.wait_ge(S["group_ready"], it + 1)

                def block_out(s, m):
                    i = s * 4 + m
                    act.wait_ge(S["fm_done"], n8 + (i + 1))
                    if i >= 2:
                        act.wait_ge(S["fm_ready"], n8 + (i - 1))
                    if s:
                        act.wait_ge(S["fm_out"], n8 + (m + 1))
                    b = i % 2
                    nc.scalar.copy(raw[:, b, 0:3], histg[:, s, m, :])
                    nc.scalar.activation(cv[:, b, :], psF[b][:], ACT.Identity, bias=vecg[:, TAPS, m:m + 1],
                                         scale=vecg[:, TAPS - 1, m:m + 1])
                    nc.scalar.copy(raw[:, b, 3:3 + SUP], psF[b][:])
                    nc.scalar.copy(histg[:, 1 - s, m, :], psF[b][:, SUP - 3:SUP]).then_inc(S["fm_out"], 1)

                def block_silu(s, m):
                    act.wait_ge(S["conv_done"], n8 + (s * 4 + m + 1))
                    nc.scalar.activation(fm[s][:, m, :], cv[:, m % 2, :], ACT.Silu).then_inc(S["fm_ready"], 1)

                def z_out(c):
                    act.wait_ge(S["z_done"], n8 + (c + 1))
                    nc.scalar.activation(zs[c // CS][:, c % CS, :], psZ[:, 0:GW], ACT.Silu).then_inc(S["z_ready"], 1)

                def chunk_in(c):
                    act.wait_ge(S["turned"], n8 + (c + 1))
                    if c >= 2:
                        act.wait_ge(S["scan_done"], n8 + (c - 1))
                    nc.scalar.copy(tok[c % 2][:], psT[c % 2][:, 0:3 * P]).then_inc(S["tok_ready"], 1)
                    act.wait_ge(S["seg_done"], n8 + (c + 1))
                    for h in range(HG):
                        last = nc.scalar.activation(gm[c % 2][:, h, :], psS[c % 2][:, h * P:(h + 1) * P], ACT.Exp,
                                                    bias=pkg[:, NAC * HT + c, h:h + 1])
                    last.then_inc(S["decay_ready"], 1)

                def square(c):
                    act.wait_ge(S["y_gated"], n8 + (c + 1))
                    nc.scalar.activation(ysq[:], flat(yt[c % 2][:]), ACT.Square, scale=GW ** -0.5, accum_out=ssq[:, c % 2:c % 2 + 1]
                                         ).then_inc(S["y_squared"], 1)

                for m in range(4):
                    block_out(0, m)
                    if m >= 1:
                        block_silu(0, m - 1)
                block_silu(0, 3)
                for c in range(CS):
                    z_out(c)
                for c in range(CS):
                    chunk_in(c)
                    if c >= 1:
                        square(c - 1)
                    block_out(1, c)
                    if c < 3:
                        pass
                    block_silu(1, c)
                for c in range(CS, HT):
                    z_out(c)
                chunk_in(4)
                square(3)
                for c in range(5, HT):
                    chunk_in(c)
                    square(c - 1)
                square(HT - 1)

            with act.Fori(0, HALVES) as h:
                half(h)
                with act.Fori(0, G) as g:
                    group(act.snap(h * G + g))

        @block.tensor
        def _(pe):
            def split_products(out, lhs, rhs):
                K_ = len(lhs[0])
                for n, (i, j) in enumerate(((1, 0), (0, 1), (0, 0))):
                    for k in range(K_):
                        mm = nc.tensor.matmul(out, lhs[i][k], rhs[j][k], start=(n == 0 and k == 0),
                                              stop=(n == 2 and k == K_ - 1))
                return mm

            def half(h):
                for t in range(HT):
                    pe.wait_ge(S["x_scaled"], h * HT + (t + 1))
                    if t >= 1:
                        pe.wait_ge(S["v_ready"], h * HT + t)
                    for k in range(KD):
                        mm = nc.tensor.transpose(psF[k // 4][:, (k % 4) * P:(k % 4 + 1) * P],
                                                 xt[t % 2][:, k * P:(k + 1) * P], ident[:])
                    mm.then_inc(S["x_turned"], 1)
                    pe.wait_ge(S["h_ready"], h * HT + (t + 1))
                    if t == 0:
                        pe.sem_inc(S["passed"], 1)
                    mm = split_products(psY[:, t * HEADS:(t + 1) * HEADS],
                                        [[hT[i][:, k, t * P:(t + 1) * P] for k in range(KD)] for i in range(2)],
                                        [[wdts[i][:, k, :] for k in range(KD)] for i in range(2)])
                mm.then_inc(S["dt_done"], 1)
                pe.wait_ge(S["dt_ready"], h + 1)
                nc.tensor.matmul(psS[1][:, 0:W8], upper[:], T[7], start=True, stop=True)
                nc.tensor.matmul(psS[1][:, W8:2 * W8], ones[:], T[7], start=True, stop=True).then_inc(S["cum_done"], 1)
                pe.wait_ge(S["half_ready"], h + 1)
                pe.sem_inc(S["passed"], 1)

            def group(it):
                n8 = pe.snap(it * HT)
                n6 = pe.snap(it * PIECES)

                def project(s, m):
                    i = s * 4 + m
                    if not s:
                        pe.wait_ge(S["w_low"], n6 + (m + 1))
                    if i >= 2:
                        pe.wait_ge(S["fm_out"], n8 + (i - 1))
                    split_products(psF[i % 2][:], [[wfm[j][:, m, k, :] for k in range(KD)] for j in range(2)],
                                   [[hT[j][:, k, s * SUP:(s + 1) * SUP] for k in range(KD)] for j in range(2)]
                                   ).then_inc(S["fm_done"], 1)

                def project_z(c):
                    if c == 0:
                        pe.wait_ge(S["w_low"], n6 + PIECES)
                        pe.wait_ge(S["group_ready"], it + 1)
                    else:
                        pe.wait_ge(S["z_ready"], n8 + c)
                    split_products(psZ[:, 0:GW], [[hT[j][:, k, c * P:(c + 1) * P] for k in range(KD)] for j in range(2)],
                                   [[wz[j][:, k, :] for k in range(KD)] for j in range(2)]).then_inc(S["z_done"], 1)

                def chunk_in(c):
                    s, o = c // CS, (c % CS) * P
                    if c % CS == 0:
                        pe.wait_ge(S["fm_ready"], n8 + (s + 1) * 4)
                    if c >= 2:
                        pe.wait_ge(S["y_read"], n8 + (c - 1))
                    b = c % 2
                    for m in range(3):
                        nc.tensor.transpose(psT[b][:, m * P:(m + 1) * P], fm[s][:, m, o:o + P], ident[:])
                    nc.tensor.matmul(psT[b][:, 3 * P:], fm[s][:, 2, o:o + P], fm[s][:, 3, o:o + P],
                                     start=True, stop=True).then_inc(S["turned"], 1)
                    if c == 0:
                        pe.wait_ge(S["group_ready"], it + 1)
                    for h in range(HG):
                        for j in (1, 0):
                            nc.tensor.matmul(psS[b][:, h * P:(h + 1) * P], dag[j][:, c, h:h + 1].broadcast_to([P, P]),
                                             upr[:], start=(h == 0 and j == 1), stop=False, skip_group_check=True)
                    nc.tensor.matmul(psS[b][:].rearrange("p (h i) -> p h i", h=HG), identb[:],
                                     maskb[:].unsqueeze(1).broadcast_to([P, HG, P]), start=False, stop=True,
                                     skip_group_check=True).then_inc(S["seg_done"], 1)

                def chunk_out(c):
                    s, o, b = c // CS, (c % CS) * P, c % 2
                    pe.wait_ge(S["gm_ready"], n8 + (c + 1))
                    pe.wait_ge(S["x_parts"], n8 + (c + 1))
                    pe.wait_ge(S["state_ready"], n8 + (c + 1))
                    if c >= 1:
                        pe.wait_ge(S["y_read"], n8 + c)
                    nc.tensor.matmul(psY[:, GW:2 * GW], fm[s][:, 3, o:o + P], flat(state[:]), start=True, stop=True)
                    nc.tensor.matmul(psS[b][:, 0:GW], tok[b][:, 2 * P:3 * P], flat(xde[b][:]), start=True, stop=True)
                    for h in range(HG):
                        mm = nc.tensor.matmul(psY[:, h * PD:(h + 1) * PD], gm[b][:, h, :], xdt[b][:, h, :],
                                              start=True, stop=True)
                    mm.then_inc(S["scan_done"], 1)

                for m in range(4):
                    project(0, m)
                for c in range(CS):
                    project_z(c)
                for c in range(CS):
                    chunk_in(c)
                    project(1, c)
                    chunk_out(c)
                for c in range(CS, HT):
                    project_z(c)
                chunk_in(4)
                for c in range(5, HT):
                    chunk_in(c)
                    chunk_out(c - 1)
                chunk_out(HT - 1)

            pe.wait_ge(S["vec_loaded"], 5 * 16)
            with pe.Fori(0, HALVES) as h:
                half(h)
                with pe.Fori(0, G) as g:
                    group(pe.snap(h * G + g))

        @block.vector
        def _(dve):
            first = Steps(dve, S["w_order"])
            for q in y_stored:
                dve.sem_inc(q, 16)
            dve.wait_ge(S["vec_loaded"], 5 * 16)
            first.add(nc.vector.tensor_copy(wdts[0][:], wdt[:]))
            first.add(nc.vector.tensor_copy(upr[:], upper[:]))
            first.settle()
            first.add(nc.vector.tensor_tensor(wdts[1][:], wdt[:], wdts[0][:].bitcast(F32), ALU.subtract))
            first.settle()
            dve.wait_ge(S["aneg_ready"], 1)
            first.add(nc.vector.tensor_scalar(aneg[:], aneg[:], -1.0, None, ALU.mult))
            first.settle()
            dve.wait_ge(S["zeroed"], 4)
            nc.vector.memset(ssq[:], 0.0).then_inc(S["wdt_ready"], 1)

            def half(h, own):
                for t in range(HT):
                    dve.wait_ge(S["x_rstd"], h * HT + (t + 1))
                    nc.vector.tensor_scalar(xt[t % 2], xt[t % 2], tss[:, 2:3], None, ALU.mult).then_inc(S["x_scaled"], 1)
                    dve.wait_ge(S["v_high"], h * HT + (t + 1))
                    o = slice(t * P, (t + 1) * P)
                    nc.vector.tensor_tensor(hT[1][:, :, o], v, hT[0][:, :, o].bitcast(F32), ALU.subtract
                                            ).then_inc(S["h_ready"], 1)
                per_tile = lambda a: a.unsqueeze(1).broadcast_to([P, HT, HEADS])
                shaped = lambda a: a.rearrange("p (c h) -> p c h", c=HT)
                dve.wait_ge(S["dt_done"], h + 1)
                own.add(nc.vector.tensor_tensor(shaped(T[0]), shaped(psY[:, 0:W8]), per_tile(dbias[:]), ALU.add))
                own.settle()
                nc.vector.scalar_tensor_tensor(T[1], T[0], -1.0, T[0], ALU.mult, ALU.min).then_inc(S["dt_low"], 1)
                own.add(nc.vector.tensor_scalar(T[3], T[0], 0.0, None, ALU.max))
                dve.wait_ge(S["dt_ln"], h + 1)
                own.add(nc.vector.tensor_scalar(T[5], T[2], 1.0, None, ALU.add))
                own.settle()
                own.add(nc.vector.scalar_tensor_tensor(T[6], T[5], -1.0, T[2], ALU.add, ALU.subtract))
                own.add(nc.vector.reciprocal(T[7], T[5]))
                own.add(nc.vector.tensor_tensor(T[4], T[4], T[3], ALU.add))
                own.settle()
                own.add(nc.vector.tensor_tensor(T[6], T[6], T[7], ALU.mult))
                own.settle()
                own.add(nc.vector.tensor_tensor(row(DT), T[4], T[6], ALU.subtract))
                own.settle()
                nc.vector.tensor_tensor(shaped(T[7]), shaped(row(DT)), per_tile(aneg[:]), ALU.mult
                                        ).then_inc(S["dt_ready"], 1)
                dve.wait_ge(S["dt_ready"], h + 1)
                own.add(nc.vector.tensor_copy(flat(da[0][:]), T[7]))
                own.settle()
                own.add(nc.vector.tensor_tensor(flat(da[1][:]), T[7], flat(da[0][:]).bitcast(F32), ALU.subtract))
                dve.wait_ge(S["cum_done"], h + 1)
                own.add(nc.vector.tensor_scalar(row(NAC), psS[1][:, 0:W8], -1.0, None, ALU.mult))
                own.settle()
                nc.vector.tensor_tensor(T[6], psS[1][:, W8:2 * W8], row(NAC), ALU.add).then_inc(S["cum_sub"], 1)
                dve.wait_ge(S["cum_exp"], h + 1)
                nc.vector.tensor_tensor(row(DTE), row(DT), T[5], ALU.mult).then_inc(S["half_ready"], 1)
                dve.wait_ge(S["half_ready"], h + 1)
                dve.sem_inc(S["passed"], 1)

            def group(it, g, own):
                n8 = dve.snap(it * HT)
                g4 = dve.snap(g * HG)
                own.add(nc.vector.tensor_copy(vecg[:, :, 0:2], K["conv"][:, :, bass.ds(g * 2, 2)]))
                own.add(nc.vector.tensor_copy(vecg[:, :, 2:3], K["conv"][:, :, bass.ds(g + 2 * G, 1)]))
                own.add(nc.vector.tensor_copy(vecg[:, :, 3:4], K["conv"][:, :, bass.ds(g + 3 * G, 1)]))
                own.add(nc.vector.tensor_copy(pkg[:], pk[:, :, bass.ds(g4, HG)]))
                for i in range(2):
                    own.add(nc.vector.tensor_copy(dag[i][:], da[i][:, :, bass.ds(g4, HG)]))
                own.settle()
                nc.vector.tensor_copy(flat(state[:]), states[:, bass.ds(g, 1), :].rearrange("p o n -> p (o n)")
                                      ).then_inc(S["state_ready"], 1)
                nc.vector.tensor_copy(flat(histg[:, 0]).unsqueeze(2), hist[:, :, bass.ds(g, 1)]
                                      ).then_inc(S["group_ready"], 1)
                dve.wait_ge(S["group_ready"], it + 1)

                def conv(s, m):
                    i = s * 4 + m
                    b = i % 2
                    dve.wait_ge(S["fm_out"], n8 + (i + 1))
                    for tap in range(TAPS - 1):
                        ins = nc.vector.scalar_tensor_tensor(cv[:, b, :], raw[:, b, tap:tap + SUP],
                                                             vecg[:, tap, m:m + 1], cv[:, b, :], ALU.mult, ALU.add)
                        if tap < TAPS - 2:
                            own.add(ins)
                            own.settle()
                    ins.then_inc(S["conv_done"], 1)

                def decays(c):
                    dve.wait_ge(S["decay_ready"], n8 + (c + 1))
                    cb = psT[c % 2][:, 3 * P:].unsqueeze(1).broadcast_to([P, HG, P])
                    nc.vector.tensor_tensor(gm[c % 2][:], gm[c % 2][:], cb, ALU.mult).then_inc(S["gm_ready"], 1)

                def gate(c):
                    b = c % 2
                    by = lambda col: col.unsqueeze(2).broadcast_to([P, HG, PD])
                    halves = lambda a: a.rearrange("p (h d) -> p h d", h=HG)
                    dve.wait_ge(S["scan_done"], n8 + (c + 1))
                    own.add(nc.vector.tensor_tensor(state[:], state[:], by(dtcol(CDEC, c)), ALU.mult))
                    own.add(nc.vector.tensor_tensor(yt[b][:], halves(psY[:, GW:2 * GW]), by(dtcol(EAC, c)), ALU.mult))
                    own.settle()
                    ins = nc.vector.tensor_tensor(state[:], state[:], halves(psS[b][:, 0:GW]), ALU.add)
                    if c < HT - 1:
                        ins.then_inc(S["state_ready"], 1)
                    else:
                        own.add(ins)
                    nc.vector.tensor_tensor(yt[b][:], yt[b][:], halves(psY[:, 0:GW]), ALU.add).then_inc(S["y_read"], 1)
                    dve.wait_ge(S["y_read"], n8 + (c + 1))
                    own.add(nc.vector.tensor_tensor(yt[b][:], yt[b][:], xd[b][:], ALU.add))
                    own.settle()
                    dve.wait_ge(S["z_ready"], n8 + (c + 1))
                    nc.vector.tensor_tensor(flat(yt[b][:]), flat(yt[b][:]), zs[c // CS][:, c % CS, :], ALU.mult
                                            ).then_inc(S["y_gated"], 1)

                def norm(c):
                    b = c % 2
                    dve.wait_ge(S["y_rstd"], n8 + (c + 1))
                    dve.wait_ge(y_stored[b], stored + 16 * (c // 2 + 1))
                    nc.vector.scalar_tensor_tensor(yo[b][:], flat(yt[b][:]), ssq[:, 4 + b:5 + b], nw[:, bass.ds(g * GW, GW)],
                                                   ALU.mult, ALU.mult).then_inc(S["y_ready"], 1)

                stored = dve.snap(it * (HT // 2 * 16))
                for m in range(4):
                    conv(0, m)
                for c in range(CS):
                    decays(c)
                    conv(1, c)
                    gate(c)
                    norm(c)
                decays(4)
                for c in range(5, HT):
                    decays(c)
                    gate(c - 1)
                    norm(c - 1)
                gate(HT - 1)
                norm(HT - 1)
                own.settle()
                dve.sem_inc(S["passed"], 1)
                own.add(nc.vector.tensor_copy(states[:, bass.ds(g, 1), :].rearrange("p o n -> p (o n)"), flat(state[:])))
                own.add(nc.vector.tensor_copy(hist[:, :, bass.ds(g, 1)], flat(histg[:, 0]).unsqueeze(2)))
                own.settle()

            HALF_STEPS, GROUP_STEPS = 11, 49
            with dve.Fori(0, HALVES) as h:
                own = Steps(dve, S["vsteps"], dve.snap(h * HALF_STEPS))
                half(h, own)
                assert own.n == HALF_STEPS, own.n
                with dve.Fori(0, G) as g:
                    it = dve.snap(h * G + g)
                    own = Steps(dve, S["psteps"], dve.snap(it * GROUP_STEPS))
                    group(it, g, own)
                    assert own.n == GROUP_STEPS, own.n


def out_phase(nc, x, out_w, group_w, group_b, expert_w, expert_b, ydram, x1dram, xs, K):
    Q = 4
    NR = GROUPS + EXPERTS
    with ExitStack() as ctx:
        sb = lambda n, s, d=F32: ctx.enter_context(nc.sbuf_tensor(n, s, d))
        psum = lambda n: ctx.enter_context(nc.psum_tensor(n, [P, 512], F32))
        sem = semaphores(nc, ctx, "out_")
        ident, mod, a2 = K["ident"], K["mod"], K["a2"]
        wo = [sb(f"wo{i}", [P, KI, D], F32R) for i in range(2)]
        wraw = sb("wo_raw", [P, 2, D])
        y4 = sb("y4", [P, Q, 512])
        yT = [sb(f"yT{i}", [P, Q, 512], F32R) for i in range(2)]
        rows = {n: sb("row_" + n, [P, D]) for n in ("gt1", "a2", "s2")}
        xr = sb("xr", [P, D])
        tmp = sb("tmp", [P, 2, 512])
        hf = sb("hf", [P, D])
        hfT = sb("hfT", [P, KD, P])
        wr = sb("wr", [P, KD, NR])
        rb = sb("rb", [P, NR])
        st = sb("st", [P, 4])
        minus_half, eps = sb("o_minus_half", [P, 1]), sb("o_eps", [P, 1])
        lg, el = sb("lg", [P, 8]), sb("el", [P, EXPERTS])
        gm8, em8 = sb("gm8", [P, 8]), sb("em8", [P, 8])
        gi8, ei8 = sb("gi8", [P, 8], U32), sb("ei8", [P, 8], U32)
        gif, eif, ngm = sb("gif", [P, 1]), sb("eif", [P, 2]), sb("ngm", [P, 1])
        ge, gsum, dif, ex = sb("ge", [P, 4]), sb("gsum", [P, 1]), sb("dif", [P, 1]), sb("ex", [P, 1])
        den, rec = sb("den", [P, 1]), sb("rec", [P, 1])
        ohg, pen = sb("ohg", [P, EXPERTS]), sb("pen", [P, EXPERTS])
        oh = [sb(f"oh{i}", [P, EXPERTS]) for i in range(2)]
        both = sb("both", [P, EXPERTS], BF16)
        pos, base, scr = sb("pos", [P, EXPERTS]), sb("base", [P, EXPERTS]), sb("scr", [P, 2, EXPERTS])
        df, dcur = sb("df", [P, 2]), sb("dcur", [P, 2], U32)
        ii = sb("ii", [P, 3, EXPERTS], I32)
        ff = sb("ff", [P, 3, EXPERTS])
        dest, gates = K["dest"], K["gates"]
        acc = [psum("acc0"), psum("acc1")]
        psT = [psum("oT0"), psum("oT1")]
        psH = [psum("oH0"), psum("oH1")]
        psR, psC = psum("psR"), psum("psC")
        NAMES = ("vec_loaded", "raw_done", "high", "low", "y_turned", "y_high", "y_low", "acc_done", "acc_read",
                 "half_added", "squared", "mean", "rstd", "hf_scaled", "hf_ready", "hf_turned", "hf_copied",
                 "logits", "gneg", "gexp", "edif", "eexp", "picked", "ranked", "placed", "scattered",
                 "x_loaded", "x1_stored", "vsteps", "psteps", "setup", "consts", "rows_done", "rows_copied", "passed",
                 "table_steps", "y_order")
        S = {n: sem(n) for n in NAMES}
        raw_loaded = [sem(f"raw_loaded{i}") for i in range(2)]
        y_loaded = [sem(f"y_loaded{i}") for i in range(Q)]
        block = ctx.enter_context(nc.Block())

        @block.sync
        def _(sp):
            with nc.allow_non_contiguous_dma(reason="the router's weights are narrow"):
                sp.dma_start(wr[:, :, 0:GROUPS], group_w[0].rearrange("(k p) n -> p k n", p=P)).then_inc(S["vec_loaded"], 16)
                sp.dma_start(wr[:, :, GROUPS:NR], expert_w[0].rearrange("(k p) n -> p k n", p=P)).then_inc(S["vec_loaded"], 16)
            sp.dma_start(rb[:, 0:GROUPS], group_b.broadcast_to([P, GROUPS])).then_inc(S["vec_loaded"], 16)
            sp.dma_start(rb[:, GROUPS:NR], expert_b.broadcast_to([P, EXPERTS])).then_inc(S["vec_loaded"], 16)

            def load_y(t):
                for q in range(Q):
                    if not isinstance(t, int) or t:
                        sp.wait_ge(S["y_turned"], t * Q + (q - Q + 1))
                    sp.dma_start(y4[:, q, :], ydram[bass.ds(t * P, P), q * 512:(q + 1) * 512]
                                 ).then_inc(y_loaded[q], 16)

            def load_x(t):
                sp.dma_start(xr[:], x[0, bass.ds(t * P, P), :]).then_inc(S["x_loaded"], 16)

            def store_x1(t):
                sp.wait_ge(S["half_added"], t * 2 + 2)
                sp.dma_start(x1dram[bass.ds(t * P, P), :], xr[:]).then_inc(S["x1_stored"], 16)
                sp.wait_ge(S["x1_stored"], t * 16 + 16)
                sp.wait_ge(S["hf_scaled"], t + 1)

            load_y(0)
            load_x(0)
            for k in range(KI):
                if k >= 2:
                    sp.wait_ge(S["low"], k - 1)
                sp.dma_start(wraw[:, k % 2, :], out_w[0, k * P:(k + 1) * P, :]).then_inc(raw_loaded[k % 2], 16)
            with sp.Fori(1, TILES) as t:
                load_y(t)
                store_x1(t - 1)
                load_x(t)
            store_x1(TILES - 1)

        @block.gpsimd
        def _(pool):
            own = Steps(pool, S["setup"])
            own.add(nc.gpsimd.memset(minus_half[:], -0.5))
            own.add(nc.gpsimd.memset(eps[:], EPS))
            own.add(nc.gpsimd.memset(lg[:, GROUPS:8], -BIG))
            own.add(nc.gpsimd.iota(ii[:, 0, :], pattern=[[1, EXPERTS]], base=0, channel_multiplier=0))
            own.add(nc.gpsimd.iota(ii[:, 1, :], pattern=[[1, GROUPS], [0, EPG]], base=0, channel_multiplier=0))
            own.add(nc.gpsimd.iota(ii[:, 2, :], pattern=[[REGION, EXPERTS]], base=0, channel_multiplier=0))
            own.settle()
            nc.gpsimd.tensor_copy(ff[:], ii[:]).then_inc(S["consts"], 1)

            def add_half(t, n):
                if n == 0:
                    pool.wait_ge(S["x_loaded"], t * 16 + 16)
                pool.wait_ge(S["acc_read"], t * 2 + (n + 1))
                h = slice(n * 512, (n + 1) * 512)
                nc.gpsimd.tensor_tensor(xr[:, h], xr[:, h], tmp[:, n, :], ALU.add).then_inc(S["half_added"], 1)

            def norm(t):
                pool.wait_ge(S["squared"], t + 1)
                nc.gpsimd.tensor_tensor(st[:, 1:2], st[:, 0:1], eps[:], ALU.add).then_inc(S["mean"], 1)
                pool.wait_ge(S["mean"], t + 1)
                nc.gpsimd.tensor_tensor(st[:, 2:3], st[:, 1:2], minus_half[:], ALU.pow).then_inc(S["rstd"], 1)
                pool.wait_ge(S["hf_scaled"], t + 1)
                nc.gpsimd.tensor_tensor(hf[:], hf[:], rows["s2"][:], ALU.add).then_inc(S["hf_ready"], 1)

            def scatter(t):
                pool.wait_ge(S["placed"], t + 1)
                pool.sem_inc(S["passed"], 1)
                for j in range(2):
                    nc.gpsimd.indirect_dma_start(xs, bass.IndirectOffsetOnAxis(ap=dcur[:, j:j + 1], axis=0), hf[:], None
                                                 ).then_inc(S["scattered"], 16)

            def tile(t, n):
                if n >= 2:
                    scatter(t - 2)
                if n >= 1:
                    add_half(t - 1, 1)
                    norm(t - 1)
                add_half(t, 0)

            tile(0, 0)
            tile(1, 1)
            with pool.Fori(2, TILES) as t:
                tile(t, 2)
            scatter(TILES - 2)
            add_half(TILES - 1, 1)
            norm(TILES - 1)
            scatter(TILES - 1)
            pool.wait_ge(S["scattered"], TILES * 32)

        @block.scalar
        def _(act):
            for k in range(KI):
                act.wait_ge(raw_loaded[k % 2], 16 * (k // 2 + 1))
                nc.scalar.copy(wo[0][:, k, :], wraw[:, k % 2, :]).then_inc(S["high"], 1)

            def high(t, q):
                act.wait_ge(S["y_turned"], t * Q + (q + 1))
                nc.scalar.copy(yT[0][:, q, :], psT[q % 2][:]).then_inc(S["y_high"], 1)

            def square(t):
                act.wait_ge(S["half_added"], t * 2 + 2)
                nc.scalar.activation(hf[:], xr[:], ACT.Square, scale=D ** -0.5, accum_out=st[:, 0:1]
                                     ).then_inc(S["squared"], 1)

            def copy_hf(t):
                act.wait_ge(S["hf_turned"], t + 1)
                for i in range(2):
                    last = nc.scalar.copy(hfT[:, i * 4:(i + 1) * 4, :].rearrange("p a b -> p (a b)"), psH[i][:])
                last.then_inc(S["hf_copied"], 1)

            def soft(t):
                act.wait_ge(S["gneg"], t + 1)
                nc.scalar.activation(ge[:], lg[:, 0:GROUPS], ACT.Exp, bias=ngm[:], accum_out=gsum[:]).then_inc(S["gexp"], 1)
                act.wait_ge(S["edif"], t + 1)
                nc.scalar.activation(ex[:], dif[:], ACT.Exp).then_inc(S["eexp"], 1)

            def tile(t, n):
                for q in range(Q):
                    high(t, q)
                if n >= 1:
                    if n >= 2:
                        act.wait_ge(S["scattered"], t * 32 - 32)
                    square(t - 1)
                    copy_hf(t - 1)
                    soft(t - 1)

            tile(0, 0)
            tile(1, 1)
            with act.Fori(2, TILES) as t:
                tile(t, 2)
            act.wait_ge(S["scattered"], (TILES - 1) * 32)
            square(TILES - 1)
            copy_hf(TILES - 1)
            soft(TILES - 1)

        @block.tensor
        def _(pe):
            for r, (src, off) in enumerate(((mod, 2 * KD), (a2, 0), (mod, 3 * KD))):
                for i in range(2):
                    if r:
                        pe.wait_ge(S["rows_copied"], 2 * r - 1 + i)
                    for k in range(4):
                        o = off + 4 * i + k
                        mm = nc.tensor.matmul(acc[i][:, k * P:(k + 1) * P], src[:, o:o + 1].broadcast_to([P, P]),
                                              ident[:], start=True, stop=True)
                    mm.then_inc(S["rows_done"], 1)

            def turn(t, q):
                pe.wait_ge(y_loaded[q], t * 16 + 16)
                if q >= 2:
                    pe.wait_ge(S["y_low"], t * Q + (q - 1))
                for k in range(4):
                    mm = nc.tensor.transpose(psT[q % 2][:, k * P:(k + 1) * P], y4[:, q, k * P:(k + 1) * P], ident[:])
                mm.then_inc(S["y_turned"], 1)

            def product(t, n, q, first=False):
                if n == 0:
                    pe.wait_ge(S["y_low"], t * Q + (q + 1))
                for k in range(4 * q, 4 * q + 4):
                    if first:
                        pe.wait_ge(S["low"], k + 1)
                    o = (k % 4) * P
                    for i, j in ((1, 0), (0, 1), (0, 0)):
                        mm = nc.tensor.matmul(acc[n][:], yT[i][:, q, o:o + P], wo[j][:, k, n * 512:(n + 1) * 512],
                                              start=(k == 0 and i == 1), stop=(k == KI - 1 and i == 0 and j == 0))
                if q == Q - 1:
                    mm.then_inc(S["acc_done"], 1)

            def route_a(t):
                pe.wait_ge(S["hf_ready"], t + 1)
                for k in range(KD):
                    mm = nc.tensor.transpose(psH[k // 4][:, (k % 4) * P:(k % 4 + 1) * P], hf[:, k * P:(k + 1) * P], ident[:])
                mm.then_inc(S["hf_turned"], 1)

            def route_b(t):
                pe.wait_ge(S["hf_copied"], t + 1)
                for k in range(KD):
                    mm = nc.tensor.matmul(psR[:, 0:NR], hfT[:, k, :], wr[:, k, :], start=(k == 0), stop=(k == KD - 1))
                mm.then_inc(S["logits"], 1)

            def route_c(t):
                pe.wait_ge(S["picked"], t + 1)
                nc.tensor.matmul(psC[:, 0:EXPERTS], K["strictb"][:], both[:], start=True, stop=True)
                nc.tensor.matmul(psC[:, EXPERTS:2 * EXPERTS], K["onesb"][:], both[:], start=True, stop=True
                                 ).then_inc(S["ranked"], 1)

            def tile(t, n):
                for q in range(Q):
                    if n >= 1:
                        if q == 0:
                            pe.wait_ge(S["acc_read"], t * 2 - 2 if n == 2 else 1)
                        product(t - 1, 1, q)
                    turn(t, q)
                    if n >= 2 and q == 2:
                        route_c(t - 2)
                if n >= 1:
                    pe.wait_ge(S["acc_read"], t * 2 - 1)
                else:
                    pe.wait_ge(S["rows_copied"], 6)
                for q in range(Q):
                    if q == Q - 1 and n >= 1:
                        route_a(t - 1)
                    product(t, 0, q, first=(n == 0))
                if n >= 1:
                    route_b(t - 1)

            pe.wait_ge(S["vec_loaded"], 4 * 16)
            tile(0, 0)
            tile(1, 1)
            with pe.Fori(2, TILES) as t:
                tile(t, 2)
            for q in range(Q):
                if q == 0:
                    pe.wait_ge(S["acc_read"], TILES * 2 - 2)
                product(TILES - 1, 1, q)
            route_c(TILES - 2)
            route_a(TILES - 1)
            route_b(TILES - 1)
            route_c(TILES - 1)

        @block.vector
        def _(dve):
            for r, name in enumerate(("gt1", "a2", "s2")):
                for i in range(2):
                    dve.wait_ge(S["rows_done"], 2 * r + i + 1)
                    nc.vector.tensor_copy(rows[name][:, i * 512:(i + 1) * 512], acc[i][:]).then_inc(S["rows_copied"], 1)
            for k in range(KI):
                dve.wait_ge(S["high"], k + 1)
                nc.vector.tensor_tensor(wo[1][:, k, :], wraw[:, k % 2, :], wo[0][:, k, :].bitcast(F32), ALU.subtract
                                        ).then_inc(S["low"], 1)
            dve.wait_ge(S["consts"], 1)
            nc.vector.tensor_copy(base[:], ff[:, 2, :]).then_inc(S["y_order"], 1)
            dve.wait_ge(S["y_order"], 1)

            def low(t, q):
                dve.wait_ge(S["y_high"], t * Q + (q + 1))
                nc.vector.tensor_tensor(yT[1][:, q, :], psT[q % 2][:], yT[0][:, q, :].bitcast(F32), ALU.subtract
                                        ).then_inc(S["y_low"], 1)

            def gated(t, n):
                dve.wait_ge(S["acc_done"], t * 2 + (n + 1))
                nc.vector.tensor_tensor(tmp[:, n, :], acc[n][:], rows["gt1"][:, n * 512:(n + 1) * 512], ALU.mult
                                        ).then_inc(S["acc_read"], 1)

            def scaled(t):
                dve.wait_ge(S["rstd"], t + 1)
                nc.vector.scalar_tensor_tensor(hf[:], xr[:], st[:, 2:3], rows["a2"][:], ALU.mult, ALU.mult
                                               ).then_inc(S["hf_scaled"], 1)

            def pick(t, own):
                step = lambda ins: (own.add(ins), own.settle())
                dve.wait_ge(S["logits"], t + 1)
                own.add(nc.vector.tensor_tensor(lg[:, 0:GROUPS], psR[:, 0:GROUPS], rb[:, 0:GROUPS], ALU.add))
                own.add(nc.vector.tensor_tensor(el[:], psR[:, GROUPS:NR], rb[:, GROUPS:NR], ALU.add))
                own.settle()
                dve.sem_inc(S["passed"], 1)
                step(nc.vector.max(gm8[:], lg[:]))
                nc.vector.tensor_scalar(ngm[:], gm8[:, 0:1], -1.0, None, ALU.mult).then_inc(S["gneg"], 1)
                own.add(nc.vector.max_index(gi8[:], gm8[:], lg[:]))
                own.settle()
                step(nc.vector.tensor_copy(gif[:], gi8[:, 0:1]))
                step(nc.vector.tensor_scalar(ohg[:], ff[:, 1, :], gif[:], None, ALU.is_equal))
                own.add(nc.vector.tensor_scalar(pen[:], ohg[:], -1.0, BIG, ALU.add, ALU.mult))
                step(nc.vector.tensor_tensor(el[:], el[:], ohg[:], ALU.mult))
                step(nc.vector.tensor_tensor(el[:], el[:], pen[:], ALU.add))
                dve.sem_inc(S["passed"], 1)
                step(nc.vector.max(em8[:], el[:]))
                nc.vector.tensor_tensor(dif[:], em8[:, 1:2], em8[:, 0:1], ALU.subtract).then_inc(S["edif"], 1)
                own.add(nc.vector.max_index(ei8[:], em8[:], el[:]))
                own.settle()
                step(nc.vector.tensor_copy(eif[:], ei8[:, 0:2]))
                for j in range(2):
                    own.add(nc.vector.tensor_scalar(oh[j][:], ff[:, 0, :], eif[:, j:j + 1], None, ALU.is_equal))
                own.settle()
                nc.vector.tensor_tensor(both[:], oh[0][:], oh[1][:], ALU.add).then_inc(S["picked"], 1)
                dve.wait_ge(S["eexp"], t + 1)
                step(nc.vector.tensor_scalar(den[:], ex[:], 1.0, None, ALU.add))
                step(nc.vector.tensor_tensor(den[:], den[:], gsum[:], ALU.mult))
                step(nc.vector.reciprocal(rec[:], den[:]))
                dve.sem_inc(S["passed"], 1)
                gt = lambda j: gates[:, bass.ds(t * 2 + j, 1)]
                own.add(nc.vector.tensor_copy(gt(0), rec[:]))
                own.add(nc.vector.tensor_tensor(gt(1), rec[:], ex[:], ALU.mult))
                own.settle()

            def place(t, own):
                step = lambda ins: (own.add(ins), own.settle())
                dve.wait_ge(S["ranked"], t + 1)
                step(nc.vector.tensor_tensor(pos[:], base[:], psC[:, 0:EXPERTS], ALU.add))
                for j in range(2):
                    own.add(nc.vector.tensor_tensor_reduce(out=scr[:, j, :], in0=oh[j][:], in1=pos[:], scale=1.0,
                                                           scalar=0.0, op0=ALU.mult, op1=ALU.add,
                                                           accum_out=df[:, j:j + 1]))
                own.add(nc.vector.tensor_tensor(base[:], base[:], psC[:, EXPERTS:2 * EXPERTS], ALU.add))
                own.settle()
                if not isinstance(t, int) or t:
                    dve.wait_ge(S["scattered"], t * 32)
                nc.vector.tensor_copy(dcur[:], df[:]).then_inc(S["placed"], 1)
                own.add(nc.vector.tensor_copy(dest[:, bass.ds(t * 2, 2)], df[:]))
                own.settle()

            def tile(t, n, own):
                for q in range(Q):
                    low(t, q)
                    if q == 2 and n >= 2:
                        place(t - 2, own)
                if n >= 1:
                    gated(t - 1, 1)
                    scaled(t - 1)
                gated(t, 0)
                if n >= 1:
                    pick(t - 1, own)

            STEPS = 24
            own = Steps(dve, S["vsteps"])
            tile(0, 0, own)
            tile(1, 1, own)
            n1 = own.n
            with dve.Fori(2, TILES) as t:
                own = Steps(dve, S["vsteps"], dve.snap(t * STEPS + (n1 - 2 * STEPS)))
                tile(t, 2, own)
                assert own.n == STEPS, own.n
            own = Steps(dve, S["vsteps"], n1 + (TILES - 2) * STEPS)
            place(TILES - 2, own)
            gated(TILES - 1, 1)
            scaled(TILES - 1)
            pick(TILES - 1, own)
            place(TILES - 1, own)
            nc.vector.tensor_tensor(K["count"][:], base[:], ff[:, 2, :], ALU.subtract).then_inc(S["table_steps"], 1)


PEELED = 3
MAXB = 2 * SEQ // P + EXPERTS - 1


def plan_phase(nc, K):
    with ExitStack() as ctx:
        sb = lambda n, s, d=F32: ctx.enter_context(nc.sbuf_tensor(n, s, d))
        sem = semaphores(nc, ctx, "plan_")
        count, ones, tab = K["count"], K["ones"], K["tab"]
        ii, ip = sb("p_ii", [P, EXPERTS], I32), sb("p_ip", [P, 1], I32)
        ex, bl = sb("p_expert", [P, EXPERTS]), sb("p_block", [P, 1])
        t0, ti = sb("p_t0", [P, EXPERTS]), sb("p_ti", [P, EXPERTS], I32)
        nb, inc, exc, last = (sb("p_" + n, [P, EXPERTS]) for n in ("nb", "inc", "exc", "last"))
        own_, scr = sb("p_own", [P, EXPERTS]), sb("p_scr", [P, 5, EXPERTS])
        of = sb("p_of", [P, 5])
        cols = sb("p_cols", [P, 5])
        start, shift = sb("p_start", [P, EXPERTS]), sb("p_shift", [P, EXPERTS])
        pe_, pf = sb("p_pe", [P, 2 * TILES], U32), sb("p_pf", [P, 2 * TILES])
        df, match = sb("p_df", [P, 2 * TILES]), sb("p_match", [P, 2 * TILES, EXPERTS])
        ps = [ctx.enter_context(nc.psum_tensor(f"p_ps{i}", [P, 512], F32)) for i in range(2)]
        consts, steps, turned, cols_ready = sem("consts"), sem("steps"), sem("turned"), sem("cols_ready")
        block = ctx.enter_context(nc.Block())

        @block.gpsimd
        def _(pool):
            nc.gpsimd.iota(ii[:], pattern=[[1, EXPERTS]], base=0, channel_multiplier=0).then_inc(consts, 1)
            nc.gpsimd.iota(ip[:], pattern=[[0, 1]], base=0, channel_multiplier=1).then_inc(consts, 1)

        @block.tensor
        def _(pe):
            pe.wait_ge(cols_ready, 1)
            for j in range(5):
                mm = nc.tensor.matmul(ps[j // 4][0:1, (j % 4) * P:(j % 4 + 1) * P], cols[:, j:j + 1], K["ident"][:],
                                      start=True, stop=True)
            mm.then_inc(turned, 1)

        @block.vector
        def _(dve):
            own = Steps(dve, steps)
            step = lambda ins: (own.add(ins), own.settle())
            ts = nc.vector.tensor_scalar
            dve.wait_ge(consts, 2)
            own.add(nc.vector.tensor_copy(ex[:], ii[:]))
            own.add(nc.vector.tensor_copy(bl[:], ip[:]))
            own.add(ts(last[:], count[:], -float(P), 0.0, ALU.add, ALU.max))
            step(ts(t0[:], count[:], 1.0, float(P - 1), ALU.max, ALU.add))
            step(nc.vector.tensor_copy(ti[:], t0[:]))
            step(ts(ti[:], ti[:], 7, None, ALU.arith_shift_right))
            step(nc.vector.tensor_copy(nb[:], ti[:]))
            step(nc.vector.tensor_tensor_scan(inc[:], ones[:, 0:EXPERTS], nb[:], 0.0, ALU.mult, ALU.add))
            step(nc.vector.tensor_tensor(exc[:], inc[:], nb[:], ALU.subtract))
            own.add(ts(K["before"][:], exc[:], -1.0, 0.0, ALU.add, ALU.max))
            own.add(ts(K["more"][:], inc[:, EXPERTS - 1:EXPERTS], -float(PEELED), None, ALU.add))
            own.add(ts(own_[:], exc[:], bl[:], None, ALU.is_le))
            step(ts(t0[:], inc[:], bl[:], None, ALU.is_le))
            step(nc.vector.tensor_tensor(own_[:], own_[:], t0[:], ALU.subtract))
            step(nc.vector.tensor_tensor_scan(start[:], ones[:, 0:EXPERTS], count[:], 0.0, ALU.mult, ALU.add))
            step(nc.vector.tensor_tensor(start[:], start[:], count[:], ALU.subtract))
            for j, v in enumerate((ex, exc, inc, last, start)):
                own.add(nc.vector.tensor_tensor_reduce(out=scr[:, j, :], in0=own_[:], in1=v[:], scale=1.0, scalar=0.0,
                                                       op0=ALU.mult, op1=ALU.add, accum_out=of[:, j:j + 1]))
            own.settle()
            own.add(nc.vector.tensor_copy(cols[:, 0:1], of[:, 0:1]))
            step(nc.vector.tensor_tensor(cols[:, 1:2], bl[:], of[:, 1:2], ALU.subtract))
            step(ts(cols[:, 1:2], cols[:, 1:2], float(P), of[:, 3:4], ALU.mult, ALU.min))
            own.add(nc.vector.tensor_tensor(cols[:, 4:5], cols[:, 1:2], of[:, 4:5], ALU.add))
            step(nc.vector.scalar_tensor_tensor(shift[:], ex[:], -float(REGION), start[:], ALU.mult, ALU.add))
            step(nc.vector.scalar_tensor_tensor(cols[:, 1:2], of[:, 0:1], float(REGION), cols[:, 1:2], ALU.mult, ALU.add))
            step(ts(of[:, 2:3], of[:, 2:3], -1.0, bl[:], ALU.add, ALU.is_equal))
            for j, most in ((2, EXPERTS - 2), (3, EXPERTS - 3)):
                step(ts(cols[:, j:j + 1], of[:, 0:1], most + 0.5, None, ALU.is_lt))
                step(nc.vector.tensor_tensor(cols[:, j:j + 1], cols[:, j:j + 1], of[:, 2:3], ALU.mult))
            nc.vector.memset(scr[:], 0.0).then_inc(cols_ready, 1)
            dve.wait_ge(turned, 1)
            own.add(nc.vector.tensor_copy(tab[:, 0:4, :].rearrange("p q b -> p (q b)"), ps[0][0:1, :]))
            own.add(nc.vector.tensor_copy(tab[:, 4, :], ps[1][0:1, 0:P]))
            step(ts(pe_[:], K["dest"][:], REGION.bit_length() - 1, None, ALU.logical_shift_right))
            own.add(nc.vector.tensor_copy(pf[:], pe_[:]))
            step(nc.vector.tensor_copy(df[:], K["dest"][:]))
            wide = lambda a: a.unsqueeze(1).broadcast_to([P, 2 * TILES, EXPERTS])
            step(nc.vector.tensor_tensor(match[:], pf[:].unsqueeze(2).broadcast_to([P, 2 * TILES, EXPERTS]), wide(ex[:]),
                                         ALU.is_equal))
            step(nc.vector.tensor_tensor(match[:], match[:], wide(shift[:]), ALU.mult))
            step(nc.vector.tensor_reduce(pf[:], match[:], AX, ALU.add))
            step(nc.vector.tensor_tensor(df[:], df[:], pf[:], ALU.add))
            own.add(nc.vector.tensor_copy(K["dest"][:], df[:]))


def experts_phase(nc, w1, w3, w2, xs, ys, K):
    EXPERT, ROW, NEXT, AFTER, OUT = range(5)
    with ExitStack() as ctx:
        sb = lambda n, s, d=F32: ctx.enter_context(nc.sbuf_tensor(n, s, d))
        psum = lambda n: ctx.enter_context(nc.psum_tensor(n, [P, 512], F32))
        sem = semaphores(nc, ctx, "experts_")
        ident, tab = K["ident"], K["tab"]
        NP, NP2 = 8, 4
        wh = [sb(f"wh{i}", [P, NP, 2, FF], F32R) for i in range(2)]
        wy = [sb(f"wy{i}", [P, KF, D], F32R) for i in range(2)]
        wraw, wraw2 = sb("e_raw", [P, NP, 2 * FF]), sb("e_raw2", [P, NP2, D])
        xb = sb("xb", [P, D])
        xT = [sb(f"xT{i}", [P, KD, P], F32R) for i in range(2)]
        sg, hb = sb("sg", [P, FF]), sb("hb", [P, FF])
        hT = [sb(f"e_hT{i}", [P, FF], F32R) for i in range(2)]
        ob = sb("ob", [P, D])
        flat = lambda a: a.rearrange("p a b -> p (a b)")
        psX = [psum("psX0"), psum("psX1")]
        ps1, ps3, psH = psum("ps1"), psum("ps3"), psum("psHt")
        psO = [psum("psO0"), psum("psO1")]
        NAMES = ("high", "low", "low2", "used", "used2", "x_loaded", "x_turned", "x_high", "x_low", "silu", "h_ready",
                 "h_turned", "h_high", "h_low", "out0", "out1", "out_stored", "high2", "passed", "released")
        S = {n: sem(n) for n in NAMES}
        raw_loaded = [sem(f"raw_loaded{i}") for i in range(NP)]
        raw2_loaded = [sem(f"raw2_loaded{i}") for i in range(NP2)]
        block = ctx.enter_context(nc.Block())

        def entry(eng, what, b, top=None):
            top = top or (EXPERTS - 1, (EXPERTS - 1) * REGION + SEQ - P, 1, 1, 2 * SEQ)[what]
            return eng.value_load(tab[0:1, what, bass.ds(b, 1)], min_val=0, max_val=top)

        def load_w(eng, e, i):
            w, r = (w1, i) if i < 4 else (w3, i - 4)
            src = w[0, bass.ds(e, 1), r * 2 * P:(r + 1) * 2 * P, :].rearrange("o (k p) f -> p (o k) f", p=P)
            eng.dma_start(wraw[:, i, :].rearrange("p (k f) -> p k f", k=2), src).then_inc(raw_loaded[i], 16)

        def load_w2(eng, e, i):
            src = w2[0, bass.ds(e, 1), i * P:(i + 1) * P, :].rearrange("o p f -> p (o f)")
            eng.dma_start(wraw2[:, i, :], src).then_inc(raw2_loaded[i], 16)

        def blocks(eng, run):
            nb = eng.value_load(K["more"][0:1, 0:1], min_val=EXPERTS - PEELED, max_val=MAXB - PEELED) + PEELED
            for b in range(PEELED):
                run(b, b)
            with eng.Fori(PEELED, nb) as b:
                run(b, PEELED)
            return nb

        @block.sync
        def _(sp):
            def store(j, n):
                sp.wait_ge(S["out0"], j + 1)
                sp.wait_ge(S["out1"], j + 1)
                sp.sem_inc(S["passed"], 1)
                sp.dma_start(ys[bass.ds(entry(sp, OUT, j), P), :], ob[:]).then_inc(S["out_stored"], 16)

            def run(b, n):
                if n:
                    sp.wait_ge(S["x_turned"], b + 0)
                    sp.sem_inc(S["passed"], 1)
                sp.dma_start(xb[:], xs[bass.ds(entry(sp, ROW, b), P), :]).then_inc(S["x_loaded"], 16)
                if n == 3:
                    store(b - 3, n)

            nb = blocks(sp, run)
            for j in range(3):
                store(nb + (j - 3), 3)
            sp.wait_ge(S["out_stored"], nb * 16)
            sp.sem_inc(S["passed"], 1)

        @block.gpsimd
        def _(pool):
            def split(e, more):
                if not isinstance(e, int) or e:
                    before = pool.value_load(K["before"][0:1, bass.ds(e, 1)], min_val=0, max_val=MAXB)
                for i in range(NP2):
                    pool.wait_ge(raw2_loaded[i], e * 16 + 16)
                    if not isinstance(e, int) or e:
                        pool.wait_ge(S["used2"], before * NP2 + (i + 1))
                    pool.sem_inc(S["released"], 1)
                    nc.gpsimd.tensor_copy(wy[0][:, i, :], wraw2[:, i, :]).then_inc(S["high2"], 1)
                    pool.wait_ge(S["high2"], e * NP2 + (i + 1))
                    nc.gpsimd.tensor_tensor(wy[1][:, i, :], wraw2[:, i, :], wy[0][:, i, :].bitcast(F32), ALU.subtract
                                            ).then_inc(S["low2"], 1)
                    if more:
                        pool.wait_ge(S["low2"], e * NP2 + (i + 1))
                        pool.sem_inc(S["released"], 1)
                        load_w2(pool, e + 1, i)

            for i in range(NP2):
                load_w2(pool, 0, i)
            split(0, True)
            with pool.Fori(1, EXPERTS - 1) as e:
                split(e, True)
            split(EXPERTS - 1, False)

        def next_expert(eng, b, pieces, load=None):
            with eng.If(entry(eng, NEXT, b) == 1):
                pieces(entry(eng, EXPERT, b, EXPERTS - 2) + 1, b)
            if load:
                with eng.If(entry(eng, AFTER, b) == 1):
                    load(entry(eng, EXPERT, b, EXPERTS - 3) + 2)

        @block.scalar
        def _(act):
            def pieces(e, b=None):
                for i in range(NP):
                    act.wait_ge(raw_loaded[i], e * 16 + 16)
                    if b is not None:
                        act.wait_ge(S["used"], b * NP + (i + 1))
                    nc.scalar.copy(flat(wh[0][:, i]), wraw[:, i, :]).then_inc(S["high"], 1)

            def load(e):
                for i in range(NP):
                    act.wait_ge(S["low"], e * NP + (i + 1 - NP))
                    act.sem_inc(S["passed"], 1)
                    load_w(act, e, i)

            def out(j, n):
                act.wait_ge(S["used2"], j * NP2 + NP2)
                if n:
                    act.wait_ge(S["out_stored"], j * 16)
                nc.scalar.copy(ob[:, 0:512], psO[0][:]).then_inc(S["out0"], 1)

            def h_high(j):
                act.wait_ge(S["h_turned"], j + 1)
                nc.scalar.copy(hT[0][:], psH[:]).then_inc(S["h_high"], 1)

            def run(b, n):
                act.wait_ge(S["x_turned"], b + 1)
                if n:
                    act.wait_ge(S["used"], b * NP)
                for i in range(2):
                    last = nc.scalar.copy(flat(xT[0][:, 4 * i:4 * i + 4]), psX[i][:])
                last.then_inc(S["x_high"], 1)
                if n >= 2:
                    out(b - 2, n - 2)
                if n >= 1:
                    h_high(b - 1)
                act.wait_ge(S["used"], b * NP + 4)
                if n:
                    act.wait_ge(S["h_ready"], b + 0)
                nc.scalar.activation(sg[:], ps1[:], ACT.Silu).then_inc(S["silu"], 1)
                next_expert(act, b, pieces, load)

            for i in range(NP):
                load_w(act, 0, i)
            pieces(0)
            for i in range(NP):
                act.wait_ge(S["low"], i + 1)
                load_w(act, 1, i)
            nb = blocks(act, run)
            out(nb - 2, 3)
            h_high(nb - 1)
            out(nb - 1, 3)

        @block.tensor
        def _(pe):
            def turn(b, n):
                pe.wait_ge(S["x_loaded"], b * 16 + 16)
                if n:
                    pe.wait_ge(S["x_low"], b + 0)
                for k in range(KD):
                    mm = nc.tensor.transpose(psX[k // 4][:, (k % 4) * P:(k % 4 + 1) * P], xb[:, k * P:(k + 1) * P], ident[:])
                mm.then_inc(S["x_turned"], 1)

            def first_products(b, n):
                e8 = pe.snap(entry(pe, EXPERT, b) * NP)
                pe.wait_ge(S["x_low"], b + 1)
                if n:
                    pe.wait_ge(S["h_ready"], b + 0)
                for i in range(NP):
                    ps, r = (ps1, i) if i < 4 else (ps3, i - 4)
                    pe.wait_ge(S["low"], e8 + (i + 1))
                    for k in range(2):
                        for l, w in ((1, 0), (0, 1), (0, 0)):
                            mm = nc.tensor.matmul(ps[:], xT[l][:, 2 * r + k, :], wh[w][:, i, k, :],
                                                  start=(r == 0 and k == 0 and l == 1),
                                                  stop=(r == 3 and k == 1 and l == 0 and w == 0))
                    mm.then_inc(S["used"], 1)

            def second_product(j, n):
                e4 = pe.snap(entry(pe, EXPERT, j) * NP2)
                pe.wait_ge(S["h_low"], j + 1)
                if n:
                    pe.wait_ge(S["out0"], j + 0)
                    pe.wait_ge(S["out1"], j + 0)
                for k in range(KF):
                    pe.wait_ge(S["low2"], e4 + (k + 1))
                    for o in range(2):
                        for l, w in ((1, 0), (0, 1), (0, 0)):
                            mm = nc.tensor.matmul(psO[o][:], hT[l][:, k * P:(k + 1) * P], wy[w][:, k, o * 512:(o + 1) * 512],
                                                  start=(k == 0 and l == 1), stop=(k == KF - 1 and l == 0 and w == 0))
                    mm.then_inc(S["used2"], 1)

            def turn_h(j):
                pe.wait_ge(S["h_ready"], j + 1)
                for k in range(KF):
                    mm = nc.tensor.transpose(psH[:, k * P:(k + 1) * P], hb[:, k * P:(k + 1) * P], ident[:])
                mm.then_inc(S["h_turned"], 1)

            def run(b, n):
                turn(b, n)
                if n >= 2:
                    second_product(b - 2, n - 2)
                if n >= 1:
                    turn_h(b - 1)
                first_products(b, n)

            nb = blocks(pe, run)
            second_product(nb - 2, 3)
            turn_h(nb - 1)
            second_product(nb - 1, 3)

        @block.vector
        def _(dve):
            def pieces(e, b=None):
                for i in range(NP):
                    dve.wait_ge(S["high"], e * NP + (i + 1))
                    nc.vector.tensor_tensor(flat(wh[1][:, i]), wraw[:, i, :], flat(wh[0][:, i]).bitcast(F32), ALU.subtract
                                            ).then_inc(S["low"], 1)

            def out(j, n):
                dve.wait_ge(S["used2"], j * NP2 + NP2)
                if n:
                    dve.wait_ge(S["out_stored"], j * 16)
                nc.vector.tensor_copy(ob[:, 512:1024], psO[1][:]).then_inc(S["out1"], 1)

            def h_low(j):
                dve.wait_ge(S["h_high"], j + 1)
                nc.vector.tensor_tensor(hT[1][:], psH[:], hT[0][:].bitcast(F32), ALU.subtract).then_inc(S["h_low"], 1)

            def run(b, n):
                dve.wait_ge(S["x_high"], b + 1)
                for i in range(2):
                    last = nc.vector.tensor_tensor(flat(xT[1][:, 4 * i:4 * i + 4]), psX[i][:],
                                                   flat(xT[0][:, 4 * i:4 * i + 4]).bitcast(F32), ALU.subtract)
                last.then_inc(S["x_low"], 1)
                if n >= 2:
                    out(b - 2, n - 2)
                if n >= 1:
                    h_low(b - 1)
                dve.wait_ge(S["silu"], b + 1)
                dve.wait_ge(S["used"], b * NP + NP)
                if n:
                    dve.wait_ge(S["h_turned"], b + 0)
                nc.vector.tensor_tensor(hb[:], sg[:], ps3[:], ALU.mult).then_inc(S["h_ready"], 1)
                next_expert(dve, b, pieces)

            pieces(0)
            nb = blocks(dve, run)
            out(nb - 2, 3)
            h_low(nb - 1)
            out(nb - 1, 3)


def final_phase(nc, final_w, x1dram, ys, outd, K):
    with ExitStack() as ctx:
        sb = lambda n, s, d=F32: ctx.enter_context(nc.sbuf_tensor(n, s, d))
        sem = semaphores(nc, ctx, "final_")
        dest, gates = K["dest"], K["gates"]
        r = [[sb(f"r{i}{j}", [P, D]) for j in range(2)] for i in range(2)]
        x1 = [sb(f"fx{i}", [P, D]) for i in range(2)]
        sq = [sb(f"fsq{i}", [P, D]) for i in range(2)]
        fo = [sb(f"fo{i}", [P, D]) for i in range(2)]
        g2row, fw = sb("g2row", [P, D]), sb("fw", [P, D])
        di = [sb(f"di{i}", [P, 2], U32) for i in range(2)]
        gi = [sb(f"gi{i}", [P, 2]) for i in range(2)]
        st = [sb(f"fst{i}", [P, 4]) for i in range(2)]
        minus_half, eps = sb("f_minus_half", [P, 1]), sb("f_eps", [P, 1])
        ps = [ctx.enter_context(nc.psum_tensor(f"f_ps{i}", [P, 512], F32)) for i in range(2)]
        NAMES = ("rows_done", "rows_copied", "w_loaded", "index", "scaled", "mixed", "gated", "added", "squared", "mean",
                 "rstd", "normed", "consts", "passed")
        S = {n: sem(n) for n in NAMES}
        gathered = [sem(f"gathered{i}") for i in range(2)]
        x_loaded = [sem(f"x_loaded{i}") for i in range(2)]
        stored = [sem(f"stored{i}") for i in range(2)]
        block = ctx.enter_context(nc.Block())

        def pairs(eng, run):
            run(0, 0, 0)
            run(1, 1, 0)
            with eng.Fori(1, TILES // 2) as p:
                for i in range(2):
                    run(p * 2 + i, i, 1)

        @block.sync
        def _(sp):
            sp.dma_start(fw[:], final_w.rearrange("(o d) -> o d", o=1).broadcast_to([P, D])).then_inc(S["w_loaded"], 16)

            def load(t, i, n):
                if n:
                    sp.wait_ge(S["normed"], t - 1)
                sp.dma_start(x1[i][:], x1dram[bass.ds(t * P, P), :]).then_inc(x_loaded[i], 16)

            pairs(sp, load)

        @block.gpsimd
        def _(pool):
            nc.gpsimd.memset(minus_half[:], -0.5).then_inc(S["consts"], 1)
            nc.gpsimd.memset(eps[:], EPS).then_inc(S["consts"], 1)
            pool.wait_ge(S["consts"], 2)

            def gather(t, i, n):
                pool.wait_ge(S["index"], t + 1)
                if n:
                    pool.wait_ge(S["added"], t - 1)
                pool.sem_inc(S["passed"], 1)
                for j in range(2):
                    nc.gpsimd.indirect_dma_start(r[i][j][:], None, ys[0:2 * SEQ, :], bass.IndirectOffsetOnAxis(ap=di[i][:, j:j + 1], axis=0)
                                                 ).then_inc(gathered[i], 16)

            def add(t, i):
                pool.wait_ge(x_loaded[i], (t - i) * 8 + 16)
                pool.wait_ge(S["gated"], t + 1)
                nc.gpsimd.tensor_tensor(x1[i][:], x1[i][:], r[i][0][:], ALU.add).then_inc(S["added"], 1)

            def rstd(t, i):
                pool.wait_ge(S["squared"], t + 1)
                nc.gpsimd.tensor_tensor(st[i][:, 1:2], st[i][:, 0:1], eps[:], ALU.add).then_inc(S["mean"], 1)
                pool.wait_ge(S["mean"], t + 1)
                nc.gpsimd.tensor_tensor(st[i][:, 2:3], st[i][:, 1:2], minus_half[:], ALU.pow).then_inc(S["rstd"], 1)

            gather(0, 0, 0)
            gather(1, 1, 0)
            with pool.Fori(0, TILES // 2 - 1) as p:
                for i in range(2):
                    t = p * 2 + i
                    add(t, i)
                    gather(t + 2, i, 1)
                    rstd(t, i)
            for i in range(2):
                add(TILES - 2 + i, i)
                rstd(TILES - 2 + i, i)

        @block.scalar
        def _(act):
            def scale(t, i, n):
                act.wait_ge(gathered[i], (t - i) * 16 + 32)
                nc.scalar.activation(r[i][0][:], r[i][0][:], ACT.Copy, scale=gi[i][:, 0:1]).then_inc(S["scaled"], 1)

            def square(t, i, n):
                act.wait_ge(S["added"], t + 1)
                nc.scalar.activation(sq[i][:], x1[i][:], ACT.Square, scale=D ** -0.5, accum_out=st[i][:, 0:1]
                                     ).then_inc(S["squared"], 1)

            def store(t, i):
                act.wait_ge(S["normed"], t + 1)
                act.sem_inc(S["passed"], 1)
                act.dma_start(outd[0, bass.ds(t * P, P), :], fo[i][:]).then_inc(stored[i], 16)

            scale(0, 0, 0)
            square(0, 0, 0)
            scale(1, 1, 0)
            square(1, 1, 0)
            with act.Fori(1, TILES // 2) as p:
                for i in range(2):
                    t = p * 2 + i
                    scale(t, i, 1)
                    store(t - 2, i)
                    square(t, i, 1)
            for i in range(2):
                store(TILES - 2 + i, i)
            for i in range(2):
                act.wait_ge(stored[i], TILES // 2 * 16)

        @block.tensor
        def _(pe):
            for i in range(2):
                for k in range(4):
                    o = 5 * KD + 4 * i + k
                    mm = nc.tensor.matmul(ps[i][:, k * P:(k + 1) * P], K["mod"][:, o:o + 1].broadcast_to([P, P]),
                                          K["ident"][:], start=True, stop=True)
                mm.then_inc(S["rows_done"], 1)

        @block.vector
        def _(dve):
            def index(t, i, n):
                if n:
                    dve.wait_ge(S["mixed"], t - 1)
                    dve.wait_ge(gathered[i], (t - i) * 16)
                    dve.sem_inc(S["passed"], 1)
                nc.vector.tensor_copy(gi[i][:], gates[:, bass.ds(t * 2, 2)])
                nc.vector.tensor_copy(di[i][:], dest[:, bass.ds(t * 2, 2)]).then_inc(S["index"], 1)

            def mix(t, i):
                dve.wait_ge(S["scaled"], t + 1)
                nc.vector.scalar_tensor_tensor(r[i][0][:], r[i][1][:], gi[i][:, 1:2], r[i][0][:], ALU.mult, ALU.add
                                               ).then_inc(S["mixed"], 1)
                dve.wait_ge(S["mixed"], t + 1)
                nc.vector.tensor_tensor(r[i][0][:], r[i][0][:], g2row[:], ALU.mult).then_inc(S["gated"], 1)

            def norm(t, i, n):
                dve.wait_ge(S["rstd"], t + 1)
                if n:
                    dve.wait_ge(stored[i], (t - i) * 8)
                nc.vector.scalar_tensor_tensor(fo[i][:], x1[i][:], st[i][:, 2:3], fw[:], ALU.mult, ALU.mult
                                               ).then_inc(S["normed"], 1)

            index(0, 0, 0)
            index(1, 1, 0)
            for i in range(2):
                dve.wait_ge(S["rows_done"], i + 1)
                nc.vector.tensor_copy(g2row[:, i * 512:(i + 1) * 512], ps[i][:]).then_inc(S["rows_copied"], 1)
            dve.wait_ge(S["rows_copied"], 2)
            dve.wait_ge(S["w_loaded"], 16)
            for i in range(2):
                mix(i, i)
                index(i + 2, i, 1)
                norm(i, i, 0)
            with dve.Fori(1, TILES // 2 - 1) as p:
                for i in range(2):
                    t = p * 2 + i
                    mix(t, i)
                    index(t + 2, i, 1)
                    norm(t, i, 1)
            for i in range(2):
                mix(TILES - 2 + i, i)
                norm(TILES - 2 + i, i, 1)


def build(nc, a, out, xs, ydram, x1dram, ys):
    with ExitStack() as ctx:
        sb = lambda n, s, d=F32: ctx.enter_context(nc.sbuf_tensor(n, s, d))
        keep = lambda *which: {n: sb("k_" + n, s, d) for n, s, d in which}
        K = keep(
            ("ident", [P, P], F32), ("upper", [P, P], F32), ("ones", [P, P], F32), ("mask", [P, P], F32),
            ("identb", [P, P], BF16), ("maskb", [P, P], BF16), ("strictb", [P, P], BF16), ("onesb", [P, P], BF16),
            ("mod", [P, 6 * KD], F32), ("a1", [P, KD], F32), ("a2", [P, KD], F32),
            ("conv", [P, TAPS + 1, CB], F32), ("scratch", [P, 2], F32))
        mod_phase(nc, a["c"], a["ada_w"], a["ada_b"], a["norm_mix_w"], a["norm_ffn_w"], a["ssm_conv_w"],
                  a["ssm_conv_b"], xs, K)
        mixer_phase(nc, a["x"], a["ssm_in_w"], a["ssm_dt_bias"], a["ssm_a_log"], a["ssm_d"], a["ssm_norm_w"], ydram, K)
        K.update(keep(
            ("dest", [P, 2 * TILES], U32), ("gates", [P, 2 * TILES], F32), ("count", [P, EXPERTS], F32),
            ("tab", [1, 5, P], I32), ("before", [P, EXPERTS], I32), ("more", [P, 1], I32)))
        out_phase(nc, a["x"], a["ssm_out_w"], a["moe_group_w"], a["moe_group_b"], a["moe_expert_w"],
                  a["moe_expert_b"], ydram, x1dram, xs, K)
        plan_phase(nc, K)
        experts_phase(nc, a["moe_w1"], a["moe_w3"], a["moe_w2"], xs, ys, K)
        final_phase(nc, a["final_norm_w"], x1dram, ys, out, K)


USED = ("x", "c", "ada_w", "ada_b", "norm_mix_w", "norm_ffn_w", "ssm_in_w", "ssm_conv_w", "ssm_conv_b", "ssm_dt_bias",
        "ssm_a_log", "ssm_d", "ssm_norm_w", "ssm_out_w", "moe_group_w", "moe_group_b", "moe_expert_w", "moe_expert_b",
        "moe_w1", "moe_w3", "moe_w2", "final_norm_w")


def kernel(**inputs):
    import numpy as np
    import concourse.bacc as bacc
    from concourse.bass_utils import run_bass_kernel_spmd

    nc = bacc.Bacc("TRN2", target_bir_lowering=False, num_devices=1)
    arrays, args = {}, {}
    for name in USED:
        arrays[f"in_{name}"] = np.ascontiguousarray(inputs[name])
        args[name] = nc.dram_tensor(f"in_{name}", arrays[f"in_{name}"].shape, F32, kind="ExternalInput").ap()
    out = nc.dram_tensor("out", (1, SEQ, D), F32, kind="ExternalOutput").ap()
    scratch = lambda name, shape: nc.dram_tensor(name, shape, F32, kind="Internal").ap()
    build(nc, args, out, scratch("xs", (EXPERTS * REGION, D)), scratch("y_inner", (SEQ, DI)),
          scratch("x1", (SEQ, D)), scratch("ys", (2 * SEQ + P, D)))
    r = run_bass_kernel_spmd(nc, [arrays], core_ids=[0])
    return r.results[0]["out"]
```

```python
from contextlib import ExitStack

import concourse.bass as bass
from concourse import mybir

F32 = mybir.dt.float32
F32R = mybir.dt.float32r
BF16 = mybir.dt.bfloat16
I32 = mybir.dt.int32
U32 = mybir.dt.uint32
ALU = mybir.AluOpType
ACT = mybir.ActivationFunctionType
AX = mybir.AxisListType.X

P = 128
D = 1024
KD = D // P
SEQ = 2048
TILES = SEQ // P
HALVES = 2
HT = TILES // HALVES
HTOK = HT * P
EPS = 1e-6

DI = 2048
G = 8
GW = DI // G
HG = 4
HEADS = G * HG
PD = 64
N = 128
CONV_DIM = DI + 2 * G * N
CB = CONV_DIM // P
TAPS = 4
KI = DI // P
SUP = 512
CS = SUP // P
PIECES = 6

GROUPS = 4
EPG = 8
EXPERTS = GROUPS * EPG
FF = 512
KF = FF // P
REGION = SEQ
BIG = 1e30


def semaphores(nc, ctx, phase):
    taken = []

    def take(name):
        taken.append(nc.alloc_semaphore(phase + name))
        return taken[-1]

    def give_back():
        nc.clear_and_free_semaphores(taken)
        nc.all_engine_barrier()

    ctx.callback(give_back)
    return take


class Steps:

    def __init__(self, eng, sem, base=0):
        self.eng, self.sem, self.base, self.n = eng, sem, base, 0

    def add(self, ins):
        ins.then_inc(self.sem, 1)
        self.n += 1

    def settle(self):
        self.eng.wait_ge(self.sem, self.base + self.n)


def mod_phase(nc, c, ada_w, ada_b, norm_mix_w, norm_ffn_w, conv_w, conv_b, K):
    NV = KD + 6 * KD + 2 * KD + CB
    with ExitStack() as ctx:
        sb = lambda n, s, d=F32: ctx.enter_context(nc.sbuf_tensor(n, s, d))
        sem = semaphores(nc, ctx, "mod_")
        W = [sb(f"ada_w{i}", [P, KD, D]) for i in range(3)]
        acc = [sb(f"mod_sum{i}", [P, D]) for i in range(2)]
        vrows = sb("vrows", [NV, P])
        trows = sb("trows", [P, P])
        vcols = sb("vcols", [P, NV])
        cs = sb("cs", [P, KD])
        ps = ctx.enter_context(nc.psum_tensor("ps_mod", [P, 512], F32))
        pv = ctx.enter_context(nc.psum_tensor("ps_vec", [P, 512], F32))
        rows_loaded, w_loaded = sem("rows_loaded"), [sem(f"w_loaded{i}") for i in range(3)]
        turned, cols_ready, cs_ready = sem("turned"), sem("cols_ready"), sem("cs_ready")
        mod_done, consts_ready, psteps, vsteps = sem("mod_done"), sem("consts_ready"), sem("psteps"), sem("vsteps")
        summed = sem("summed")
        ident, upper = K["ident"], K["upper"]
        mod = K["mod"]
        block = ctx.enter_context(nc.Block())

        @block.sync
        def _(sp):
            r = 0
            for src in (c, ada_b, norm_mix_w, norm_ffn_w, conv_b):
                src = src.rearrange("o (k p) -> (o k) p", p=P)
                sp.dma_start(vrows[r:r + src.shape[0], :], src).then_inc(rows_loaded, 16)
                r += src.shape[0]
            sp.dma_start(trows[:], conv_w[0].rearrange("t (b p) -> (t b) p", p=P)).then_inc(rows_loaded, 16)
            for j in range(6):
                if j >= 3:
                    sp.wait_ge(summed, j - 2)
                sp.dma_start(W[j % 3][:], ada_w[0, :, j * D:(j + 1) * D].rearrange("(k p) n -> p k n", p=P)
                             ).then_inc(w_loaded[j % 3], 16)

        @block.gpsimd
        def _(pool):
            own = Steps(pool, psteps)
            own.add(nc.gpsimd.memset(ident[:], 0.0))
            own.add(nc.gpsimd.memset(upper[:], 1.0))
            own.add(nc.gpsimd.memset(K["ones"][:], 1.0))
            own.add(nc.gpsimd.memset(K["mask"][:], 0.0))
            own.settle()
            own.add(nc.gpsimd.affine_select(out=ident[:], in_=ident[:], compare_op=ALU.not_equal, fill=1.0,
                                            base=0, pattern=[[-1, P]], channel_multiplier=1))
            own.add(nc.gpsimd.affine_select(out=upper[:], in_=upper[:], compare_op=ALU.is_ge, fill=0.0,
                                            base=0, pattern=[[1, P]], channel_multiplier=-1))
            own.add(nc.gpsimd.affine_select(out=K["mask"][:], in_=K["mask"][:], compare_op=ALU.is_ge, fill=-BIG,
                                            base=0, pattern=[[1, P]], channel_multiplier=-1))
            own.settle()
            own.add(nc.gpsimd.tensor_copy(K["identb"][:], ident[:]))
            own.add(nc.gpsimd.tensor_copy(K["maskb"][:], K["mask"][:]))
            own.add(nc.gpsimd.tensor_tensor(K["strictb"][:], upper[:], ident[:], ALU.subtract))
            own.add(nc.gpsimd.tensor_copy(K["onesb"][:], K["ones"][:]))
            own.settle()
            pool.sem_inc(consts_ready, 1)

        @block.scalar
        def _(act):
            act.wait_ge(cols_ready, 1)
            nc.scalar.activation(cs[:], vcols[:, 0:KD], ACT.Silu).then_inc(cs_ready, 1)

        @block.tensor
        def _(pe):
            pe.wait_ge(consts_ready, 1)
            pe.wait_ge(rows_loaded, 6 * 16)
            nc.tensor.transpose(pv[:, 0:NV], vrows[:], ident[0:NV, 0:NV]).then_inc(turned, 1)
            nc.tensor.transpose(pv[:, P:2 * P], trows[:], ident[:]).then_inc(turned, 1)
            for j in range(6):
                pe.wait_ge(summed, j + 1)
                for m in range(KD):
                    mm = nc.tensor.matmul(ps[:, j * KD + m:j * KD + m + 1], acc[j % 2][:, m * P:(m + 1) * P],
                                          K["ones"][:, 0:1], start=True, stop=True)
                mm.then_inc(mod_done, 1)

        @block.vector
        def _(dve):
            own = Steps(dve, vsteps)
            dve.wait_ge(turned, 2)
            nc.vector.tensor_copy(vcols[:], pv[:, 0:NV]).then_inc(cols_ready, 1)
            own.add(nc.vector.tensor_scalar(K["conv"][:, 0:TAPS, :], pv[:, P:2 * P].rearrange("p (t b) -> p t b", t=TAPS),
                                            0.5, None, ALU.mult))
            dve.wait_ge(cols_ready, 1)
            own.add(nc.vector.tensor_scalar(K["conv"][:, TAPS, :], vcols[:, 9 * KD:9 * KD + CB], 0.5, None, ALU.mult))
            dve.wait_ge(cs_ready, 1)
            for j in range(6):
                dve.wait_ge(w_loaded[j % 3], 16 * (j // 3 + 1))
                if j >= 2:
                    dve.wait_ge(mod_done, j - 1)
                own.add(nc.vector.tensor_scalar(acc[j % 2][:], W[j % 3][:, 0, :], cs[:, 0:1], None, ALU.mult))
                for k in range(1, KD):
                    own.settle()
                    ins = nc.vector.scalar_tensor_tensor(acc[j % 2][:], W[j % 3][:, k, :], cs[:, k:k + 1], acc[j % 2][:],
                                                         ALU.mult, ALU.add)
                    if k < KD - 1:
                        own.add(ins)
                ins.then_inc(summed, 1)
            dve.wait_ge(mod_done, 6)
            own.add(nc.vector.tensor_tensor(mod[:], ps[:, 0:6 * KD], vcols[:, KD:7 * KD], ALU.add))
            own.settle()
            own.add(nc.vector.scalar_tensor_tensor(K["a1"][:], mod[:, KD:2 * KD], 1.0, vcols[:, 7 * KD:8 * KD],
                                                   ALU.add, ALU.mult))
            own.add(nc.vector.scalar_tensor_tensor(K["a2"][:], mod[:, 4 * KD:5 * KD], 1.0, vcols[:, 8 * KD:9 * KD],
                                                   ALU.add, ALU.mult))


def mixer_phase(nc, x, in_w, dt_bias, a_log, d_skip, norm_w, ydram, xs, K):
    with ExitStack() as ctx:
        sb = lambda n, s, d=F32: ctx.enter_context(nc.sbuf_tensor(n, s, d))
        psum = lambda n: ctx.enter_context(nc.psum_tensor(n, [P, 512], F32))
        sem = semaphores(nc, ctx, "mixer_")
        ident, upper, ones, maskb, identb = (K[x] for x in ("ident", "upper", "ones", "maskb", "identb"))
        hT = [sb(f"hT{i}", [P, KD, HTOK], F32R) for i in range(2)]
        wfm = [sb(f"wfm{i}", [P, 4, KD, P], F32R) for i in range(2)]
        wz = [sb(f"wz{i}", [P, KD, GW], F32R) for i in range(2)]
        wraw = sb("wraw", [P, 3, KD * P])
        raw = sb("raw", [P, 2, 3 + SUP])
        cv = sb("cv", [P, 2, SUP])
        fm = [sb(f"fm{i}", [P, 4, SUP]) for i in range(2)]
        zs = sb("zs", [P, CS, GW])
        zero = sb("zero", [P, D])
        tok = [sb(f"tok{i}", [P, 3 * P]) for i in range(2)]
        gm = [sb(f"gm{i}", [P, HG, P]) for i in range(2)]
        xdt = [sb(f"xdt{i}", [P, HG, PD]) for i in range(2)]
        xde = [sb(f"xde{i}", [P, HG, PD]) for i in range(2)]
        xd = [sb(f"xd{i}", [P, HG, PD]) for i in range(2)]
        yt = [sb(f"yt{i}", [P, HG, PD]) for i in range(2)]
        ysq = sb("ysq", [P, GW])
        yo = [sb(f"yo{i}", [P, GW]) for i in range(2)]
        ssq = sb("ssq", [P, 6])
        state = sb("state", [P, HG, PD])
        states = sb("states", [P, G, HG * PD])
        hist = sb("hist", [P, 12, G])
        histg = sb("histg", [P, 2, 4, 3])
        nw = sb("nw", [P, DI])
        vecg = sb("vecg", [P, TAPS + 1, 4])
        dbias = sb("dbias", [P, HEADS])
        aneg = sb("aneg", [P, HEADS])
        W8 = HT * HEADS
        pk = sb("pk", [P, 5 * HT + 1, HEADS])
        pkg = sb("pkg", [P, 5 * HT + 1, HG])
        da = [sb(f"da{i}", [P, HT, HEADS], F32R) for i in range(2)]
        dag = [sb(f"dag{i}", [P, HT, HG], F32R) for i in range(2)]
        wdt = sb("wdt", [P, KD, HEADS])
        wdts = [sb(f"wdts{i}", [P, KD, HEADS], F32R) for i in range(2)]
        upr = sb("upr", [P, P], F32R)
        tss = sb("tss", [P, 2, 3])
        minus_half = sb("minus_half", [P, 1])
        eps = sb("eps", [P, 1])
        flat = lambda a: a.rearrange("p a b -> p (a b)")
        xt = [flat(fm[i][:, 0:2, :]) for i in range(2)]
        xsq = [flat(fm[0][:, 2:4, :]), flat(zs[:])]
        v = [a.rearrange("p (k n) -> p k n", k=KD) for a in (flat(fm[1][:, 2:4, :]), flat(cv[:]))]
        T = [cv[:, i // 2, (i % 2) * W8:(i % 2 + 1) * W8] for i in range(4)]
        T += [zs[:, i, :] for i in range(4)]
        row = lambda i: flat(pk[:, i * HT:(i + 1) * HT, :])
        DT, NAC, EAC, DTE, CDEC = range(5)
        dtcol = lambda q, c: pkg[:, q * HT + c, :]

        psF = [psum("psF0"), psum("psF1")]
        psZ = psum("psZ")
        psT = [psum("psT0"), psum("psT1")]
        psS = [psum("psS0"), psum("psS1")]
        turned_x = [psF, psT]
        psY = psum("psY")
        NAMES = ("vec_loaded", "x_sq", "x_scaled", "x_turned", "v_ready", "v_high", "h_ready", "wdt_ready", "dt_done",
                 "dt_low", "dt_exp", "dt_ln", "dt_ready", "cum_done", "cum_sub", "cum_exp", "aneg_ready", "x_mean",
                 "x_rstd", "half_ready", "w_high", "w_low", "z_low", "taps_ready", "fm_done", "fm_out", "conv_done",
                 "fm_tanh", "fm_ready", "z_done", "z_tanh", "z_ready", "turned", "seg_done", "tok_ready",
                 "decay_ready", "gm_ready", "x_parts", "scan_done", "state_ready", "y_read", "y_gated", "y_squared",
                 "y_mean", "y_rstd", "y_ready", "group_ready", "half_steps", "loop_steps", "last_steps", "start_steps",
                 "zeroed", "passed", "w_order", "zero_stored")
        S = {n: sem(n) for n in NAMES}
        x_loaded = [sem(f"x_loaded{i}") for i in range(2)]
        raw_loaded = [sem(f"raw_loaded{i}") for i in range(3)]
        y_stored = [sem(f"y_stored{i}") for i in range(2)]
        block = ctx.enter_context(nc.Block())

        @block.sync
        def _(sp):
            sp.dma_start(dbias[:], dt_bias.broadcast_to([P, HEADS])).then_inc(S["vec_loaded"], 16)
            sp.dma_start(aneg[:], a_log.broadcast_to([P, HEADS])).then_inc(S["vec_loaded"], 16)
            sp.dma_start(pk[:, 5 * HT, :], d_skip.broadcast_to([P, HEADS])).then_inc(S["vec_loaded"], 16)
            sp.dma_start(nw[:], norm_w.broadcast_to([P, DI])).then_inc(S["vec_loaded"], 16)
            sp.dma_start(wdt[:], in_w[0, :, DI + CONV_DIM:].rearrange("(k p) n -> p k n", p=P)
                         ).then_inc(S["vec_loaded"], 16)

            def load_x(h):
                for t in range(HT):
                    if t >= 2:
                        sp.wait_ge(S["x_turned"], h * HT + t - 1)
                    elif h:
                        sp.wait_ge(S["y_ready"], h * G * HT)
                    sp.dma_start(xt[t % 2], x[0, h * HTOK + t * P:h * HTOK + (t + 1) * P, :]
                                 ).then_inc(x_loaded[t % 2], 16)

            def load_piece(it, g, m):
                if m >= 3:
                    sp.wait_ge(S["w_low"], it * 4 + (m - 2))
                elif m >= 1:
                    sp.wait_ge(S["z_low"], it * 2)
                else:
                    sp.wait_ge(S["w_low"], it * 4)
                sp.sem_inc(S["passed"], 1)
                if m < 2:
                    src = in_w[0, :, bass.ds(DI + g * GW + m * P, P)].rearrange("(k p) n -> p k n", p=P)
                elif m < 4:
                    src = in_w[0, :, bass.ds(2 * DI + (m - 2) * G * N + g * N, P)].rearrange("(k p) n -> p k n", p=P)
                else:
                    src = in_w[0, (m - 4) * 4 * P:(m - 3) * 4 * P, bass.ds(g * GW, GW)].rearrange("(k p) n -> p k n", p=P)
                dst = wraw[:, m % 3, :].rearrange("p (k n) -> p k n", k=src.shape[1])
                sp.dma_start(dst, src).then_inc(raw_loaded[m % 3], 16)

            def store_y(h, it, g, c):
                sp.wait_ge(S["y_ready"], it * HT + (c + 1))
                sp.dma_start(ydram[h * HTOK + c * P:h * HTOK + (c + 1) * P, bass.ds(g * GW, GW)], yo[c % 2][:]
                             ).then_inc(y_stored[c % 2], 16)

            def store_zeros(it):
                for i in range(EXPERTS // (HALVES * G)):
                    e = it * (EXPERTS // (HALVES * G)) + i
                    sp.dma_start(xs[bass.ds(e * REGION, P), :], zero[:]).then_inc(S["zero_stored"], 16)

            sp.wait_ge(S["zeroed"], 5)
            for h in range(HALVES):
                for m in range(3):
                    load_piece(h * G, 0, m)
                load_x(h)
                for m in range(3, PIECES):
                    load_piece(h * G, 0, m)
                with sp.Fori(0, G - 1) as g:
                    it = g + h * G
                    for m in range(3):
                        load_piece(it + 1, g + 1, m)
                    store_y(h, it, g, 0)
                    for m in range(3, PIECES):
                        store_y(h, it, g, m - 2)
                        load_piece(it + 1, g + 1, m)
                    store_zeros(it)
                    for c in range(PIECES - 2, HT):
                        store_y(h, it, g, c)
                for c in range(HT):
                    store_y(h, h * G + G - 1, G - 1, c)
                store_zeros(h * G + G - 1)
            sp.wait_ge(S["zero_stored"], 16 * EXPERTS)
            for q in y_stored:
                sp.wait_ge(q, 16 * (HALVES * G * HT // 2 + 1))

        @block.gpsimd
        def _(pool):
            nc.gpsimd.memset(states[:], 0.0).then_inc(S["zeroed"], 1)
            nc.gpsimd.memset(hist[:], 0.0).then_inc(S["zeroed"], 1)
            nc.gpsimd.memset(minus_half[:], -0.5).then_inc(S["zeroed"], 1)
            nc.gpsimd.memset(eps[:], EPS).then_inc(S["zeroed"], 1)
            nc.gpsimd.memset(zero[:], 0.0).then_inc(S["zeroed"], 1)
            pool.wait_ge(S["zeroed"], 5)

            def half(h):
                for t in range(HT):
                    pool.wait_ge(S["x_sq"], h * HT + (t + 1))
                    s = tss[:, t % 2]
                    nc.gpsimd.tensor_tensor(s[:, 1:2], s[:, 0:1], eps[:], ALU.add).then_inc(S["x_mean"], 1)
                    pool.wait_ge(S["x_mean"], h * HT + (t + 1))
                    nc.gpsimd.tensor_tensor(s[:, 2:3], s[:, 1:2], minus_half[:], ALU.pow).then_inc(S["x_rstd"], 1)

            def split_piece(it, m):
                pool.wait_ge(S["w_high"], it * PIECES + (m + 1))
                nc.gpsimd.tensor_tensor(flat(wfm[1][:, m]), wraw[:, m % 3, :], flat(wfm[0][:, m]).bitcast(F32),
                                        ALU.subtract).then_inc(S["w_low"], 1)

            def group(it, following):
                n8 = pool.snap(it * HT)
                pool.wait_ge(S["group_ready"], it + 1)
                for c in range(HT):
                    pool.wait_ge(S["tok_ready"], n8 + (c + 1))
                    if c >= 2:
                        pool.wait_ge(S["y_gated"], n8 + (c - 1))
                    xv = tok[c % 2][:, 0:GW].rearrange("p (h d) -> p h d", h=HG)
                    by = lambda col: col.unsqueeze(2).broadcast_to([P, HG, PD])
                    nc.gpsimd.tensor_tensor(xdt[c % 2][:], xv, by(dtcol(DT, c)), ALU.mult)
                    nc.gpsimd.tensor_tensor(xde[c % 2][:], xv, by(dtcol(DTE, c)), ALU.mult)
                    nc.gpsimd.tensor_tensor(xd[c % 2][:], xv, by(pkg[:, 5 * HT, :]), ALU.mult
                                            ).then_inc(S["x_parts"], 1)
                    if c >= 1:
                        rstd(c - 1, n8)
                    if following and 1 <= c <= 4:
                        split_piece(pool.snap(it + 1), c - 1)
                rstd(HT - 1, n8)

            def rstd(c, n8):
                b = c % 2
                pool.wait_ge(S["y_squared"], n8 + (c + 1))
                nc.gpsimd.tensor_tensor(ssq[:, 2 + b:3 + b], ssq[:, b:b + 1], eps[:], ALU.add).then_inc(S["y_mean"], 1)
                pool.wait_ge(S["y_mean"], n8 + (c + 1))
                nc.gpsimd.tensor_tensor(ssq[:, 4 + b:5 + b], ssq[:, 2 + b:3 + b], minus_half[:], ALU.pow
                                        ).then_inc(S["y_rstd"], 1)

            with pool.Fori(0, HALVES) as h:
                half(h)
                for m in range(4):
                    split_piece(pool.snap(h * G), m)
                with pool.Fori(0, G - 1) as g:
                    group(pool.snap(h * G + g), True)
                group(pool.snap(h * G + (G - 1)), False)

        @block.scalar
        def _(act):
            act.wait_ge(S["vec_loaded"], 5 * 16)
            nc.scalar.activation(aneg[:], aneg[:], ACT.Exp).then_inc(S["aneg_ready"], 1)

            def half(h):
                def square(t):
                    act.wait_ge(x_loaded[t % 2], h * (HT // 2 * 16) + 16 * (t // 2 + 1))
                    if t >= 2:
                        act.wait_ge(S["x_scaled"], h * HT + (t - 1))
                    nc.scalar.activation(xsq[t % 2], xt[t % 2], ACT.Square, scale=D ** -0.5, accum_out=tss[:, t % 2, 0:1]
                                         ).then_inc(S["x_sq"], 1)

                square(0)
                for t in range(HT):
                    if t + 1 < HT:
                        square(t + 1)
                    act.wait_ge(S["x_turned"], h * HT + (t + 1))
                    if t >= 2:
                        act.wait_ge(S["h_ready"], h * HT + (t - 1))
                    for k in range(KD):
                        last = nc.scalar.activation(v[t % 2][:, k, :],
                                                    turned_x[t % 2][k // 4][:, (k % 4) * P:(k % 4 + 1) * P],
                                                    ACT.Identity, bias=K["mod"][:, k:k + 1], scale=K["a1"][:, k:k + 1])
                    last.then_inc(S["v_ready"], 1)
                act.wait_ge(S["dt_low"], h + 1)
                nc.scalar.activation(T[2], T[1], ACT.Exp).then_inc(S["dt_exp"], 1)
                act.wait_ge(S["dt_exp"], h + 1)
                nc.scalar.activation(T[4], T[2], ACT.Ln, bias=1.0).then_inc(S["dt_ln"], 1)
                act.wait_ge(S["cum_sub"], h + 1)
                nc.scalar.activation(row(EAC), row(NAC), ACT.Exp, scale=-1.0)
                nc.scalar.activation(row(CDEC), psS[1][:, W8:2 * W8], ACT.Exp)
                nc.scalar.activation(T[5], T[6], ACT.Exp).then_inc(S["cum_exp"], 1)

            def piece_high(it, m):
                act.wait_ge(raw_loaded[m % 3], it * 32 + 16 * (m // 3 + 1))
                hi = flat(wfm[0][:, m]) if m < 4 else flat(wz[0][:, (m - 4) * 4:(m - 3) * 4])
                nc.scalar.copy(hi, wraw[:, m % 3, :]).then_inc(S["w_high"], 1)

            def block_out(n8, i):
                s, m, b = i // 4, i % 4, i % 2
                act.wait_ge(S["fm_done"], n8 + (i + 1))
                if i >= 2:
                    act.wait_ge(S["fm_ready"], n8 + (i - 1))
                if s:
                    act.wait_ge(S["fm_out"], n8 + (m + 1))
                nc.scalar.copy(raw[:, b, 0:3], histg[:, s, m, :])
                nc.scalar.activation(cv[:, b, :], psF[b][:], ACT.Identity, bias=vecg[:, TAPS, m:m + 1],
                                     scale=vecg[:, TAPS - 1, m:m + 1])
                nc.scalar.copy(raw[:, b, 3:3 + SUP], psF[b][:])
                nc.scalar.copy(histg[:, 1 - s, m, :], psF[b][:, SUP - 3:SUP]).then_inc(S["fm_out"], 1)

            def block_tanh(n8, i):
                act.wait_ge(S["conv_done"], n8 + (i + 1))
                nc.scalar.activation(fm[i // 4][:, i % 4, :], cv[:, i % 2, :], ACT.Tanh).then_inc(S["fm_tanh"], 1)

            def start(it):
                for m in range(PIECES):
                    piece_high(it, m)
                act.wait_ge(S["taps_ready"], it + 1)
                n8 = act.snap(it * HT)
                for m in range(4):
                    block_out(n8, m)
                    if m >= 1:
                        block_tanh(n8, m - 1)
                block_tanh(n8, 3)

            def group(it, following):
                n8 = act.snap(it * HT)
                next8 = act.snap(it * HT + HT)
                it1 = act.snap(it + 1)

                def z_out(c):
                    act.wait_ge(S["z_done"], n8 + (c + 1))
                    nc.scalar.activation(zs[:, c % CS, :], psZ[:, 0:GW], ACT.Tanh, scale=0.5).then_inc(S["z_tanh"], 1)

                def chunk_in(c):
                    act.wait_ge(S["turned"], n8 + (c + 1))
                    if c >= 2:
                        act.wait_ge(S["scan_done"], n8 + (c - 1))
                    nc.scalar.copy(tok[c % 2][:], psT[c % 2][:, 0:3 * P]).then_inc(S["tok_ready"], 1)
                    act.wait_ge(S["seg_done"], n8 + (c + 1))
                    for h in range(HG):
                        last = nc.scalar.activation(gm[c % 2][:, h, :], psS[c % 2][:, h * P:(h + 1) * P], ACT.Exp,
                                                    bias=pkg[:, NAC * HT + c, h:h + 1])
                    last.then_inc(S["decay_ready"], 1)

                def square(c):
                    act.wait_ge(S["y_gated"], n8 + (c + 1))
                    nc.scalar.activation(ysq[:], flat(yt[c % 2][:]), ACT.Square, scale=GW ** -0.5,
                                         accum_out=ssq[:, c % 2:c % 2 + 1]).then_inc(S["y_squared"], 1)

                for c in range(HT):
                    base, i = (n8, 4 + c) if c < CS else (next8, c - CS)
                    convolves = c < CS or following
                    if c == CS and following:
                        act.wait_ge(S["taps_ready"], it1 + 1)
                    chunk_in(c)
                    if c >= 1:
                        square(c - 1)
                    if convolves:
                        if CS <= c < CS + 2:
                            act.wait_ge(S["fm_ready"], next8 + (i - 1))
                        block_out(base, i)
                    z_out(c)
                    if following and 1 <= c <= 4:
                        piece_high(it1, c - 1)
                    if following and c == HT - 1:
                        piece_high(it1, 4)
                        piece_high(it1, 5)
                    if convolves:
                        block_tanh(base, i)
                square(HT - 1)

            with act.Fori(0, HALVES) as h:
                half(h)
                start(act.snap(h * G))
                with act.Fori(0, G - 1) as g:
                    group(act.snap(h * G + g), True)
                group(act.snap(h * G + (G - 1)), False)

        @block.tensor
        def _(pe):
            def split_products(out, lhs, rhs):
                K_ = len(lhs[0])
                for n, (i, j) in enumerate(((1, 0), (0, 1), (0, 0))):
                    for k in range(K_):
                        mm = nc.tensor.matmul(out, lhs[i][k], rhs[j][k], start=(n == 0 and k == 0),
                                              stop=(n == 2 and k == K_ - 1))
                return mm

            def half(h):
                def turn(t):
                    pe.wait_ge(S["x_scaled"], h * HT + (t + 1))
                    if t >= 2:
                        pe.wait_ge(S["v_ready"], h * HT + (t - 1))
                    for k in range(KD):
                        mm = nc.tensor.transpose(turned_x[t % 2][k // 4][:, (k % 4) * P:(k % 4 + 1) * P],
                                                 xt[t % 2][:, k * P:(k + 1) * P], ident[:])
                    mm.then_inc(S["x_turned"], 1)

                turn(0)
                for t in range(HT):
                    if t + 1 < HT:
                        turn(t + 1)
                    pe.wait_ge(S["h_ready"], h * HT + (t + 1))
                    if t == 0:
                        pe.sem_inc(S["passed"], 1)
                    mm = split_products(psY[:, t * HEADS:(t + 1) * HEADS],
                                        [[hT[i][:, k, t * P:(t + 1) * P] for k in range(KD)] for i in range(2)],
                                        [[wdts[i][:, k, :] for k in range(KD)] for i in range(2)])
                mm.then_inc(S["dt_done"], 1)
                pe.wait_ge(S["dt_ready"], h + 1)
                nc.tensor.matmul(psS[1][:, 0:W8], upper[:], T[7], start=True, stop=True)
                nc.tensor.matmul(psS[1][:, W8:2 * W8], ones[:], T[7], start=True, stop=True).then_inc(S["cum_done"], 1)
                pe.wait_ge(S["half_ready"], h + 1)
                pe.sem_inc(S["passed"], 1)

            def project(it, n8, s, m):
                i = s * 4 + m
                if not s:
                    pe.wait_ge(S["w_low"], it * 4 + (m + 1))
                if i >= 2:
                    pe.wait_ge(S["fm_out"], n8 + (i - 1))
                split_products(psF[i % 2][:], [[wfm[j][:, m, k, :] for k in range(KD)] for j in range(2)],
                               [[hT[j][:, k, s * SUP:(s + 1) * SUP] for k in range(KD)] for j in range(2)]
                               ).then_inc(S["fm_done"], 1)

            def group(it, following):
                n8 = pe.snap(it * HT)
                next8 = pe.snap(it * HT + HT)
                it1 = pe.snap(it + 1)

                def project_z(c):
                    if c == 0:
                        pe.wait_ge(S["z_low"], it * 2 + 2)
                    pe.wait_ge(S["z_ready"], n8 + c)
                    split_products(psZ[:, 0:GW], [[hT[j][:, k, c * P:(c + 1) * P] for k in range(KD)] for j in range(2)],
                                   [[wz[j][:, k, :] for k in range(KD)] for j in range(2)]).then_inc(S["z_done"], 1)

                def chunk_in(c):
                    s, o = c // CS, (c % CS) * P
                    if c % CS == 0:
                        pe.wait_ge(S["fm_ready"], n8 + (s + 1) * 4)
                    if c >= 2:
                        pe.wait_ge(S["y_read"], n8 + (c - 1))
                    elif c == 0:
                        pe.wait_ge(S["y_read"], n8)
                    b = c % 2
                    for m in range(3):
                        nc.tensor.transpose(psT[b][:, m * P:(m + 1) * P], fm[s][:, m, o:o + P], ident[:])
                    nc.tensor.matmul(psT[b][:, 3 * P:], fm[s][:, 2, o:o + P], fm[s][:, 3, o:o + P],
                                     start=True, stop=True).then_inc(S["turned"], 1)
                    if c == 0:
                        pe.wait_ge(S["group_ready"], it + 1)
                    for h in range(HG):
                        for j in (1, 0):
                            nc.tensor.matmul(psS[b][:, h * P:(h + 1) * P], dag[j][:, c, h:h + 1].broadcast_to([P, P]),
                                             upr[:], start=(h == 0 and j == 1), stop=False, skip_group_check=True)
                    nc.tensor.matmul(psS[b][:].rearrange("p (h i) -> p h i", h=HG), identb[:],
                                     maskb[:].unsqueeze(1).broadcast_to([P, HG, P]), start=False, stop=True,
                                     skip_group_check=True).then_inc(S["seg_done"], 1)

                def chunk_out(c):
                    s, o, b = c // CS, (c % CS) * P, c % 2
                    pe.wait_ge(S["gm_ready"], n8 + (c + 1))
                    pe.wait_ge(S["x_parts"], n8 + (c + 1))
                    pe.wait_ge(S["state_ready"], n8 + (c + 1))
                    if c >= 1:
                        pe.wait_ge(S["y_read"], n8 + c)
                    nc.tensor.matmul(psY[:, GW:2 * GW], fm[s][:, 3, o:o + P], flat(state[:]), start=True, stop=True)
                    nc.tensor.matmul(psS[b][:, 0:GW], tok[b][:, 2 * P:3 * P], flat(xde[b][:]), start=True, stop=True)
                    for h in range(HG):
                        mm = nc.tensor.matmul(psY[:, h * PD:(h + 1) * PD], gm[b][:, h, :], xdt[b][:, h, :],
                                              start=True, stop=True)
                    mm.then_inc(S["scan_done"], 1)

                for c in range(HT):
                    if c == 0:
                        project(it, n8, 1, 0)
                    chunk_in(c)
                    if 1 <= c < CS:
                        project(it, n8, 1, c)
                    elif c >= CS and following:
                        if c < CS + 2:
                            pe.wait_ge(S["fm_out"], next8 + (c - CS - 1))
                        project(it1, next8, 0, c - CS)
                    project_z(c)
                    chunk_out(c)

            pe.wait_ge(S["vec_loaded"], 5 * 16)
            with pe.Fori(0, HALVES) as h:
                half(h)
                it = pe.snap(h * G)
                for m in range(4):
                    project(it, pe.snap(it * HT), 0, m)
                with pe.Fori(0, G - 1) as g:
                    group(pe.snap(h * G + g), True)
                group(pe.snap(h * G + (G - 1)), False)

        @block.vector
        def _(dve):
            first = Steps(dve, S["w_order"])
            for q in y_stored:
                dve.sem_inc(q, 16)
            dve.wait_ge(S["vec_loaded"], 5 * 16)
            first.add(nc.vector.tensor_copy(wdts[0][:], wdt[:]))
            first.add(nc.vector.tensor_copy(upr[:], upper[:]))
            first.settle()
            first.add(nc.vector.tensor_tensor(wdts[1][:], wdt[:], wdts[0][:].bitcast(F32), ALU.subtract))
            first.settle()
            dve.wait_ge(S["aneg_ready"], 1)
            first.add(nc.vector.tensor_scalar(aneg[:], aneg[:], -1.0, None, ALU.mult))
            first.settle()
            dve.wait_ge(S["zeroed"], 5)
            nc.vector.memset(ssq[:], 0.0).then_inc(S["wdt_ready"], 1)

            def half(h, own):
                def scale(t):
                    dve.wait_ge(S["x_rstd"], h * HT + (t + 1))
                    nc.vector.tensor_scalar(xt[t % 2], xt[t % 2], tss[:, t % 2, 2:3], None, ALU.mult
                                            ).then_inc(S["x_scaled"], 1)

                scale(0)
                for t in range(HT):
                    if t + 1 < HT:
                        scale(t + 1)
                    dve.wait_ge(S["v_ready"], h * HT + (t + 1))
                    o = slice(t * P, (t + 1) * P)
                    nc.vector.tensor_copy(hT[0][:, :, o], v[t % 2]).then_inc(S["v_high"], 1)
                    dve.wait_ge(S["v_high"], h * HT + (t + 1))
                    nc.vector.tensor_tensor(hT[1][:, :, o], v[t % 2], hT[0][:, :, o].bitcast(F32), ALU.subtract
                                            ).then_inc(S["h_ready"], 1)
                per_tile = lambda a: a.unsqueeze(1).broadcast_to([P, HT, HEADS])
                shaped = lambda a: a.rearrange("p (c h) -> p c h", c=HT)
                dve.wait_ge(S["dt_done"], h + 1)
                own.add(nc.vector.tensor_tensor(shaped(T[0]), shaped(psY[:, 0:W8]), per_tile(dbias[:]), ALU.add))
                own.settle()
                nc.vector.scalar_tensor_tensor(T[1], T[0], -1.0, T[0], ALU.mult, ALU.min).then_inc(S["dt_low"], 1)
                own.add(nc.vector.tensor_scalar(T[3], T[0], 0.0, None, ALU.max))
                dve.wait_ge(S["dt_ln"], h + 1)
                own.add(nc.vector.tensor_scalar(T[5], T[2], 1.0, None, ALU.add))
                own.settle()
                own.add(nc.vector.scalar_tensor_tensor(T[6], T[5], -1.0, T[2], ALU.add, ALU.subtract))
                own.add(nc.vector.reciprocal(T[7], T[5]))
                own.add(nc.vector.tensor_tensor(T[4], T[4], T[3], ALU.add))
                own.settle()
                own.add(nc.vector.tensor_tensor(T[6], T[6], T[7], ALU.mult))
                own.settle()
                own.add(nc.vector.tensor_tensor(row(DT), T[4], T[6], ALU.subtract))
                own.settle()
                nc.vector.tensor_tensor(shaped(T[7]), shaped(row(DT)), per_tile(aneg[:]), ALU.mult
                                        ).then_inc(S["dt_ready"], 1)
                dve.wait_ge(S["dt_ready"], h + 1)
                own.add(nc.vector.tensor_copy(flat(da[0][:]), T[7]))
                own.settle()
                own.add(nc.vector.tensor_tensor(flat(da[1][:]), T[7], flat(da[0][:]).bitcast(F32), ALU.subtract))
                dve.wait_ge(S["cum_done"], h + 1)
                own.add(nc.vector.tensor_scalar(row(NAC), psS[1][:, 0:W8], -1.0, None, ALU.mult))
                own.settle()
                nc.vector.tensor_tensor(T[6], psS[1][:, W8:2 * W8], row(NAC), ALU.add).then_inc(S["cum_sub"], 1)
                dve.wait_ge(S["cum_exp"], h + 1)
                nc.vector.tensor_tensor(row(DTE), row(DT), T[5], ALU.mult).then_inc(S["half_ready"], 1)
                dve.wait_ge(S["half_ready"], h + 1)
                dve.sem_inc(S["passed"], 1)

            def load_taps(g, own):
                own.add(nc.vector.tensor_copy(vecg[:, :, 0:2], K["conv"][:, :, bass.ds(g * 2, 2)]))
                own.add(nc.vector.tensor_copy(vecg[:, :, 2:3], K["conv"][:, :, bass.ds(g + 2 * G, 1)]))
                own.add(nc.vector.tensor_copy(vecg[:, :, 3:4], K["conv"][:, :, bass.ds(g + 3 * G, 1)]))
                own.settle()
                nc.vector.tensor_copy(flat(histg[:, 0]).unsqueeze(2), hist[:, :, bass.ds(g, 1)]).then_inc(S["taps_ready"], 1)

            def load_group(g, own):
                g4 = dve.snap(g * HG)
                own.add(nc.vector.tensor_copy(pkg[:], pk[:, :, bass.ds(g4, HG)]))
                for i in range(2):
                    own.add(nc.vector.tensor_copy(dag[i][:], da[i][:, :, bass.ds(g4, HG)]))
                own.settle()
                nc.vector.tensor_copy(flat(state[:]), states[:, bass.ds(g, 1), :].rearrange("p o n -> p (o n)")
                                      ).then_inc(S["state_ready"], 1)
                dve.sem_inc(S["group_ready"], 1)

            def conv(n8, i, own):
                m, b = i % 4, i % 2
                dve.wait_ge(S["fm_out"], n8 + (i + 1))
                for tap in range(TAPS - 1):
                    ins = nc.vector.scalar_tensor_tensor(cv[:, b, :], raw[:, b, tap:tap + SUP], vecg[:, tap, m:m + 1],
                                                         cv[:, b, :], ALU.mult, ALU.add)
                    if tap < TAPS - 2:
                        own.add(ins)
                        own.settle()
                ins.then_inc(S["conv_done"], 1)

            def block_silu(n8, i):
                dve.wait_ge(S["fm_tanh"], n8 + (i + 1))
                f = fm[i // 4][:, i % 4, :]
                nc.vector.scalar_tensor_tensor(f, f, 1.0, cv[:, i % 2, :], ALU.add, ALU.mult).then_inc(S["fm_ready"], 1)

            def z_low(it, m):
                dve.wait_ge(S["w_high"], it * PIECES + (m + 1))
                k4 = slice((m - 4) * 4, (m - 3) * 4)
                nc.vector.tensor_tensor(flat(wz[1][:, k4]), wraw[:, m % 3, :], flat(wz[0][:, k4]).bitcast(F32),
                                        ALU.subtract).then_inc(S["z_low"], 1)

            def start(it, own):
                load_taps(0, own)
                load_group(0, own)
                z_low(it, 4)
                z_low(it, 5)
                n8 = dve.snap(it * HT)
                for m in range(4):
                    conv(n8, m, own)
                    if m >= 1:
                        block_silu(n8, m - 1)
                block_silu(n8, 3)

            def group(it, g, own, following):
                n8 = dve.snap(it * HT)
                next8 = dve.snap(it * HT + HT)
                it1 = dve.snap(it + 1)
                g1 = dve.snap(g + 1) if following else None
                dve.wait_ge(S["state_ready"], n8 + 1)

                def decays(c):
                    dve.wait_ge(S["decay_ready"], n8 + (c + 1))
                    cb = psT[c % 2][:, 3 * P:].unsqueeze(1).broadcast_to([P, HG, P])
                    nc.vector.tensor_tensor(gm[c % 2][:], gm[c % 2][:], cb, ALU.mult).then_inc(S["gm_ready"], 1)

                def gate(c):
                    b = c % 2
                    by = lambda col: col.unsqueeze(2).broadcast_to([P, HG, PD])
                    halves = lambda a: a.rearrange("p (h d) -> p h d", h=HG)
                    dve.wait_ge(S["scan_done"], n8 + (c + 1))
                    own.add(nc.vector.tensor_tensor(state[:], state[:], by(dtcol(CDEC, c)), ALU.mult))
                    own.add(nc.vector.tensor_tensor(yt[b][:], halves(psY[:, GW:2 * GW]), by(dtcol(EAC, c)), ALU.mult))
                    own.settle()
                    ins = nc.vector.tensor_tensor(state[:], state[:], halves(psS[b][:, 0:GW]), ALU.add)
                    if c < HT - 1:
                        ins.then_inc(S["state_ready"], 1)
                    else:
                        own.add(ins)
                    nc.vector.tensor_tensor(yt[b][:], yt[b][:], halves(psY[:, 0:GW]), ALU.add).then_inc(S["y_read"], 1)
                    dve.wait_ge(S["y_read"], n8 + (c + 1))
                    own.add(nc.vector.tensor_tensor(yt[b][:], yt[b][:], xd[b][:], ALU.add))
                    own.settle()
                    dve.wait_ge(S["z_ready"], n8 + (c + 1))
                    nc.vector.scalar_tensor_tensor(flat(yt[b][:]), flat(yt[b][:]), 0.5, zs[:, c % CS, :], ALU.mult, ALU.mult
                                                   ).then_inc(S["y_gated"], 1)

                def z_silu(c):
                    dve.wait_ge(S["z_tanh"], n8 + (c + 1))
                    z = zs[:, c % CS, :]
                    nc.vector.scalar_tensor_tensor(z, z, 1.0, psZ[:, 0:GW], ALU.add, ALU.mult).then_inc(S["z_ready"], 1)

                def norm(c):
                    b = c % 2
                    dve.wait_ge(S["y_rstd"], n8 + (c + 1))
                    dve.wait_ge(y_stored[b], stored + 16 * (c // 2 + 1))
                    nc.vector.scalar_tensor_tensor(yo[b][:], flat(yt[b][:]), ssq[:, 4 + b:5 + b], nw[:, bass.ds(g * GW, GW)],
                                                   ALU.mult, ALU.mult).then_inc(S["y_ready"], 1)

                stored = dve.snap(it * (HT // 2 * 16))
                for c in range(HT):
                    base, i = (n8, 4 + c) if c < CS else (next8, c - CS)
                    convolves = c < CS or following
                    decays(c)
                    if c >= 1:
                        norm(c - 1)
                    if convolves:
                        conv(base, i, own)
                    z_silu(c)
                    if c == CS - 1:
                        dve.wait_ge(S["conv_done"], n8 + HT)
                        own.add(nc.vector.tensor_copy(hist[:, :, bass.ds(g, 1)], flat(histg[:, 0]).unsqueeze(2)))
                        own.settle()
                        if following:
                            load_taps(g1, own)
                    if convolves:
                        block_silu(base, i)
                    if following and c == HT - 1:
                        z_low(it1, 4)
                        z_low(it1, 5)
                    gate(c)
                own.settle()
                own.add(nc.vector.tensor_copy(states[:, bass.ds(g, 1), :].rearrange("p o n -> p (o n)"), flat(state[:])))
                own.settle()
                if following:
                    dve.wait_ge(S["y_gated"], n8 + HT)
                    load_group(g1, own)
                norm(HT - 1)

            HALF_STEPS, START_STEPS, LOOP_STEPS, LAST_STEPS = 11, 14, 49, 35
            with dve.Fori(0, HALVES) as h:
                own = Steps(dve, S["half_steps"], dve.snap(h * HALF_STEPS))
                half(h, own)
                assert own.n == HALF_STEPS, own.n
                own = Steps(dve, S["start_steps"], dve.snap(h * START_STEPS))
                start(dve.snap(h * G), own)
                assert own.n == START_STEPS, own.n
                with dve.Fori(0, G - 1) as g:
                    own = Steps(dve, S["loop_steps"], dve.snap((h * (G - 1) + g) * LOOP_STEPS))
                    group(dve.snap(h * G + g), g, own, True)
                    assert own.n == LOOP_STEPS, own.n
                own = Steps(dve, S["last_steps"], dve.snap(h * LAST_STEPS))
                group(dve.snap(h * G + (G - 1)), G - 1, own, False)
                assert own.n == LAST_STEPS, own.n


def out_phase(nc, x, out_w, group_w, group_b, expert_w, expert_b, ydram, x1dram, xs, K):
    Q = 4
    NR = GROUPS + EXPERTS
    SLOTS = 4
    with ExitStack() as ctx:
        sb = lambda n, s, d=F32: ctx.enter_context(nc.sbuf_tensor(n, s, d))
        psum = lambda n: ctx.enter_context(nc.psum_tensor(n, [P, 512], F32))
        sem = semaphores(nc, ctx, "out_")
        ident, mod, a2 = K["ident"], K["mod"], K["a2"]
        wo = [sb(f"wo{i}", [P, KI, D], F32R) for i in range(2)]
        wraw = sb("wo_raw", [P, SLOTS, D])
        y4 = sb("y4", [P, Q, 512])
        yT = [sb(f"yT{i}", [P, Q, 512], F32R) for i in range(2)]
        rows = {n: sb("row_" + n, [P, D]) for n in ("gt1", "a2", "s2")}
        xr = sb("xr", [P, D])
        tmp = sb("tmp", [P, 2, 512])
        hf = sb("hf", [P, D])
        hfT = sb("hfT", [P, KD, P])
        wr = sb("wr", [P, KD, NR])
        rb = sb("rb", [P, NR])
        st = sb("st", [P, 4])
        minus_half, eps = sb("o_minus_half", [P, 1]), sb("o_eps", [P, 1])
        lg, el = sb("lg", [P, 8]), sb("el", [P, EXPERTS])
        gm8, em8 = sb("gm8", [P, 8]), sb("em8", [P, 8])
        gi8, ei8 = sb("gi8", [P, 8], U32), sb("ei8", [P, 8], U32)
        gif, eif, ngm = sb("gif", [P, 1]), sb("eif", [P, 2]), sb("ngm", [P, 1])
        ge, gsum, dif, ex = sb("ge", [P, 4]), sb("gsum", [P, 1]), sb("dif", [P, 1]), sb("ex", [P, 1])
        den, rec = sb("den", [P, 1]), sb("rec", [P, 1])
        ohg, pen = sb("ohg", [P, EXPERTS]), sb("pen", [P, EXPERTS])
        oh = [sb(f"oh{i}", [P, EXPERTS]) for i in range(2)]
        both = sb("both", [P, EXPERTS], BF16)
        pos, base, scr = sb("pos", [P, EXPERTS]), sb("base", [P, EXPERTS]), sb("scr", [P, 2, EXPERTS])
        df, dcur = sb("df", [P, 2]), sb("dcur", [P, 2], U32)
        ii = sb("ii", [P, 3, EXPERTS], I32)
        ff = sb("ff", [P, 3, EXPERTS])
        dest, gates = K["dest"], K["gates"]
        acc = [psum("acc0"), psum("acc1")]
        psT = [psum("oT0"), psum("oT1")]
        psH = [psum("oH0"), psum("oH1")]
        psR, psC = psum("psR"), psum("psC")
        NAMES = ("vec_loaded", "raw_done", "high", "low", "y_turned", "y_high", "y_low", "acc_done", "acc_read",
                 "half_added", "squared", "mean", "rstd", "hf_scaled", "hf_ready", "hf_turned", "hf_copied",
                 "logits", "gneg", "gexp", "edif", "eexp", "picked", "ranked", "placed", "scattered",
                 "x_loaded", "x1_stored", "vsteps", "psteps", "setup", "consts", "rows_done", "rows_copied", "passed",
                 "table_steps", "y_order")
        S = {n: sem(n) for n in NAMES}
        raw_loaded = [sem(f"raw_loaded{i}") for i in range(SLOTS)]
        y_loaded = [sem(f"y_loaded{i}") for i in range(Q)]
        block = ctx.enter_context(nc.Block())

        @block.sync
        def _(sp):
            with nc.allow_non_contiguous_dma(reason="the router's weights are narrow"):
                sp.dma_start(wr[:, :, 0:GROUPS], group_w[0].rearrange("(k p) n -> p k n", p=P)).then_inc(S["vec_loaded"], 16)
                sp.dma_start(wr[:, :, GROUPS:NR], expert_w[0].rearrange("(k p) n -> p k n", p=P)).then_inc(S["vec_loaded"], 16)
            sp.dma_start(rb[:, 0:GROUPS], group_b.broadcast_to([P, GROUPS])).then_inc(S["vec_loaded"], 16)
            sp.dma_start(rb[:, GROUPS:NR], expert_b.broadcast_to([P, EXPERTS])).then_inc(S["vec_loaded"], 16)

            def load_y(t):
                for q in range(Q):
                    if not isinstance(t, int) or t:
                        sp.wait_ge(S["y_turned"], t * Q + (q - Q + 1))
                    sp.dma_start(y4[:, q, :], ydram[bass.ds(t * P, P), q * 512:(q + 1) * 512]
                                 ).then_inc(y_loaded[q], 16)

            def load_x(t):
                sp.dma_start(xr[:], x[0, bass.ds(t * P, P), :]).then_inc(S["x_loaded"], 16)

            def store_x1(t):
                sp.wait_ge(S["half_added"], t * 2 + 2)
                sp.dma_start(x1dram[bass.ds(t * P, P), :], xr[:]).then_inc(S["x1_stored"], 16)
                sp.wait_ge(S["x1_stored"], t * 16 + 16)
                sp.wait_ge(S["hf_scaled"], t + 1)

            load_y(0)
            load_x(0)
            for k in range(KI):
                if k >= SLOTS:
                    sp.wait_ge(S["low"], k - SLOTS + 1)
                sp.dma_start(wraw[:, k % SLOTS, :], out_w[0, k * P:(k + 1) * P, :]).then_inc(raw_loaded[k % SLOTS], 16)
            with sp.Fori(1, TILES) as t:
                load_y(t)
                store_x1(t - 1)
                load_x(t)
            store_x1(TILES - 1)

        @block.gpsimd
        def _(pool):
            own = Steps(pool, S["setup"])
            own.add(nc.gpsimd.memset(minus_half[:], -0.5))
            own.add(nc.gpsimd.memset(eps[:], EPS))
            own.add(nc.gpsimd.memset(lg[:, GROUPS:8], -BIG))
            own.add(nc.gpsimd.iota(ii[:, 0, :], pattern=[[1, EXPERTS]], base=0, channel_multiplier=0))
            own.add(nc.gpsimd.iota(ii[:, 1, :], pattern=[[1, GROUPS], [0, EPG]], base=0, channel_multiplier=0))
            own.add(nc.gpsimd.iota(ii[:, 2, :], pattern=[[REGION, EXPERTS]], base=0, channel_multiplier=0))
            own.settle()
            nc.gpsimd.tensor_copy(ff[:], ii[:]).then_inc(S["consts"], 1)

            def add_half(t, n):
                if n == 0:
                    pool.wait_ge(S["x_loaded"], t * 16 + 16)
                pool.wait_ge(S["acc_read"], t * 2 + (n + 1))
                h = slice(n * 512, (n + 1) * 512)
                nc.gpsimd.tensor_tensor(xr[:, h], xr[:, h], tmp[:, n, :], ALU.add).then_inc(S["half_added"], 1)

            def norm(t):
                pool.wait_ge(S["squared"], t + 1)
                nc.gpsimd.tensor_tensor(st[:, 1:2], st[:, 0:1], eps[:], ALU.add).then_inc(S["mean"], 1)
                pool.wait_ge(S["mean"], t + 1)
                nc.gpsimd.tensor_tensor(st[:, 2:3], st[:, 1:2], minus_half[:], ALU.pow).then_inc(S["rstd"], 1)
                pool.wait_ge(S["hf_scaled"], t + 1)
                nc.gpsimd.tensor_tensor(hf[:], hf[:], rows["s2"][:], ALU.add).then_inc(S["hf_ready"], 1)

            def scatter(t):
                pool.wait_ge(S["placed"], t + 1)
                pool.sem_inc(S["passed"], 1)
                for j in range(2):
                    nc.gpsimd.indirect_dma_start(xs, bass.IndirectOffsetOnAxis(ap=dcur[:, j:j + 1], axis=0), hf[:], None
                                                 ).then_inc(S["scattered"], 16)

            def tile(t, n):
                if n >= 2:
                    scatter(t - 2)
                if n >= 1:
                    add_half(t - 1, 1)
                    norm(t - 1)
                add_half(t, 0)

            tile(0, 0)
            tile(1, 1)
            with pool.Fori(2, TILES) as t:
                tile(t, 2)
            scatter(TILES - 2)
            add_half(TILES - 1, 1)
            norm(TILES - 1)
            scatter(TILES - 1)
            pool.wait_ge(S["scattered"], TILES * 32)

        @block.scalar
        def _(act):
            for k in range(KI):
                act.wait_ge(raw_loaded[k % SLOTS], 16 * (k // SLOTS + 1))
                nc.scalar.copy(wo[0][:, k, :], wraw[:, k % SLOTS, :]).then_inc(S["high"], 1)

            def high(t, q):
                act.wait_ge(S["y_turned"], t * Q + (q + 1))
                nc.scalar.copy(yT[0][:, q, :], psT[q % 2][:]).then_inc(S["y_high"], 1)

            def square(t):
                act.wait_ge(S["half_added"], t * 2 + 2)
                nc.scalar.activation(hf[:], xr[:], ACT.Square, scale=D ** -0.5, accum_out=st[:, 0:1]
                                     ).then_inc(S["squared"], 1)

            def copy_hf(t):
                act.wait_ge(S["hf_turned"], t + 1)
                for i in range(2):
                    last = nc.scalar.copy(hfT[:, i * 4:(i + 1) * 4, :].rearrange("p a b -> p (a b)"), psH[i][:])
                last.then_inc(S["hf_copied"], 1)

            def soft(t):
                act.wait_ge(S["gneg"], t + 1)
                nc.scalar.activation(ge[:], lg[:, 0:GROUPS], ACT.Exp, bias=ngm[:], accum_out=gsum[:]).then_inc(S["gexp"], 1)
                act.wait_ge(S["edif"], t + 1)
                nc.scalar.activation(ex[:], dif[:], ACT.Exp).then_inc(S["eexp"], 1)

            def tile(t, n):
                for q in range(Q):
                    high(t, q)
                if n >= 1:
                    if n >= 2:
                        act.wait_ge(S["scattered"], t * 32 - 32)
                    square(t - 1)
                    copy_hf(t - 1)
                    soft(t - 1)

            tile(0, 0)
            tile(1, 1)
            with act.Fori(2, TILES) as t:
                tile(t, 2)
            act.wait_ge(S["scattered"], (TILES - 1) * 32)
            square(TILES - 1)
            copy_hf(TILES - 1)
            soft(TILES - 1)

        @block.tensor
        def _(pe):
            for r, (src, off) in enumerate(((mod, 2 * KD), (a2, 0), (mod, 3 * KD))):
                for i in range(2):
                    if r:
                        pe.wait_ge(S["rows_copied"], 2 * r - 1 + i)
                    for k in range(4):
                        o = off + 4 * i + k
                        mm = nc.tensor.matmul(acc[i][:, k * P:(k + 1) * P], src[:, o:o + 1].broadcast_to([P, P]),
                                              ident[:], start=True, stop=True)
                    mm.then_inc(S["rows_done"], 1)

            def turn(t, q):
                pe.wait_ge(y_loaded[q], t * 16 + 16)
                if q >= 2:
                    pe.wait_ge(S["y_low"], t * Q + (q - 1))
                for k in range(4):
                    mm = nc.tensor.transpose(psT[q % 2][:, k * P:(k + 1) * P], y4[:, q, k * P:(k + 1) * P], ident[:])
                mm.then_inc(S["y_turned"], 1)

            def product(t, n, q, first=False):
                if n == 0:
                    pe.wait_ge(S["y_low"], t * Q + (q + 1))
                for k in range(4 * q, 4 * q + 4):
                    if first:
                        pe.wait_ge(S["low"], k + 1)
                    o = (k % 4) * P
                    for i, j in ((1, 0), (0, 1), (0, 0)):
                        mm = nc.tensor.matmul(acc[n][:], yT[i][:, q, o:o + P], wo[j][:, k, n * 512:(n + 1) * 512],
                                              start=(k == 0 and i == 1), stop=(k == KI - 1 and i == 0 and j == 0))
                if q == Q - 1:
                    mm.then_inc(S["acc_done"], 1)

            def route_a(t):
                pe.wait_ge(S["hf_ready"], t + 1)
                for k in range(KD):
                    mm = nc.tensor.transpose(psH[k // 4][:, (k % 4) * P:(k % 4 + 1) * P], hf[:, k * P:(k + 1) * P], ident[:])
                mm.then_inc(S["hf_turned"], 1)

            def route_b(t):
                pe.wait_ge(S["hf_copied"], t + 1)
                for k in range(KD):
                    mm = nc.tensor.matmul(psR[:, 0:NR], hfT[:, k, :], wr[:, k, :], start=(k == 0), stop=(k == KD - 1))
                mm.then_inc(S["logits"], 1)

            def route_c(t):
                pe.wait_ge(S["picked"], t + 1)
                nc.tensor.matmul(psC[:, 0:EXPERTS], K["strictb"][:], both[:], start=True, stop=True)
                nc.tensor.matmul(psC[:, EXPERTS:2 * EXPERTS], K["onesb"][:], both[:], start=True, stop=True
                                 ).then_inc(S["ranked"], 1)

            def tile(t, n):
                for q in range(Q):
                    if n >= 1:
                        if q == 0:
                            pe.wait_ge(S["acc_read"], t * 2 - 2 if n == 2 else 1)
                        product(t - 1, 1, q)
                    turn(t, q)
                    if n >= 2 and q == 0:
                        route_b(t - 2)
                    if n >= 2 and q == 2:
                        route_c(t - 2)
                if n >= 1:
                    pe.wait_ge(S["acc_read"], t * 2 - 1)
                else:
                    pe.wait_ge(S["rows_copied"], 6)
                for q in range(Q):
                    product(t, 0, q, first=(n == 0))
                if n >= 1:
                    route_a(t - 1)

            pe.wait_ge(S["vec_loaded"], 4 * 16)
            tile(0, 0)
            tile(1, 1)
            with pe.Fori(2, TILES) as t:
                tile(t, 2)
            for q in range(Q):
                if q == 0:
                    pe.wait_ge(S["acc_read"], TILES * 2 - 2)
                product(TILES - 1, 1, q)
                if q == 0:
                    route_b(TILES - 2)
            route_c(TILES - 2)
            route_a(TILES - 1)
            route_b(TILES - 1)
            route_c(TILES - 1)

        @block.vector
        def _(dve):
            for r, name in enumerate(("gt1", "a2", "s2")):
                for i in range(2):
                    dve.wait_ge(S["rows_done"], 2 * r + i + 1)
                    nc.vector.tensor_copy(rows[name][:, i * 512:(i + 1) * 512], acc[i][:]).then_inc(S["rows_copied"], 1)
            for k in range(KI):
                dve.wait_ge(S["high"], k + 1)
                nc.vector.tensor_tensor(wo[1][:, k, :], wraw[:, k % SLOTS, :], wo[0][:, k, :].bitcast(F32), ALU.subtract
                                        ).then_inc(S["low"], 1)
            dve.wait_ge(S["consts"], 1)
            nc.vector.tensor_copy(base[:], ff[:, 2, :]).then_inc(S["y_order"], 1)
            dve.wait_ge(S["y_order"], 1)

            def low(t, q):
                dve.wait_ge(S["y_high"], t * Q + (q + 1))
                nc.vector.tensor_tensor(yT[1][:, q, :], psT[q % 2][:], yT[0][:, q, :].bitcast(F32), ALU.subtract
                                        ).then_inc(S["y_low"], 1)

            def gated(t, n):
                dve.wait_ge(S["acc_done"], t * 2 + (n + 1))
                nc.vector.tensor_tensor(tmp[:, n, :], acc[n][:], rows["gt1"][:, n * 512:(n + 1) * 512], ALU.mult
                                        ).then_inc(S["acc_read"], 1)

            def scaled(t):
                dve.wait_ge(S["rstd"], t + 1)
                nc.vector.scalar_tensor_tensor(hf[:], xr[:], st[:, 2:3], rows["a2"][:], ALU.mult, ALU.mult
                                               ).then_inc(S["hf_scaled"], 1)

            def pick(t, own):
                step = lambda ins: (own.add(ins), own.settle())
                dve.wait_ge(S["logits"], t + 1)
                own.add(nc.vector.tensor_tensor(lg[:, 0:GROUPS], psR[:, 0:GROUPS], rb[:, 0:GROUPS], ALU.add))
                own.add(nc.vector.tensor_tensor(el[:], psR[:, GROUPS:NR], rb[:, GROUPS:NR], ALU.add))
                own.settle()
                dve.sem_inc(S["passed"], 1)
                step(nc.vector.max(gm8[:], lg[:]))
                nc.vector.tensor_scalar(ngm[:], gm8[:, 0:1], -1.0, None, ALU.mult).then_inc(S["gneg"], 1)
                own.add(nc.vector.max_index(gi8[:], gm8[:], lg[:]))
                own.settle()
                step(nc.vector.tensor_copy(gif[:], gi8[:, 0:1]))
                step(nc.vector.tensor_scalar(ohg[:], ff[:, 1, :], gif[:], None, ALU.is_equal))
                own.add(nc.vector.tensor_scalar(pen[:], ohg[:], -1.0, BIG, ALU.add, ALU.mult))
                step(nc.vector.tensor_tensor(el[:], el[:], ohg[:], ALU.mult))
                step(nc.vector.tensor_tensor(el[:], el[:], pen[:], ALU.add))
                dve.sem_inc(S["passed"], 1)
                step(nc.vector.max(em8[:], el[:]))
                nc.vector.tensor_tensor(dif[:], em8[:, 1:2], em8[:, 0:1], ALU.subtract).then_inc(S["edif"], 1)
                own.add(nc.vector.max_index(ei8[:], em8[:], el[:]))
                own.settle()
                step(nc.vector.tensor_copy(eif[:], ei8[:, 0:2]))
                for j in range(2):
                    own.add(nc.vector.tensor_scalar(oh[j][:], ff[:, 0, :], eif[:, j:j + 1], None, ALU.is_equal))
                own.settle()
                nc.vector.tensor_tensor(both[:], oh[0][:], oh[1][:], ALU.add).then_inc(S["picked"], 1)
                dve.wait_ge(S["eexp"], t + 1)
                step(nc.vector.tensor_scalar(den[:], ex[:], 1.0, None, ALU.add))
                step(nc.vector.tensor_tensor(den[:], den[:], gsum[:], ALU.mult))
                step(nc.vector.reciprocal(rec[:], den[:]))
                dve.sem_inc(S["passed"], 1)
                gt = lambda j: gates[:, bass.ds(t * 2 + j, 1)]
                own.add(nc.vector.tensor_copy(gt(0), rec[:]))
                own.add(nc.vector.tensor_tensor(gt(1), rec[:], ex[:], ALU.mult))
                own.settle()

            def place(t, own):
                step = lambda ins: (own.add(ins), own.settle())
                dve.wait_ge(S["ranked"], t + 1)
                step(nc.vector.tensor_tensor(pos[:], base[:], psC[:, 0:EXPERTS], ALU.add))
                for j in range(2):
                    own.add(nc.vector.tensor_tensor_reduce(out=scr[:, j, :], in0=oh[j][:], in1=pos[:], scale=1.0,
                                                           scalar=0.0, op0=ALU.mult, op1=ALU.add,
                                                           accum_out=df[:, j:j + 1]))
                own.add(nc.vector.tensor_tensor(base[:], base[:], psC[:, EXPERTS:2 * EXPERTS], ALU.add))
                own.settle()
                if not isinstance(t, int) or t:
                    dve.wait_ge(S["scattered"], t * 32)
                nc.vector.tensor_copy(dcur[:], df[:]).then_inc(S["placed"], 1)
                own.add(nc.vector.tensor_copy(dest[:, bass.ds(t * 2, 2)], df[:]))
                own.settle()

            def tile(t, n, own):
                for q in range(Q):
                    low(t, q)
                    if q == 2 and n >= 2:
                        place(t - 2, own)
                if n >= 1:
                    gated(t - 1, 1)
                    scaled(t - 1)
                gated(t, 0)
                if n >= 1:
                    pick(t - 1, own)

            STEPS = 24
            own = Steps(dve, S["vsteps"])
            tile(0, 0, own)
            tile(1, 1, own)
            n1 = own.n
            with dve.Fori(2, TILES) as t:
                own = Steps(dve, S["vsteps"], dve.snap(t * STEPS + (n1 - 2 * STEPS)))
                tile(t, 2, own)
                assert own.n == STEPS, own.n
            own = Steps(dve, S["vsteps"], n1 + (TILES - 2) * STEPS)
            place(TILES - 2, own)
            gated(TILES - 1, 1)
            scaled(TILES - 1)
            pick(TILES - 1, own)
            place(TILES - 1, own)
            nc.vector.tensor_tensor(K["count"][:], base[:], ff[:, 2, :], ALU.subtract).then_inc(S["table_steps"], 1)


PEELED = 3
MAXB = 2 * SEQ // P + EXPERTS - 1


def plan_phase(nc, K):
    with ExitStack() as ctx:
        sb = lambda n, s, d=F32: ctx.enter_context(nc.sbuf_tensor(n, s, d))
        sem = semaphores(nc, ctx, "plan_")
        count, ones, tab = K["count"], K["ones"], K["tab"]
        ii, ip = sb("p_ii", [P, EXPERTS], I32), sb("p_ip", [P, 1], I32)
        ex, bl = sb("p_expert", [P, EXPERTS]), sb("p_block", [P, 1])
        t0, ti = sb("p_t0", [P, EXPERTS]), sb("p_ti", [P, EXPERTS], I32)
        nb, inc, exc, last = (sb("p_" + n, [P, EXPERTS]) for n in ("nb", "inc", "exc", "last"))
        own_, scr = sb("p_own", [P, EXPERTS]), sb("p_scr", [P, 5, EXPERTS])
        of = sb("p_of", [P, 5])
        cols = sb("p_cols", [P, 5])
        start, shift = sb("p_start", [P, EXPERTS]), sb("p_shift", [P, EXPERTS])
        pe_, pf = sb("p_pe", [P, 2 * TILES], U32), sb("p_pf", [P, 2 * TILES])
        df, match = sb("p_df", [P, 2 * TILES]), sb("p_match", [P, 2 * TILES, EXPERTS])
        ps = [ctx.enter_context(nc.psum_tensor(f"p_ps{i}", [P, 512], F32)) for i in range(2)]
        consts, steps, turned, cols_ready = sem("consts"), sem("steps"), sem("turned"), sem("cols_ready")
        block = ctx.enter_context(nc.Block())

        @block.gpsimd
        def _(pool):
            nc.gpsimd.iota(ii[:], pattern=[[1, EXPERTS]], base=0, channel_multiplier=0).then_inc(consts, 1)
            nc.gpsimd.iota(ip[:], pattern=[[0, 1]], base=0, channel_multiplier=1).then_inc(consts, 1)

        @block.tensor
        def _(pe):
            pe.wait_ge(cols_ready, 1)
            for j in range(5):
                mm = nc.tensor.matmul(ps[j // 4][0:1, (j % 4) * P:(j % 4 + 1) * P], cols[:, j:j + 1], K["ident"][:],
                                      start=True, stop=True)
            mm.then_inc(turned, 1)

        @block.vector
        def _(dve):
            own = Steps(dve, steps)
            step = lambda ins: (own.add(ins), own.settle())
            ts = nc.vector.tensor_scalar
            dve.wait_ge(consts, 2)
            own.add(nc.vector.tensor_copy(ex[:], ii[:]))
            own.add(nc.vector.tensor_copy(bl[:], ip[:]))
            own.add(ts(last[:], count[:], -float(P), 0.0, ALU.add, ALU.max))
            step(ts(t0[:], count[:], 1.0, float(P - 1), ALU.max, ALU.add))
            step(nc.vector.tensor_copy(ti[:], t0[:]))
            step(ts(ti[:], ti[:], 7, None, ALU.arith_shift_right))
            step(nc.vector.tensor_copy(nb[:], ti[:]))
            step(nc.vector.tensor_tensor_scan(inc[:], ones[:, 0:EXPERTS], nb[:], 0.0, ALU.mult, ALU.add))
            step(nc.vector.tensor_tensor(exc[:], inc[:], nb[:], ALU.subtract))
            own.add(ts(K["more"][:], inc[:, EXPERTS - 1:EXPERTS], -float(PEELED), None, ALU.add))
            own.add(ts(own_[:], exc[:], bl[:], None, ALU.is_le))
            step(ts(t0[:], inc[:], bl[:], None, ALU.is_le))
            step(nc.vector.tensor_tensor(own_[:], own_[:], t0[:], ALU.subtract))
            step(nc.vector.tensor_tensor_scan(start[:], ones[:, 0:EXPERTS], count[:], 0.0, ALU.mult, ALU.add))
            step(nc.vector.tensor_tensor(start[:], start[:], count[:], ALU.subtract))
            for j, v in enumerate((ex, exc, inc, last, start)):
                own.add(nc.vector.tensor_tensor_reduce(out=scr[:, j, :], in0=own_[:], in1=v[:], scale=1.0, scalar=0.0,
                                                       op0=ALU.mult, op1=ALU.add, accum_out=of[:, j:j + 1]))
            own.settle()
            own.add(nc.vector.tensor_copy(cols[:, 0:1], of[:, 0:1]))
            step(nc.vector.tensor_tensor(cols[:, 1:2], bl[:], of[:, 1:2], ALU.subtract))
            step(ts(cols[:, 1:2], cols[:, 1:2], float(P), of[:, 3:4], ALU.mult, ALU.min))
            own.add(nc.vector.tensor_tensor(cols[:, 4:5], cols[:, 1:2], of[:, 4:5], ALU.add))
            step(nc.vector.scalar_tensor_tensor(shift[:], ex[:], -float(REGION), start[:], ALU.mult, ALU.add))
            step(nc.vector.scalar_tensor_tensor(cols[:, 1:2], of[:, 0:1], float(REGION), cols[:, 1:2], ALU.mult, ALU.add))
            step(ts(of[:, 2:3], of[:, 2:3], -1.0, bl[:], ALU.add, ALU.is_equal))
            for j, most in ((2, EXPERTS - 2), (3, EXPERTS - 3)):
                step(ts(cols[:, j:j + 1], of[:, 0:1], most + 0.5, None, ALU.is_lt))
                step(nc.vector.tensor_tensor(cols[:, j:j + 1], cols[:, j:j + 1], of[:, 2:3], ALU.mult))
            nc.vector.memset(scr[:], 0.0).then_inc(cols_ready, 1)
            dve.wait_ge(turned, 1)
            own.add(nc.vector.tensor_copy(tab[:, 0:4, :].rearrange("p q b -> p (q b)"), ps[0][0:1, :]))
            own.add(nc.vector.tensor_copy(tab[:, 4, :], ps[1][0:1, 0:P]))
            step(ts(pe_[:], K["dest"][:], REGION.bit_length() - 1, None, ALU.logical_shift_right))
            own.add(nc.vector.tensor_copy(pf[:], pe_[:]))
            step(nc.vector.tensor_copy(df[:], K["dest"][:]))
            wide = lambda a: a.unsqueeze(1).broadcast_to([P, 2 * TILES, EXPERTS])
            step(nc.vector.tensor_tensor(match[:], pf[:].unsqueeze(2).broadcast_to([P, 2 * TILES, EXPERTS]), wide(ex[:]),
                                         ALU.is_equal))
            step(nc.vector.tensor_tensor(match[:], match[:], wide(shift[:]), ALU.mult))
            step(nc.vector.tensor_reduce(pf[:], match[:], AX, ALU.add))
            step(nc.vector.tensor_tensor(df[:], df[:], pf[:], ALU.add))
            own.add(nc.vector.tensor_copy(K["dest"][:], df[:]))


def experts_phase(nc, w1, w3, w2, xs, ys, K):
    EXPERT, ROW, NEXT, AFTER, OUT = range(5)
    with ExitStack() as ctx:
        sb = lambda n, s, d=F32: ctx.enter_context(nc.sbuf_tensor(n, s, d))
        psum = lambda n: ctx.enter_context(nc.psum_tensor(n, [P, 512], F32))
        sem = semaphores(nc, ctx, "experts_")
        ident, tab = K["ident"], K["tab"]
        NP, NP2 = 8, 4
        wh = [sb(f"wh{i}", [P, NP, 2, FF], F32R) for i in range(2)]
        wy = [sb(f"wy{i}", [P, KF, D], F32R) for i in range(2)]
        wraw, wraw2 = sb("e_raw", [P, NP, 2 * FF]), sb("e_raw2", [P, NP2, D])
        xb = sb("xb", [P, D])
        xT = [sb(f"xT{i}", [P, KD, P], F32R) for i in range(2)]
        sg, hb = sb("sg", [P, FF]), sb("hb", [P, FF])
        hT = [sb(f"e_hT{i}", [P, FF], F32R) for i in range(2)]
        ob = sb("ob", [P, D])
        flat = lambda a: a.rearrange("p a b -> p (a b)")
        psX = [psum("psX0"), psum("psX1")]
        ps1, ps3, psH = psum("ps1"), psum("ps3"), psum("psHt")
        psO = [psum("psO0"), psum("psO1")]
        NAMES = ("high", "low", "low2", "used", "used2", "x_loaded", "x_turned", "x_high", "x_low", "silu", "h_ready",
                 "h_turned", "h_high", "h_low", "out0", "out1", "out_stored", "high2", "passed", "released")
        S = {n: sem(n) for n in NAMES}
        raw_loaded = [sem(f"raw_loaded{i}") for i in range(NP // 2)]
        raw2_loaded = [sem(f"raw2_loaded{i}") for i in range(NP2 // 2)]
        block = ctx.enter_context(nc.Block())

        def entry(eng, what, b, top=None):
            top = top or (EXPERTS - 1, (EXPERTS - 1) * REGION + SEQ - P, 1, 1, 2 * SEQ)[what]
            return eng.value_load(tab[0:1, what, bass.ds(b, 1)], min_val=0, max_val=top)

        def blocks(eng, run):
            nb = eng.value_load(K["more"][0:1, 0:1], min_val=EXPERTS - PEELED, max_val=MAXB - PEELED) + PEELED
            for b in range(PEELED):
                run(b, b)
            with eng.Fori(PEELED, nb) as b:
                run(b, PEELED)
            return nb

        @block.sync
        def _(sp):
            def load_w(e, first):
                for i in range(NP // 2):
                    if not first:
                        sp.wait_ge(S["low"], e * NP + (2 * i + 2 - NP))
                        sp.sem_inc(S["passed"], 1)
                    w, r = (w1, i) if i < 2 else (w3, i - 2)
                    src = w[0, bass.ds(e, 1), r * 4 * P:(r + 1) * 4 * P, :].rearrange("o (k p) f -> p (o k) f", p=P)
                    sp.dma_start(wraw[:, 2 * i:2 * i + 2, :].rearrange("p i (k f) -> p (i k) f", k=2), src
                                 ).then_inc(raw_loaded[i], 16)

            def load_w2(e, first):
                for i in range(NP2 // 2):
                    if not first:
                        sp.wait_ge(S["low2"], e * NP2 + (2 * i + 2 - NP2))
                        sp.sem_inc(S["passed"], 1)
                    src = w2[0, bass.ds(e, 1), i * 2 * P:(i + 1) * 2 * P, :].rearrange("o (k p) f -> p (o k) f", p=P)
                    sp.dma_start(wraw2[:, 2 * i:2 * i + 2, :], src).then_inc(raw2_loaded[i], 16)

            load_w(0, True)
            load_w2(0, True)
            load_w(1, False)
            with sp.Fori(1, EXPERTS - 1) as e:
                load_w(e + 1, False)
                load_w2(e, False)
            load_w2(EXPERTS - 1, False)

        @block.gpsimd
        def _(pool):
            def store(j, n):
                pool.wait_ge(S["out0"], j + 1)
                pool.wait_ge(S["out1"], j + 1)
                pool.sem_inc(S["passed"], 1)
                pool.dma_start(ys[bass.ds(entry(pool, OUT, j), P), :], ob[:]).then_inc(S["out_stored"], 16)

            def run(b, n):
                if n:
                    pool.wait_ge(S["x_turned"], b + 0)
                    pool.sem_inc(S["passed"], 1)
                pool.dma_start(xb[:], xs[bass.ds(entry(pool, ROW, b), P), :]).then_inc(S["x_loaded"], 16)
                if n == 3:
                    store(b - 3, n)

            nb = blocks(pool, run)
            for j in range(3):
                store(nb + (j - 3), 3)
            pool.wait_ge(S["out_stored"], nb * 16)
            pool.sem_inc(S["passed"], 1)

        def next_w2(eng, j, pieces2):
            with eng.If(entry(eng, NEXT, j) == 1):
                pieces2(entry(eng, EXPERT, j, EXPERTS - 2) + 1)

        def next_expert(eng, b, pieces):
            with eng.If(entry(eng, NEXT, b) == 1):
                pieces(entry(eng, EXPERT, b, EXPERTS - 2) + 1, b)

        @block.scalar
        def _(act):
            def pieces(e, b=None):
                for i in range(NP):
                    act.wait_ge(raw_loaded[i // 2], e * 16 + 16)
                    if b is not None:
                        act.wait_ge(S["used"], b * NP + (i + 1))
                    nc.scalar.copy(flat(wh[0][:, i]), wraw[:, i, :]).then_inc(S["high"], 1)

            def pieces2(e):
                for i in range(NP2):
                    act.wait_ge(raw2_loaded[i // 2], e * 16 + 16)
                    nc.scalar.copy(wy[0][:, i, :], wraw2[:, i, :]).then_inc(S["high2"], 1)

            def out(j, n):
                act.wait_ge(S["used2"], j * NP2 + NP2)
                if n:
                    act.wait_ge(S["out_stored"], j * 16)
                nc.scalar.copy(ob[:, 0:512], psO[0][:]).then_inc(S["out0"], 1)

            def h_high(j):
                act.wait_ge(S["h_turned"], j + 1)
                nc.scalar.copy(hT[0][:], psH[:]).then_inc(S["h_high"], 1)

            def run(b, n):
                act.wait_ge(S["x_turned"], b + 1)
                if n:
                    act.wait_ge(S["used"], b * NP)
                for i in range(2):
                    last = nc.scalar.copy(flat(xT[0][:, 4 * i:4 * i + 4]), psX[i][:])
                last.then_inc(S["x_high"], 1)
                if n >= 2:
                    out(b - 2, n - 2)
                if n >= 1:
                    h_high(b - 1)
                if n >= 2:
                    next_w2(act, b - 2, pieces2)
                act.wait_ge(S["used"], b * NP + 4)
                if n:
                    act.wait_ge(S["h_ready"], b + 0)
                nc.scalar.activation(sg[:], ps1[:], ACT.Silu).then_inc(S["silu"], 1)
                next_expert(act, b, pieces)

            pieces(0)
            pieces2(0)
            nb = blocks(act, run)
            out(nb - 2, 3)
            h_high(nb - 1)
            next_w2(act, nb - 2, pieces2)
            out(nb - 1, 3)

        @block.tensor
        def _(pe):
            def turn(b, n):
                pe.wait_ge(S["x_loaded"], b * 16 + 16)
                if n:
                    pe.wait_ge(S["x_low"], b + 0)
                for k in range(KD):
                    mm = nc.tensor.transpose(psX[k // 4][:, (k % 4) * P:(k % 4 + 1) * P], xb[:, k * P:(k + 1) * P], ident[:])
                mm.then_inc(S["x_turned"], 1)

            def first_products(b, n):
                e8 = pe.snap(entry(pe, EXPERT, b) * NP)
                pe.wait_ge(S["x_low"], b + 1)
                if n:
                    pe.wait_ge(S["h_ready"], b + 0)
                for i in range(NP):
                    ps, r = (ps1, i) if i < 4 else (ps3, i - 4)
                    pe.wait_ge(S["low"], e8 + (i + 1))
                    for k in range(2):
                        for l, w in ((1, 0), (0, 1), (0, 0)):
                            mm = nc.tensor.matmul(ps[:], xT[l][:, 2 * r + k, :], wh[w][:, i, k, :],
                                                  start=(r == 0 and k == 0 and l == 1),
                                                  stop=(r == 3 and k == 1 and l == 0 and w == 0))
                    mm.then_inc(S["used"], 1)

            def second_product(j, n):
                e4 = pe.snap(entry(pe, EXPERT, j) * NP2)
                pe.wait_ge(S["h_low"], j + 1)
                if n:
                    pe.wait_ge(S["out0"], j + 0)
                    pe.wait_ge(S["out1"], j + 0)
                for k in range(KF):
                    pe.wait_ge(S["low2"], e4 + (k + 1))
                    for o in range(2):
                        for l, w in ((1, 0), (0, 1), (0, 0)):
                            mm = nc.tensor.matmul(psO[o][:], hT[l][:, k * P:(k + 1) * P], wy[w][:, k, o * 512:(o + 1) * 512],
                                                  start=(k == 0 and l == 1), stop=(k == KF - 1 and l == 0 and w == 0))
                    mm.then_inc(S["used2"], 1)

            def turn_h(j):
                pe.wait_ge(S["h_ready"], j + 1)
                for k in range(KF):
                    mm = nc.tensor.transpose(psH[:, k * P:(k + 1) * P], hb[:, k * P:(k + 1) * P], ident[:])
                mm.then_inc(S["h_turned"], 1)

            def run(b, n):
                turn(b, n)
                if n >= 2:
                    second_product(b - 2, n - 2)
                if n >= 1:
                    turn_h(b - 1)
                first_products(b, n)

            nb = blocks(pe, run)
            second_product(nb - 2, 3)
            turn_h(nb - 1)
            second_product(nb - 1, 3)

        @block.vector
        def _(dve):
            def pieces(e, b=None):
                for i in range(NP):
                    dve.wait_ge(S["high"], e * NP + (i + 1))
                    nc.vector.tensor_tensor(flat(wh[1][:, i]), wraw[:, i, :], flat(wh[0][:, i]).bitcast(F32), ALU.subtract
                                            ).then_inc(S["low"], 1)

            def pieces2(e):
                for i in range(NP2):
                    dve.wait_ge(S["high2"], e * NP2 + (i + 1))
                    nc.vector.tensor_tensor(wy[1][:, i, :], wraw2[:, i, :], wy[0][:, i, :].bitcast(F32), ALU.subtract
                                            ).then_inc(S["low2"], 1)

            def out(j, n):
                dve.wait_ge(S["used2"], j * NP2 + NP2)
                if n:
                    dve.wait_ge(S["out_stored"], j * 16)
                nc.vector.tensor_copy(ob[:, 512:1024], psO[1][:]).then_inc(S["out1"], 1)

            def h_low(j):
                dve.wait_ge(S["h_high"], j + 1)
                nc.vector.tensor_tensor(hT[1][:], psH[:], hT[0][:].bitcast(F32), ALU.subtract).then_inc(S["h_low"], 1)

            def run(b, n):
                dve.wait_ge(S["x_high"], b + 1)
                for i in range(2):
                    last = nc.vector.tensor_tensor(flat(xT[1][:, 4 * i:4 * i + 4]), psX[i][:],
                                                   flat(xT[0][:, 4 * i:4 * i + 4]).bitcast(F32), ALU.subtract)
                last.then_inc(S["x_low"], 1)
                if n >= 2:
                    out(b - 2, n - 2)
                if n >= 1:
                    h_low(b - 1)
                if n >= 2:
                    next_w2(dve, b - 2, pieces2)
                dve.wait_ge(S["silu"], b + 1)
                dve.wait_ge(S["used"], b * NP + NP)
                if n:
                    dve.wait_ge(S["h_turned"], b + 0)
                nc.vector.tensor_tensor(hb[:], sg[:], ps3[:], ALU.mult).then_inc(S["h_ready"], 1)
                next_expert(dve, b, pieces)

            pieces(0)
            pieces2(0)
            nb = blocks(dve, run)
            out(nb - 2, 3)
            h_low(nb - 1)
            next_w2(dve, nb - 2, pieces2)
            out(nb - 1, 3)


def final_phase(nc, final_w, x1dram, ys, outd, K):
    with ExitStack() as ctx:
        sb = lambda n, s, d=F32: ctx.enter_context(nc.sbuf_tensor(n, s, d))
        sem = semaphores(nc, ctx, "final_")
        dest, gates = K["dest"], K["gates"]
        r = [[sb(f"r{i}{j}", [P, D]) for j in range(2)] for i in range(2)]
        x1 = [sb(f"fx{i}", [P, D]) for i in range(2)]
        sq = [sb(f"fsq{i}", [P, D]) for i in range(2)]
        fo = [sb(f"fo{i}", [P, D]) for i in range(2)]
        g2row, fw = sb("g2row", [P, D]), sb("fw", [P, D])
        di = [sb(f"di{i}", [P, 2], U32) for i in range(2)]
        gi = [sb(f"gi{i}", [P, 2]) for i in range(2)]
        st = [sb(f"fst{i}", [P, 4]) for i in range(2)]
        minus_half, eps = sb("f_minus_half", [P, 1]), sb("f_eps", [P, 1])
        ps = [ctx.enter_context(nc.psum_tensor(f"f_ps{i}", [P, 512], F32)) for i in range(2)]
        NAMES = ("rows_done", "rows_copied", "w_loaded", "index", "scaled", "mixed", "gated", "added", "squared", "mean",
                 "rstd", "normed", "consts", "passed")
        S = {n: sem(n) for n in NAMES}
        gathered = [sem(f"gathered{i}") for i in range(2)]
        x_loaded = [sem(f"x_loaded{i}") for i in range(2)]
        stored = [sem(f"stored{i}") for i in range(2)]
        block = ctx.enter_context(nc.Block())

        def pairs(eng, run):
            run(0, 0, 0)
            run(1, 1, 0)
            with eng.Fori(1, TILES // 2) as p:
                for i in range(2):
                    run(p * 2 + i, i, 1)

        @block.sync
        def _(sp):
            sp.dma_start(fw[:], final_w.rearrange("(o d) -> o d", o=1).broadcast_to([P, D])).then_inc(S["w_loaded"], 16)

            def load(t, i, n):
                if n:
                    sp.wait_ge(S["normed"], t - 1)
                sp.dma_start(x1[i][:], x1dram[bass.ds(t * P, P), :]).then_inc(x_loaded[i], 16)

            pairs(sp, load)

        @block.gpsimd
        def _(pool):
            nc.gpsimd.memset(minus_half[:], -0.5).then_inc(S["consts"], 1)
            nc.gpsimd.memset(eps[:], EPS).then_inc(S["consts"], 1)
            pool.wait_ge(S["consts"], 2)

            def gather(t, i, n):
                pool.wait_ge(S["index"], t + 1)
                if n:
                    pool.wait_ge(S["added"], t - 1)
                pool.sem_inc(S["passed"], 1)
                for j in range(2):
                    nc.gpsimd.indirect_dma_start(r[i][j][:], None, ys[0:2 * SEQ, :], bass.IndirectOffsetOnAxis(ap=di[i][:, j:j + 1], axis=0)
                                                 ).then_inc(gathered[i], 16)

            def add(t, i):
                pool.wait_ge(x_loaded[i], (t - i) * 8 + 16)
                pool.wait_ge(S["gated"], t + 1)
                nc.gpsimd.tensor_tensor(x1[i][:], x1[i][:], r[i][0][:], ALU.add).then_inc(S["added"], 1)

            def rstd(t, i):
                pool.wait_ge(S["squared"], t + 1)
                nc.gpsimd.tensor_tensor(st[i][:, 1:2], st[i][:, 0:1], eps[:], ALU.add).then_inc(S["mean"], 1)
                pool.wait_ge(S["mean"], t + 1)
                nc.gpsimd.tensor_tensor(st[i][:, 2:3], st[i][:, 1:2], minus_half[:], ALU.pow).then_inc(S["rstd"], 1)

            gather(0, 0, 0)
            gather(1, 1, 0)
            with pool.Fori(0, TILES // 2 - 1) as p:
                for i in range(2):
                    t = p * 2 + i
                    add(t, i)
                    gather(t + 2, i, 1)
                    rstd(t, i)
            for i in range(2):
                add(TILES - 2 + i, i)
                rstd(TILES - 2 + i, i)

        @block.scalar
        def _(act):
            def scale(t, i, n):
                act.wait_ge(gathered[i], (t - i) * 16 + 32)
                nc.scalar.activation(r[i][0][:], r[i][0][:], ACT.Copy, scale=gi[i][:, 0:1]).then_inc(S["scaled"], 1)

            def square(t, i, n):
                act.wait_ge(S["added"], t + 1)
                nc.scalar.activation(sq[i][:], x1[i][:], ACT.Square, scale=D ** -0.5, accum_out=st[i][:, 0:1]
                                     ).then_inc(S["squared"], 1)

            def store(t, i):
                act.wait_ge(S["normed"], t + 1)
                act.sem_inc(S["passed"], 1)
                act.dma_start(outd[0, bass.ds(t * P, P), :], fo[i][:]).then_inc(stored[i], 16)

            scale(0, 0, 0)
            square(0, 0, 0)
            scale(1, 1, 0)
            square(1, 1, 0)
            with act.Fori(1, TILES // 2) as p:
                for i in range(2):
                    t = p * 2 + i
                    scale(t, i, 1)
                    store(t - 2, i)
                    square(t, i, 1)
            for i in range(2):
                store(TILES - 2 + i, i)
            for i in range(2):
                act.wait_ge(stored[i], TILES // 2 * 16)

        @block.tensor
        def _(pe):
            for i in range(2):
                for k in range(4):
                    o = 5 * KD + 4 * i + k
                    mm = nc.tensor.matmul(ps[i][:, k * P:(k + 1) * P], K["mod"][:, o:o + 1].broadcast_to([P, P]),
                                          K["ident"][:], start=True, stop=True)
                mm.then_inc(S["rows_done"], 1)

        @block.vector
        def _(dve):
            def index(t, i, n):
                if n:
                    dve.wait_ge(S["mixed"], t - 1)
                    dve.wait_ge(gathered[i], (t - i) * 16)
                    dve.sem_inc(S["passed"], 1)
                nc.vector.tensor_copy(gi[i][:], gates[:, bass.ds(t * 2, 2)])
                nc.vector.tensor_copy(di[i][:], dest[:, bass.ds(t * 2, 2)]).then_inc(S["index"], 1)

            def mix(t, i):
                dve.wait_ge(S["scaled"], t + 1)
                nc.vector.scalar_tensor_tensor(r[i][0][:], r[i][1][:], gi[i][:, 1:2], r[i][0][:], ALU.mult, ALU.add
                                               ).then_inc(S["mixed"], 1)
                dve.wait_ge(S["mixed"], t + 1)
                nc.vector.tensor_tensor(r[i][0][:], r[i][0][:], g2row[:], ALU.mult).then_inc(S["gated"], 1)

            def norm(t, i, n):
                dve.wait_ge(S["rstd"], t + 1)
                if n:
                    dve.wait_ge(stored[i], (t - i) * 8)
                nc.vector.scalar_tensor_tensor(fo[i][:], x1[i][:], st[i][:, 2:3], fw[:], ALU.mult, ALU.mult
                                               ).then_inc(S["normed"], 1)

            index(0, 0, 0)
            index(1, 1, 0)
            for i in range(2):
                dve.wait_ge(S["rows_done"], i + 1)
                nc.vector.tensor_copy(g2row[:, i * 512:(i + 1) * 512], ps[i][:]).then_inc(S["rows_copied"], 1)
            dve.wait_ge(S["rows_copied"], 2)
            dve.wait_ge(S["w_loaded"], 16)
            for i in range(2):
                mix(i, i)
                index(i + 2, i, 1)
                norm(i, i, 0)
            with dve.Fori(1, TILES // 2 - 1) as p:
                for i in range(2):
                    t = p * 2 + i
                    mix(t, i)
                    index(t + 2, i, 1)
                    norm(t, i, 1)
            for i in range(2):
                mix(TILES - 2 + i, i)
                norm(TILES - 2 + i, i, 1)


def build(nc, a, out, xs, ydram, x1dram, ys):
    with ExitStack() as ctx:
        sb = lambda n, s, d=F32: ctx.enter_context(nc.sbuf_tensor(n, s, d))
        keep = lambda *which: {n: sb("k_" + n, s, d) for n, s, d in which}
        K = keep(
            ("ident", [P, P], F32), ("upper", [P, P], F32), ("ones", [P, P], F32), ("mask", [P, P], F32),
            ("identb", [P, P], BF16), ("maskb", [P, P], BF16), ("strictb", [P, P], BF16), ("onesb", [P, P], BF16),
            ("mod", [P, 6 * KD], F32), ("a1", [P, KD], F32), ("a2", [P, KD], F32),
            ("conv", [P, TAPS + 1, CB], F32))
        mod_phase(nc, a["c"], a["ada_w"], a["ada_b"], a["norm_mix_w"], a["norm_ffn_w"], a["ssm_conv_w"],
                  a["ssm_conv_b"], K)
        mixer_phase(nc, a["x"], a["ssm_in_w"], a["ssm_dt_bias"], a["ssm_a_log"], a["ssm_d"], a["ssm_norm_w"], ydram,
                    xs, K)
        K.update(keep(
            ("dest", [P, 2 * TILES], U32), ("gates", [P, 2 * TILES], F32), ("count", [P, EXPERTS], F32),
            ("tab", [1, 5, P], I32), ("more", [P, 1], I32)))
        out_phase(nc, a["x"], a["ssm_out_w"], a["moe_group_w"], a["moe_group_b"], a["moe_expert_w"],
                  a["moe_expert_b"], ydram, x1dram, xs, K)
        plan_phase(nc, K)
        experts_phase(nc, a["moe_w1"], a["moe_w3"], a["moe_w2"], xs, ys, K)
        final_phase(nc, a["final_norm_w"], x1dram, ys, out, K)


USED = ("x", "c", "ada_w", "ada_b", "norm_mix_w", "norm_ffn_w", "ssm_in_w", "ssm_conv_w", "ssm_conv_b", "ssm_dt_bias",
        "ssm_a_log", "ssm_d", "ssm_norm_w", "ssm_out_w", "moe_group_w", "moe_group_b", "moe_expert_w", "moe_expert_b",
        "moe_w1", "moe_w3", "moe_w2", "final_norm_w")


def kernel(**inputs):
    import numpy as np
    import concourse.bacc as bacc
    from concourse.bass_utils import run_bass_kernel_spmd

    nc = bacc.Bacc("TRN2", target_bir_lowering=False, num_devices=1)
    arrays, args = {}, {}
    for name in USED:
        arrays[f"in_{name}"] = np.ascontiguousarray(inputs[name])
        args[name] = nc.dram_tensor(f"in_{name}", arrays[f"in_{name}"].shape, F32, kind="ExternalInput").ap()
    out = nc.dram_tensor("out", (1, SEQ, D), F32, kind="ExternalOutput").ap()
    scratch = lambda name, shape: nc.dram_tensor(name, shape, F32, kind="Internal").ap()
    build(nc, args, out, scratch("xs", (EXPERTS * REGION, D)), scratch("y_inner", (SEQ, DI)),
          scratch("x1", (SEQ, D)), scratch("ys", (2 * SEQ + P, D)))
    r = run_bass_kernel_spmd(nc, [arrays], core_ids=[0])
    return r.results[0]["out"]
```

```python
from contextlib import ExitStack

import concourse.bass as bass
from concourse import mybir

F32 = mybir.dt.float32
F32R = mybir.dt.float32r
BF16 = mybir.dt.bfloat16
I32 = mybir.dt.int32
U32 = mybir.dt.uint32
ALU = mybir.AluOpType
ACT = mybir.ActivationFunctionType
AX = mybir.AxisListType.X

P = 128
D = 1024
KD = D // P
SEQ = 2048
TILES = SEQ // P
HALVES = 2
HT = TILES // HALVES
HTOK = HT * P
EPS = 1e-6

DI = 2048
G = 8
GW = DI // G
HG = 4
HEADS = G * HG
PD = 64
N = 128
CONV_DIM = DI + 2 * G * N
CB = CONV_DIM // P
TAPS = 4
KI = DI // P
SUP = 512
CS = SUP // P
PIECES = 6

GROUPS = 4
EPG = 8
EXPERTS = GROUPS * EPG
FF = 512
KF = FF // P
REGION = SEQ
BIG = 1e30


def semaphores(nc, ctx, phase):
    taken = []

    def take(name):
        taken.append(nc.alloc_semaphore(phase + name))
        return taken[-1]

    def give_back():
        nc.clear_and_free_semaphores(taken)
        nc.all_engine_barrier()

    ctx.callback(give_back)
    return take


class Steps:

    def __init__(self, eng, sem, base=0):
        self.eng, self.sem, self.base, self.n = eng, sem, base, 0

    def add(self, ins):
        ins.then_inc(self.sem, 1)
        self.n += 1

    def settle(self):
        self.eng.wait_ge(self.sem, self.base + self.n)


def mod_phase(nc, c, ada_w, ada_b, norm_mix_w, norm_ffn_w, conv_w, conv_b, K):
    NV = KD + 6 * KD + 2 * KD + CB
    with ExitStack() as ctx:
        sb = lambda n, s, d=F32: ctx.enter_context(nc.sbuf_tensor(n, s, d))
        sem = semaphores(nc, ctx, "mod_")
        W = [sb(f"ada_w{i}", [P, KD, D]) for i in range(3)]
        acc = [sb(f"mod_sum{i}", [P, D]) for i in range(2)]
        vrows = sb("vrows", [NV, P])
        trows = sb("trows", [P, P])
        vcols = sb("vcols", [P, NV])
        cs = sb("cs", [P, KD])
        ps = ctx.enter_context(nc.psum_tensor("ps_mod", [P, 512], F32))
        pv = ctx.enter_context(nc.psum_tensor("ps_vec", [P, 512], F32))
        rows_loaded, w_loaded = sem("rows_loaded"), [[sem(f"w_loaded{i}{n}") for n in range(2)] for i in range(3)]
        turned, cols_ready, cs_ready = sem("turned"), sem("cols_ready"), sem("cs_ready")
        mod_done, consts_ready, psteps, vsteps = sem("mod_done"), sem("consts_ready"), sem("psteps"), sem("vsteps")
        summed = sem("summed")
        ident, upper = K["ident"], K["upper"]
        mod = K["mod"]
        block = ctx.enter_context(nc.Block())

        @block.sync
        def _(sp):
            r = 0
            for src in (c, ada_b, norm_mix_w, norm_ffn_w, conv_b):
                src = src.rearrange("o (k p) -> (o k) p", p=P)
                sp.dma_start(vrows[r:r + src.shape[0], :], src).then_inc(rows_loaded, 16)
                r += src.shape[0]
            sp.dma_start(trows[:], conv_w[0].rearrange("t (b p) -> (t b) p", p=P)).then_inc(rows_loaded, 16)
            for j in range(6):
                if j >= 3:
                    sp.wait_ge(summed, j - 2)
                for n in range(2):
                    sp.dma_start(W[j % 3][:, 4 * n:4 * n + 4, :],
                                 ada_w[0, 4 * n * P:(4 * n + 4) * P, j * D:(j + 1) * D].rearrange("(k p) n -> p k n", p=P)
                                 ).then_inc(w_loaded[j % 3][n], 16)

        @block.gpsimd
        def _(pool):
            own = Steps(pool, psteps)
            own.add(nc.gpsimd.memset(ident[:], 0.0))
            own.add(nc.gpsimd.memset(upper[:], 1.0))
            own.add(nc.gpsimd.memset(K["ones"][:], 1.0))
            own.add(nc.gpsimd.memset(K["mask"][:], 0.0))
            own.settle()
            own.add(nc.gpsimd.affine_select(out=ident[:], in_=ident[:], compare_op=ALU.not_equal, fill=1.0,
                                            base=0, pattern=[[-1, P]], channel_multiplier=1))
            own.add(nc.gpsimd.affine_select(out=upper[:], in_=upper[:], compare_op=ALU.is_ge, fill=0.0,
                                            base=0, pattern=[[1, P]], channel_multiplier=-1))
            own.add(nc.gpsimd.affine_select(out=K["mask"][:], in_=K["mask"][:], compare_op=ALU.is_ge, fill=-BIG,
                                            base=0, pattern=[[1, P]], channel_multiplier=-1))
            own.settle()
            own.add(nc.gpsimd.tensor_copy(K["identb"][:], ident[:]))
            own.add(nc.gpsimd.tensor_copy(K["maskb"][:], K["mask"][:]))
            own.add(nc.gpsimd.tensor_tensor(K["strictb"][:], upper[:], ident[:], ALU.subtract))
            own.add(nc.gpsimd.tensor_copy(K["onesb"][:], K["ones"][:]))
            own.settle()
            pool.sem_inc(consts_ready, 1)

        @block.scalar
        def _(act):
            act.wait_ge(cols_ready, 1)
            nc.scalar.activation(cs[:], vcols[:, 0:KD], ACT.Silu).then_inc(cs_ready, 1)

        @block.tensor
        def _(pe):
            pe.wait_ge(consts_ready, 1)
            pe.wait_ge(rows_loaded, 6 * 16)
            nc.tensor.transpose(pv[:, 0:NV], vrows[:], ident[0:NV, 0:NV]).then_inc(turned, 1)
            nc.tensor.transpose(pv[:, P:2 * P], trows[:], ident[:]).then_inc(turned, 1)
            for j in range(6):
                pe.wait_ge(summed, j + 1)
                for m in range(KD):
                    mm = nc.tensor.matmul(ps[:, j * KD + m:j * KD + m + 1], acc[j % 2][:, m * P:(m + 1) * P],
                                          K["ones"][:, 0:1], start=True, stop=True)
                mm.then_inc(mod_done, 1)

        @block.vector
        def _(dve):
            own = Steps(dve, vsteps)
            dve.wait_ge(turned, 2)
            nc.vector.tensor_copy(vcols[:], pv[:, 0:NV]).then_inc(cols_ready, 1)
            own.add(nc.vector.tensor_scalar(K["conv"][:, 0:TAPS, :], pv[:, P:2 * P].rearrange("p (t b) -> p t b", t=TAPS),
                                            0.5, None, ALU.mult))
            dve.wait_ge(cols_ready, 1)
            own.add(nc.vector.tensor_scalar(K["conv"][:, TAPS, :], vcols[:, 9 * KD:9 * KD + CB], 0.5, None, ALU.mult))
            dve.wait_ge(cs_ready, 1)
            for j in range(6):
                dve.wait_ge(w_loaded[j % 3][0], 16 * (j // 3 + 1))
                if j >= 2:
                    dve.wait_ge(mod_done, j - 1)
                own.add(nc.vector.tensor_scalar(acc[j % 2][:], W[j % 3][:, 0, :], cs[:, 0:1], None, ALU.mult))
                for k in range(1, KD):
                    own.settle()
                    if k == KD // 2:
                        dve.wait_ge(w_loaded[j % 3][1], 16 * (j // 3 + 1))
                    ins = nc.vector.scalar_tensor_tensor(acc[j % 2][:], W[j % 3][:, k, :], cs[:, k:k + 1], acc[j % 2][:],
                                                         ALU.mult, ALU.add)
                    if k < KD - 1:
                        own.add(ins)
                ins.then_inc(summed, 1)
            dve.wait_ge(mod_done, 6)
            own.add(nc.vector.tensor_tensor(mod[:], ps[:, 0:6 * KD], vcols[:, KD:7 * KD], ALU.add))
            own.settle()
            own.add(nc.vector.scalar_tensor_tensor(K["a1"][:], mod[:, KD:2 * KD], 1.0, vcols[:, 7 * KD:8 * KD],
                                                   ALU.add, ALU.mult))
            own.add(nc.vector.scalar_tensor_tensor(K["a2"][:], mod[:, 4 * KD:5 * KD], 1.0, vcols[:, 8 * KD:9 * KD],
                                                   ALU.add, ALU.mult))


def mixer_phase(nc, x, in_w, dt_bias, a_log, d_skip, norm_w, ydram, xs, K):
    with ExitStack() as ctx:
        sb = lambda n, s, d=F32: ctx.enter_context(nc.sbuf_tensor(n, s, d))
        psum = lambda n: ctx.enter_context(nc.psum_tensor(n, [P, 512], F32))
        sem = semaphores(nc, ctx, "mixer_")
        ident, upper, ones, maskb, identb = (K[x] for x in ("ident", "upper", "ones", "maskb", "identb"))
        hT = [sb(f"hT{i}", [P, KD, HTOK], F32R) for i in range(2)]
        wfm = [sb(f"wfm{i}", [P, 4, KD, P], F32R) for i in range(2)]
        wz = [sb(f"wz{i}", [P, KD, GW], F32R) for i in range(2)]
        wraw = sb("wraw", [P, 3, KD * P])
        raw = sb("raw", [P, 2, 3 + SUP])
        cv = sb("cv", [P, 2, SUP])
        fm = [sb(f"fm{i}", [P, 4, SUP]) for i in range(2)]
        zs = sb("zs", [P, CS, GW])
        zero = sb("zero", [P, D])
        tok = [sb(f"tok{i}", [P, 3 * P]) for i in range(2)]
        gm = [sb(f"gm{i}", [P, HG, P]) for i in range(2)]
        xdt = [sb(f"xdt{i}", [P, HG, PD]) for i in range(2)]
        xde = [sb(f"xde{i}", [P, HG, PD]) for i in range(2)]
        xd = [sb(f"xd{i}", [P, HG, PD]) for i in range(2)]
        yt = [sb(f"yt{i}", [P, HG, PD]) for i in range(2)]
        ysq = sb("ysq", [P, GW])
        yo = [sb(f"yo{i}", [P, GW]) for i in range(2)]
        ssq = sb("ssq", [P, 6])
        state = sb("state", [P, HG, PD])
        states = sb("states", [P, G, HG * PD])
        hist = sb("hist", [P, 12, G])
        histg = sb("histg", [P, 2, 4, 3])
        nw = sb("nw", [P, DI])
        vecg = sb("vecg", [P, TAPS + 1, 4])
        dbias = sb("dbias", [P, HEADS])
        aneg = sb("aneg", [P, HEADS])
        W8 = HT * HEADS
        pk = sb("pk", [P, 5 * HT + 1, HEADS])
        pkg = sb("pkg", [P, 5 * HT + 1, HG])
        da = [sb(f"da{i}", [P, HT, HEADS], F32R) for i in range(2)]
        dag = [sb(f"dag{i}", [P, HT, HG], F32R) for i in range(2)]
        wdt = sb("wdt", [P, KD, HEADS])
        wdts = [sb(f"wdts{i}", [P, KD, HEADS], F32R) for i in range(2)]
        upr = sb("upr", [P, P], F32R)
        tss = sb("tss", [P, 2, 3])
        minus_half = sb("minus_half", [P, 1])
        eps = sb("eps", [P, 1])
        flat = lambda a: a.rearrange("p a b -> p (a b)")
        xt = [flat(fm[i][:, 0:2, :]) for i in range(2)]
        xsq = [flat(fm[0][:, 2:4, :]), flat(zs[:])]
        v = [a.rearrange("p (k n) -> p k n", k=KD) for a in (flat(fm[1][:, 2:4, :]), flat(cv[:]))]
        T = [cv[:, i // 2, (i % 2) * W8:(i % 2 + 1) * W8] for i in range(4)]
        T += [zs[:, i, :] for i in range(4)]
        row = lambda i: flat(pk[:, i * HT:(i + 1) * HT, :])
        DT, NAC, EAC, DTE, CDEC = range(5)
        dtcol = lambda q, c: pkg[:, q * HT + c, :]

        psF = [psum("psF0"), psum("psF1")]
        psZ = psum("psZ")
        psT = [psum("psT0"), psum("psT1")]
        psS = [psum("psS0"), psum("psS1")]
        turned_x = [psF, psT]
        psY = psum("psY")
        NAMES = ("vec_loaded", "nw_loaded", "x_sq", "x_scaled", "x_turned", "v_ready", "v_high", "h_ready", "wdt_ready",
                 "dt_cols", "dt_copied", "dt_done",
                 "dt_low", "dt_exp", "dt_ln", "dt_ready", "cum_done", "cum_sub", "cum_exp", "aneg_ready", "x_mean",
                 "x_rstd", "half_ready", "w_high", "w_low", "z_low", "taps_ready", "fm_done", "fm_out", "conv_done",
                 "fm_tanh", "fm_ready", "z_done", "z_tanh", "z_ready", "turned", "seg_done", "tok_ready",
                 "decay_ready", "gm_ready", "x_parts", "scan_done", "state_ready", "y_read", "y_gated", "y_squared",
                 "y_mean", "y_rstd", "y_ready", "group_ready", "half_steps", "loop_steps", "last_steps", "start_steps",
                 "zeroed", "passed", "w_order", "zero_stored")
        S = {n: sem(n) for n in NAMES}
        x_loaded = [sem(f"x_loaded{i}") for i in range(2)]
        raw_loaded = [sem(f"raw_loaded{i}") for i in range(3)]
        y_stored = [sem(f"y_stored{i}") for i in range(2)]
        block = ctx.enter_context(nc.Block())

        @block.sync
        def _(sp):
            def load_x(h, t):
                if t >= 2:
                    sp.wait_ge(S["x_turned"], h * HT + t - 1)
                elif h:
                    sp.wait_ge(S["y_gated"], h * G * HT - (0 if t else CS))
                sp.dma_start(xt[t % 2], x[0, h * HTOK + t * P:h * HTOK + (t + 1) * P, :]).then_inc(x_loaded[t % 2], 16)

            load_x(0, 0)
            load_x(0, 1)
            sp.dma_start(dbias[:], dt_bias.broadcast_to([P, HEADS])).then_inc(S["vec_loaded"], 16)
            sp.dma_start(aneg[:], a_log.broadcast_to([P, HEADS])).then_inc(S["vec_loaded"], 16)
            sp.dma_start(pk[:, 5 * HT, :], d_skip.broadcast_to([P, HEADS])).then_inc(S["vec_loaded"], 16)
            sp.dma_start(wdt[:], in_w[0, :, DI + CONV_DIM:].rearrange("(k p) n -> p k n", p=P)
                         ).then_inc(S["vec_loaded"], 16)

            def load_piece(it, g, m):
                if m >= 3:
                    sp.wait_ge(S["w_low"], it * 4 + (m - 2))
                elif m >= 1:
                    sp.wait_ge(S["z_low"], it * 2)
                else:
                    sp.wait_ge(S["w_low"], it * 4)
                sp.sem_inc(S["passed"], 1)
                if m < 2:
                    src = in_w[0, :, bass.ds(DI + g * GW + m * P, P)].rearrange("(k p) n -> p k n", p=P)
                elif m < 4:
                    src = in_w[0, :, bass.ds(2 * DI + (m - 2) * G * N + g * N, P)].rearrange("(k p) n -> p k n", p=P)
                else:
                    src = in_w[0, (m - 4) * 4 * P:(m - 3) * 4 * P, bass.ds(g * GW, GW)].rearrange("(k p) n -> p k n", p=P)
                dst = wraw[:, m % 3, :].rearrange("p (k n) -> p k n", k=src.shape[1])
                sp.dma_start(dst, src).then_inc(raw_loaded[m % 3], 16)

            def store_y(h, it, g, c):
                sp.wait_ge(S["y_ready"], it * HT + (c + 1))
                sp.dma_start(ydram[h * HTOK + c * P:h * HTOK + (c + 1) * P, bass.ds(g * GW, GW)], yo[c % 2][:]
                             ).then_inc(y_stored[c % 2], 16)

            def store_zeros(it):
                for i in range(EXPERTS // (HALVES * G)):
                    e = it * (EXPERTS // (HALVES * G)) + i
                    sp.dma_start(xs[bass.ds(e * REGION, P), :], zero[:]).then_inc(S["zero_stored"], 16)

            for h in range(HALVES):
                for m in range(3):
                    load_piece(h * G, 0, m)
                for t in range(1 if h else 2, HT):
                    load_x(h, t)
                if not h:
                    sp.dma_start(nw[:], norm_w.broadcast_to([P, DI])).then_inc(S["nw_loaded"], 16)
                for m in range(3, PIECES):
                    load_piece(h * G, 0, m)
                if not h:
                    sp.wait_ge(S["zeroed"], 5)
                with sp.Fori(0, G - 1) as g:
                    it = g + h * G
                    for m in range(3):
                        load_piece(it + 1, g + 1, m)
                    store_y(h, it, g, 0)
                    for m in range(3, PIECES):
                        store_y(h, it, g, m - 2)
                        load_piece(it + 1, g + 1, m)
                    store_zeros(it)
                    for c in range(PIECES - 2, HT):
                        store_y(h, it, g, c)
                for c in range(HT):
                    store_y(h, h * G + G - 1, G - 1, c)
                    if c == CS and h + 1 < HALVES:
                        load_x(h + 1, 0)
                store_zeros(h * G + G - 1)
            sp.wait_ge(S["zero_stored"], 16 * EXPERTS)
            for q in y_stored:
                sp.wait_ge(q, 16 * (HALVES * G * HT // 2 + 1))

        @block.gpsimd
        def _(pool):
            nc.gpsimd.memset(states[:], 0.0).then_inc(S["zeroed"], 1)
            nc.gpsimd.memset(hist[:], 0.0).then_inc(S["zeroed"], 1)
            nc.gpsimd.memset(minus_half[:], -0.5).then_inc(S["zeroed"], 1)
            nc.gpsimd.memset(eps[:], EPS).then_inc(S["zeroed"], 1)
            nc.gpsimd.memset(zero[:], 0.0).then_inc(S["zeroed"], 1)
            pool.wait_ge(S["zeroed"], 5)

            def half(h):
                for t in range(HT):
                    pool.wait_ge(S["x_sq"], h * HT + (t + 1))
                    s = tss[:, t % 2]
                    nc.gpsimd.tensor_tensor(s[:, 1:2], s[:, 0:1], eps[:], ALU.add).then_inc(S["x_mean"], 1)
                    pool.wait_ge(S["x_mean"], h * HT + (t + 1))
                    nc.gpsimd.tensor_tensor(s[:, 2:3], s[:, 1:2], minus_half[:], ALU.pow).then_inc(S["x_rstd"], 1)

            def split_piece(it, m):
                pool.wait_ge(S["w_high"], it * PIECES + (m + 1))
                nc.gpsimd.tensor_tensor(flat(wfm[1][:, m]), wraw[:, m % 3, :], flat(wfm[0][:, m]).bitcast(F32),
                                        ALU.subtract).then_inc(S["w_low"], 1)

            def group(it, following):
                n8 = pool.snap(it * HT)
                pool.wait_ge(S["group_ready"], it + 1)
                for c in range(HT):
                    pool.wait_ge(S["tok_ready"], n8 + (c + 1))
                    if c >= 2:
                        pool.wait_ge(S["y_gated"], n8 + (c - 1))
                    xv = tok[c % 2][:, 0:GW].rearrange("p (h d) -> p h d", h=HG)
                    by = lambda col: col.unsqueeze(2).broadcast_to([P, HG, PD])
                    nc.gpsimd.tensor_tensor(xdt[c % 2][:], xv, by(dtcol(DT, c)), ALU.mult)
                    nc.gpsimd.tensor_tensor(xde[c % 2][:], xv, by(dtcol(DTE, c)), ALU.mult)
                    nc.gpsimd.tensor_tensor(xd[c % 2][:], xv, by(pkg[:, 5 * HT, :]), ALU.mult
                                            ).then_inc(S["x_parts"], 1)
                    if c >= 1:
                        rstd(c - 1, n8)
                    if following and 1 <= c <= 4:
                        split_piece(pool.snap(it + 1), c - 1)
                rstd(HT - 1, n8)

            def rstd(c, n8):
                b = c % 2
                pool.wait_ge(S["y_squared"], n8 + (c + 1))
                nc.gpsimd.tensor_tensor(ssq[:, 2 + b:3 + b], ssq[:, b:b + 1], eps[:], ALU.add).then_inc(S["y_mean"], 1)
                pool.wait_ge(S["y_mean"], n8 + (c + 1))
                nc.gpsimd.tensor_tensor(ssq[:, 4 + b:5 + b], ssq[:, 2 + b:3 + b], minus_half[:], ALU.pow
                                        ).then_inc(S["y_rstd"], 1)

            with pool.Fori(0, HALVES) as h:
                half(h)
                for m in range(4):
                    split_piece(pool.snap(h * G), m)
                with pool.Fori(0, G - 1) as g:
                    group(pool.snap(h * G + g), True)
                group(pool.snap(h * G + (G - 1)), False)

        @block.scalar
        def _(act):
            act.wait_ge(S["vec_loaded"], 4 * 16)
            nc.scalar.activation(aneg[:], aneg[:], ACT.Exp).then_inc(S["aneg_ready"], 1)

            def piece_high(it, m):
                act.wait_ge(raw_loaded[m % 3], it * 32 + 16 * (m // 3 + 1))
                hi = flat(wfm[0][:, m]) if m < 4 else flat(wz[0][:, (m - 4) * 4:(m - 3) * 4])
                nc.scalar.copy(hi, wraw[:, m % 3, :]).then_inc(S["w_high"], 1)

            def half(h):
                def square(t):
                    act.wait_ge(x_loaded[t % 2], h * (HT // 2 * 16) + 16 * (t // 2 + 1))
                    if t >= 2:
                        act.wait_ge(S["x_scaled"], h * HT + (t - 1))
                    nc.scalar.activation(xsq[t % 2], xt[t % 2], ACT.Square, scale=D ** -0.5, accum_out=tss[:, t % 2, 0:1]
                                         ).then_inc(S["x_sq"], 1)

                square(0)
                for t in range(HT):
                    if t + 1 < HT:
                        square(t + 1)
                    act.wait_ge(S["x_turned"], h * HT + (t + 1))
                    if t >= 2:
                        act.wait_ge(S["h_ready"], h * HT + (t - 1))
                    for k in range(KD):
                        last = nc.scalar.activation(v[t % 2][:, k, :],
                                                    turned_x[t % 2][k // 4][:, (k % 4) * P:(k % 4 + 1) * P],
                                                    ACT.Identity, bias=K["mod"][:, k:k + 1], scale=K["a1"][:, k:k + 1])
                    last.then_inc(S["v_ready"], 1)
                    if t >= HT - 3:
                        piece_high(act.snap(h * G), t - (HT - 3))
                act.wait_ge(S["dt_low"], h + 1)
                nc.scalar.activation(T[2], T[1], ACT.Exp).then_inc(S["dt_exp"], 1)
                act.wait_ge(S["dt_exp"], h + 1)
                nc.scalar.activation(T[4], T[2], ACT.Ln, bias=1.0).then_inc(S["dt_ln"], 1)
                act.wait_ge(S["cum_sub"], h + 1)
                nc.scalar.activation(row(EAC), row(NAC), ACT.Exp, scale=-1.0)
                nc.scalar.activation(row(CDEC), psS[1][:, W8:2 * W8], ACT.Exp)
                nc.scalar.activation(T[5], T[6], ACT.Exp).then_inc(S["cum_exp"], 1)

            def block_out(n8, i):
                s, m, b = i // 4, i % 4, i % 2
                act.wait_ge(S["fm_done"], n8 + (i + 1))
                if i >= 2:
                    act.wait_ge(S["fm_ready"], n8 + (i - 1))
                if s:
                    act.wait_ge(S["fm_out"], n8 + (m + 1))
                nc.scalar.copy(raw[:, b, 0:3], histg[:, s, m, :])
                nc.scalar.activation(cv[:, b, :], psF[b][:], ACT.Identity, bias=vecg[:, TAPS, m:m + 1],
                                     scale=vecg[:, TAPS - 1, m:m + 1])
                nc.scalar.copy(raw[:, b, 3:3 + SUP], psF[b][:])
                nc.scalar.copy(histg[:, 1 - s, m, :], psF[b][:, SUP - 3:SUP]).then_inc(S["fm_out"], 1)

            def block_tanh(n8, i):
                act.wait_ge(S["conv_done"], n8 + (i + 1))
                nc.scalar.activation(fm[i // 4][:, i % 4, :], cv[:, i % 2, :], ACT.Tanh).then_inc(S["fm_tanh"], 1)

            def start(it):
                for m in range(3, PIECES):
                    piece_high(it, m)
                act.wait_ge(S["taps_ready"], it + 1)
                n8 = act.snap(it * HT)
                for m in range(4):
                    block_out(n8, m)
                    if m >= 1:
                        block_tanh(n8, m - 1)
                block_tanh(n8, 3)

            def group(it, following):
                n8 = act.snap(it * HT)
                next8 = act.snap(it * HT + HT)
                it1 = act.snap(it + 1)

                def z_out(c):
                    act.wait_ge(S["z_done"], n8 + (c + 1))
                    nc.scalar.activation(zs[:, c % CS, :], psZ[:, 0:GW], ACT.Tanh, scale=0.5).then_inc(S["z_tanh"], 1)

                def chunk_in(c):
                    act.wait_ge(S["turned"], n8 + (c + 1))
                    if c >= 2:
                        act.wait_ge(S["scan_done"], n8 + (c - 1))
                    nc.scalar.copy(tok[c % 2][:], psT[c % 2][:, 0:3 * P]).then_inc(S["tok_ready"], 1)
                    act.wait_ge(S["seg_done"], n8 + (c + 1))
                    for h in range(HG):
                        last = nc.scalar.activation(gm[c % 2][:, h, :], psS[c % 2][:, h * P:(h + 1) * P], ACT.Exp,
                                                    bias=pkg[:, NAC * HT + c, h:h + 1])
                    last.then_inc(S["decay_ready"], 1)

                def square(c):
                    act.wait_ge(S["y_gated"], n8 + (c + 1))
                    nc.scalar.activation(ysq[:], flat(yt[c % 2][:]), ACT.Square, scale=GW ** -0.5,
                                         accum_out=ssq[:, c % 2:c % 2 + 1]).then_inc(S["y_squared"], 1)

                for c in range(HT):
                    base, i = (n8, 4 + c) if c < CS else (next8, c - CS)
                    convolves = c < CS or following
                    if c == CS and following:
                        act.wait_ge(S["taps_ready"], it1 + 1)
                    chunk_in(c)
                    if c >= 1:
                        square(c - 1)
                    if convolves:
                        if CS <= c < CS + 2:
                            act.wait_ge(S["fm_ready"], next8 + (i - 1))
                        block_out(base, i)
                    z_out(c)
                    if following and 1 <= c <= 4:
                        piece_high(it1, c - 1)
                    if following and c == HT - 1:
                        piece_high(it1, 4)
                        piece_high(it1, 5)
                    if convolves:
                        block_tanh(base, i)
                square(HT - 1)

            with act.Fori(0, HALVES) as h:
                half(h)
                start(act.snap(h * G))
                with act.Fori(0, G - 1) as g:
                    group(act.snap(h * G + g), True)
                group(act.snap(h * G + (G - 1)), False)

        @block.tensor
        def _(pe):
            def split_products(out, lhs, rhs):
                K_ = len(lhs[0])
                for n, (i, j) in enumerate(((1, 0), (0, 1), (0, 0))):
                    for k in range(K_):
                        mm = nc.tensor.matmul(out, lhs[i][k], rhs[j][k], start=(n == 0 and k == 0),
                                              stop=(n == 2 and k == K_ - 1))
                return mm

            def half(h):
                def turn(t):
                    pe.wait_ge(S["x_scaled"], h * HT + (t + 1))
                    if t >= 2:
                        pe.wait_ge(S["v_ready"], h * HT + (t - 1))
                    for k in range(KD):
                        mm = nc.tensor.transpose(turned_x[t % 2][k // 4][:, (k % 4) * P:(k % 4 + 1) * P],
                                                 xt[t % 2][:, k * P:(k + 1) * P], ident[:])
                    mm.then_inc(S["x_turned"], 1)

                turn(0)
                for t in range(HT):
                    if t + 1 < HT:
                        turn(t + 1)
                    if t % CS == CS - 1:
                        s = t // CS
                        pe.wait_ge(S["h_ready"], h * HT + (t + 1))
                        if s:
                            pe.wait_ge(S["dt_copied"], h * (HT // CS) + s)
                        else:
                            pe.sem_inc(S["passed"], 1)
                        split_products(psZ[0:HEADS, :], [[wdts[i][:, k, :] for k in range(KD)] for i in range(2)],
                                       [[hT[i][:, k, s * SUP:(s + 1) * SUP] for k in range(KD)] for i in range(2)]
                                       ).then_inc(S["dt_cols"], 1)
                for t in range(HT):
                    if t % CS == 0:
                        pe.wait_ge(S["dt_copied"], h * (HT // CS) + (t // CS + 1))
                        pe.sem_inc(S["passed"], 1)
                    mm = nc.tensor.transpose(psY[:, t * HEADS:(t + 1) * HEADS],
                                             raw[0:HEADS, t // CS, (t % CS) * P:(t % CS + 1) * P],
                                             ident[0:HEADS, 0:HEADS])
                mm.then_inc(S["dt_done"], 1)
                it = pe.snap(h * G)
                n8 = pe.snap(it * HT)
                project(it, n8, 0, 0)
                pe.wait_ge(S["dt_ready"], h + 1)
                nc.tensor.matmul(psS[1][:, 0:W8], upper[:], T[7], start=True, stop=True)
                nc.tensor.matmul(psS[1][:, W8:2 * W8], ones[:], T[7], start=True, stop=True).then_inc(S["cum_done"], 1)
                for m in range(1, 4):
                    project(it, n8, 0, m)
                pe.wait_ge(S["half_ready"], h + 1)
                pe.sem_inc(S["passed"], 1)

            def project(it, n8, s, m):
                i = s * 4 + m
                if not s:
                    pe.wait_ge(S["w_low"], it * 4 + (m + 1))
                if i >= 2:
                    pe.wait_ge(S["fm_out"], n8 + (i - 1))
                split_products(psF[i % 2][:], [[wfm[j][:, m, k, :] for k in range(KD)] for j in range(2)],
                               [[hT[j][:, k, s * SUP:(s + 1) * SUP] for k in range(KD)] for j in range(2)]
                               ).then_inc(S["fm_done"], 1)

            def group(it, following):
                n8 = pe.snap(it * HT)
                next8 = pe.snap(it * HT + HT)
                it1 = pe.snap(it + 1)

                def project_z(c):
                    if c == 0:
                        pe.wait_ge(S["z_low"], it * 2 + 2)
                    pe.wait_ge(S["z_ready"], n8 + c)
                    split_products(psZ[:, 0:GW], [[hT[j][:, k, c * P:(c + 1) * P] for k in range(KD)] for j in range(2)],
                                   [[wz[j][:, k, :] for k in range(KD)] for j in range(2)]).then_inc(S["z_done"], 1)

                def chunk_in(c):
                    s, o = c // CS, (c % CS) * P
                    if c % CS == 0:
                        pe.wait_ge(S["fm_ready"], n8 + (s + 1) * 4)
                    if c >= 2:
                        pe.wait_ge(S["y_read"], n8 + (c - 1))
                    elif c == 0:
                        pe.wait_ge(S["y_read"], n8)
                    b = c % 2
                    for m in range(3):
                        nc.tensor.transpose(psT[b][:, m * P:(m + 1) * P], fm[s][:, m, o:o + P], ident[:])
                    nc.tensor.matmul(psT[b][:, 3 * P:], fm[s][:, 2, o:o + P], fm[s][:, 3, o:o + P],
                                     start=True, stop=True).then_inc(S["turned"], 1)
                    if c == 0:
                        pe.wait_ge(S["group_ready"], it + 1)
                    for h in range(HG):
                        for j in (1, 0):
                            nc.tensor.matmul(psS[b][:, h * P:(h + 1) * P], dag[j][:, c, h:h + 1].broadcast_to([P, P]),
                                             upr[:], start=(h == 0 and j == 1), stop=False, skip_group_check=True)
                    nc.tensor.matmul(psS[b][:].rearrange("p (h i) -> p h i", h=HG), identb[:],
                                     maskb[:].unsqueeze(1).broadcast_to([P, HG, P]), start=False, stop=True,
                                     skip_group_check=True).then_inc(S["seg_done"], 1)

                def chunk_out(c):
                    s, o, b = c // CS, (c % CS) * P, c % 2
                    pe.wait_ge(S["gm_ready"], n8 + (c + 1))
                    pe.wait_ge(S["x_parts"], n8 + (c + 1))
                    pe.wait_ge(S["state_ready"], n8 + (c + 1))
                    if c >= 1:
                        pe.wait_ge(S["y_read"], n8 + c)
                    nc.tensor.matmul(psY[:, GW:2 * GW], fm[s][:, 3, o:o + P], flat(state[:]), start=True, stop=True)
                    nc.tensor.matmul(psS[b][:, 0:GW], tok[b][:, 2 * P:3 * P], flat(xde[b][:]), start=True, stop=True)
                    for h in range(HG):
                        mm = nc.tensor.matmul(psY[:, h * PD:(h + 1) * PD], gm[b][:, h, :], xdt[b][:, h, :],
                                              start=True, stop=True)
                    mm.then_inc(S["scan_done"], 1)

                for c in range(HT):
                    if c == 0:
                        project(it, n8, 1, 0)
                    chunk_in(c)
                    if 1 <= c < CS:
                        project(it, n8, 1, c)
                    elif c >= CS and following:
                        if c < CS + 2:
                            pe.wait_ge(S["fm_out"], next8 + (c - CS - 1))
                        project(it1, next8, 0, c - CS)
                    project_z(c)
                    chunk_out(c)

            pe.wait_ge(S["vec_loaded"], 4 * 16)
            with pe.Fori(0, HALVES) as h:
                half(h)
                with pe.Fori(0, G - 1) as g:
                    group(pe.snap(h * G + g), True)
                group(pe.snap(h * G + (G - 1)), False)

        @block.vector
        def _(dve):
            first = Steps(dve, S["w_order"])
            for q in y_stored:
                dve.sem_inc(q, 16)
            dve.wait_ge(S["vec_loaded"], 4 * 16)
            first.add(nc.vector.tensor_copy(wdts[0][:], wdt[:]))
            first.add(nc.vector.tensor_copy(upr[:], upper[:]))
            first.settle()
            first.add(nc.vector.tensor_tensor(wdts[1][:], wdt[:], wdts[0][:].bitcast(F32), ALU.subtract))
            first.settle()
            dve.wait_ge(S["aneg_ready"], 1)
            first.add(nc.vector.tensor_scalar(aneg[:], aneg[:], -1.0, None, ALU.mult))
            first.settle()
            dve.wait_ge(S["zeroed"], 5)
            nc.vector.memset(ssq[:], 0.0).then_inc(S["wdt_ready"], 1)

            def half(h, own):
                def scale(t):
                    dve.wait_ge(S["x_rstd"], h * HT + (t + 1))
                    nc.vector.tensor_scalar(xt[t % 2], xt[t % 2], tss[:, t % 2, 2:3], None, ALU.mult
                                            ).then_inc(S["x_scaled"], 1)

                scale(0)
                for t in range(HT):
                    if t + 1 < HT:
                        scale(t + 1)
                    dve.wait_ge(S["v_ready"], h * HT + (t + 1))
                    o = slice(t * P, (t + 1) * P)
                    nc.vector.tensor_copy(hT[0][:, :, o], v[t % 2]).then_inc(S["v_high"], 1)
                    dve.wait_ge(S["v_high"], h * HT + (t + 1))
                    nc.vector.tensor_tensor(hT[1][:, :, o], v[t % 2], hT[0][:, :, o].bitcast(F32), ALU.subtract
                                            ).then_inc(S["h_ready"], 1)
                    if t in (CS + 1, HT - 1):
                        s = t // (HT - 1)
                        dve.wait_ge(S["dt_cols"], h * (HT // CS) + (s + 1))
                        nc.vector.tensor_copy(raw[0:HEADS, s, 0:SUP], psZ[0:HEADS, :]).then_inc(S["dt_copied"], 1)
                per_tile = lambda a: a.unsqueeze(1).broadcast_to([P, HT, HEADS])
                shaped = lambda a: a.rearrange("p (c h) -> p c h", c=HT)
                dve.wait_ge(S["dt_done"], h + 1)
                own.add(nc.vector.tensor_tensor(shaped(T[0]), shaped(psY[:, 0:W8]), per_tile(dbias[:]), ALU.add))
                own.settle()
                nc.vector.scalar_tensor_tensor(T[1], T[0], -1.0, T[0], ALU.mult, ALU.min).then_inc(S["dt_low"], 1)
                own.add(nc.vector.tensor_scalar(T[3], T[0], 0.0, None, ALU.max))
                dve.wait_ge(S["dt_ln"], h + 1)
                own.add(nc.vector.tensor_scalar(T[5], T[2], 1.0, None, ALU.add))
                own.settle()
                own.add(nc.vector.scalar_tensor_tensor(T[6], T[5], -1.0, T[2], ALU.add, ALU.subtract))
                own.add(nc.vector.reciprocal(T[7], T[5]))
                own.add(nc.vector.tensor_tensor(T[4], T[4], T[3], ALU.add))
                own.settle()
                own.add(nc.vector.tensor_tensor(T[6], T[6], T[7], ALU.mult))
                own.settle()
                own.add(nc.vector.tensor_tensor(row(DT), T[4], T[6], ALU.subtract))
                own.settle()
                nc.vector.tensor_tensor(shaped(T[7]), shaped(row(DT)), per_tile(aneg[:]), ALU.mult
                                        ).then_inc(S["dt_ready"], 1)
                dve.wait_ge(S["dt_ready"], h + 1)
                own.add(nc.vector.tensor_copy(flat(da[0][:]), T[7]))
                own.settle()
                own.add(nc.vector.tensor_tensor(flat(da[1][:]), T[7], flat(da[0][:]).bitcast(F32), ALU.subtract))
                dve.wait_ge(S["cum_done"], h + 1)
                own.add(nc.vector.tensor_scalar(row(NAC), psS[1][:, 0:W8], -1.0, None, ALU.mult))
                own.settle()
                nc.vector.tensor_tensor(T[6], psS[1][:, W8:2 * W8], row(NAC), ALU.add).then_inc(S["cum_sub"], 1)
                dve.wait_ge(S["cum_exp"], h + 1)
                nc.vector.tensor_tensor(row(DTE), row(DT), T[5], ALU.mult).then_inc(S["half_ready"], 1)
                dve.wait_ge(S["half_ready"], h + 1)
                dve.sem_inc(S["passed"], 1)

            def load_taps(g, own):
                own.add(nc.vector.tensor_copy(vecg[:, :, 0:2], K["conv"][:, :, bass.ds(g * 2, 2)]))
                own.add(nc.vector.tensor_copy(vecg[:, :, 2:3], K["conv"][:, :, bass.ds(g + 2 * G, 1)]))
                own.add(nc.vector.tensor_copy(vecg[:, :, 3:4], K["conv"][:, :, bass.ds(g + 3 * G, 1)]))
                own.settle()
                nc.vector.tensor_copy(flat(histg[:, 0]).unsqueeze(2), hist[:, :, bass.ds(g, 1)]).then_inc(S["taps_ready"], 1)

            def load_group(g, own):
                g4 = dve.snap(g * HG)
                own.add(nc.vector.tensor_copy(pkg[:], pk[:, :, bass.ds(g4, HG)]))
                for i in range(2):
                    own.add(nc.vector.tensor_copy(dag[i][:], da[i][:, :, bass.ds(g4, HG)]))
                own.settle()
                nc.vector.tensor_copy(flat(state[:]), states[:, bass.ds(g, 1), :].rearrange("p o n -> p (o n)")
                                      ).then_inc(S["state_ready"], 1)
                dve.sem_inc(S["group_ready"], 1)

            def conv(n8, i, own):
                m, b = i % 4, i % 2
                dve.wait_ge(S["fm_out"], n8 + (i + 1))
                for tap in range(TAPS - 1):
                    ins = nc.vector.scalar_tensor_tensor(cv[:, b, :], raw[:, b, tap:tap + SUP], vecg[:, tap, m:m + 1],
                                                         cv[:, b, :], ALU.mult, ALU.add)
                    if tap < TAPS - 2:
                        own.add(ins)
                        own.settle()
                ins.then_inc(S["conv_done"], 1)

            def block_silu(n8, i):
                dve.wait_ge(S["fm_tanh"], n8 + (i + 1))
                f = fm[i // 4][:, i % 4, :]
                nc.vector.scalar_tensor_tensor(f, f, 1.0, cv[:, i % 2, :], ALU.add, ALU.mult).then_inc(S["fm_ready"], 1)

            def z_low(it, m):
                dve.wait_ge(S["w_high"], it * PIECES + (m + 1))
                k4 = slice((m - 4) * 4, (m - 3) * 4)
                nc.vector.tensor_tensor(flat(wz[1][:, k4]), wraw[:, m % 3, :], flat(wz[0][:, k4]).bitcast(F32),
                                        ALU.subtract).then_inc(S["z_low"], 1)

            def start(it, own):
                dve.wait_ge(S["nw_loaded"], 16)
                load_taps(0, own)
                load_group(0, own)
                z_low(it, 4)
                z_low(it, 5)
                n8 = dve.snap(it * HT)
                for m in range(4):
                    conv(n8, m, own)
                    if m >= 1:
                        block_silu(n8, m - 1)
                block_silu(n8, 3)

            def group(it, g, own, following):
                n8 = dve.snap(it * HT)
                next8 = dve.snap(it * HT + HT)
                it1 = dve.snap(it + 1)
                g1 = dve.snap(g + 1) if following else None
                dve.wait_ge(S["state_ready"], n8 + 1)

                def decays(c):
                    dve.wait_ge(S["decay_ready"], n8 + (c + 1))
                    cb = psT[c % 2][:, 3 * P:].unsqueeze(1).broadcast_to([P, HG, P])
                    nc.vector.tensor_tensor(gm[c % 2][:], gm[c % 2][:], cb, ALU.mult).then_inc(S["gm_ready"], 1)

                def gate(c):
                    b = c % 2
                    by = lambda col: col.unsqueeze(2).broadcast_to([P, HG, PD])
                    halves = lambda a: a.rearrange("p (h d) -> p h d", h=HG)
                    dve.wait_ge(S["scan_done"], n8 + (c + 1))
                    own.add(nc.vector.tensor_tensor(state[:], state[:], by(dtcol(CDEC, c)), ALU.mult))
                    own.add(nc.vector.tensor_tensor(yt[b][:], halves(psY[:, GW:2 * GW]), by(dtcol(EAC, c)), ALU.mult))
                    own.settle()
                    ins = nc.vector.tensor_tensor(state[:], state[:], halves(psS[b][:, 0:GW]), ALU.add)
                    if c < HT - 1:
                        ins.then_inc(S["state_ready"], 1)
                    else:
                        own.add(ins)
                    nc.vector.tensor_tensor(yt[b][:], yt[b][:], halves(psY[:, 0:GW]), ALU.add).then_inc(S["y_read"], 1)
                    dve.wait_ge(S["y_read"], n8 + (c + 1))
                    own.add(nc.vector.tensor_tensor(yt[b][:], yt[b][:], xd[b][:], ALU.add))
                    own.settle()
                    dve.wait_ge(S["z_ready"], n8 + (c + 1))
                    nc.vector.scalar_tensor_tensor(flat(yt[b][:]), flat(yt[b][:]), 0.5, zs[:, c % CS, :], ALU.mult, ALU.mult
                                                   ).then_inc(S["y_gated"], 1)

                def z_silu(c):
                    dve.wait_ge(S["z_tanh"], n8 + (c + 1))
                    z = zs[:, c % CS, :]
                    nc.vector.scalar_tensor_tensor(z, z, 1.0, psZ[:, 0:GW], ALU.add, ALU.mult).then_inc(S["z_ready"], 1)

                def norm(c):
                    b = c % 2
                    dve.wait_ge(S["y_rstd"], n8 + (c + 1))
                    dve.wait_ge(y_stored[b], stored + 16 * (c // 2 + 1))
                    nc.vector.scalar_tensor_tensor(yo[b][:], flat(yt[b][:]), ssq[:, 4 + b:5 + b], nw[:, bass.ds(g * GW, GW)],
                                                   ALU.mult, ALU.mult).then_inc(S["y_ready"], 1)

                stored = dve.snap(it * (HT // 2 * 16))
                for c in range(HT):
                    base, i = (n8, 4 + c) if c < CS else (next8, c - CS)
                    convolves = c < CS or following
                    decays(c)
                    if c >= 1:
                        norm(c - 1)
                    if convolves:
                        conv(base, i, own)
                    z_silu(c)
                    if c == CS - 1:
                        dve.wait_ge(S["conv_done"], n8 + HT)
                        own.add(nc.vector.tensor_copy(hist[:, :, bass.ds(g, 1)], flat(histg[:, 0]).unsqueeze(2)))
                        own.settle()
                        if following:
                            load_taps(g1, own)
                    if convolves:
                        block_silu(base, i)
                    if following and c == HT - 1:
                        z_low(it1, 4)
                        z_low(it1, 5)
                    gate(c)
                own.settle()
                own.add(nc.vector.tensor_copy(states[:, bass.ds(g, 1), :].rearrange("p o n -> p (o n)"), flat(state[:])))
                own.settle()
                if following:
                    dve.wait_ge(S["y_gated"], n8 + HT)
                    load_group(g1, own)
                norm(HT - 1)

            HALF_STEPS, START_STEPS, LOOP_STEPS, LAST_STEPS = 11, 14, 49, 35
            with dve.Fori(0, HALVES) as h:
                own = Steps(dve, S["half_steps"], dve.snap(h * HALF_STEPS))
                half(h, own)
                assert own.n == HALF_STEPS, own.n
                own = Steps(dve, S["start_steps"], dve.snap(h * START_STEPS))
                start(dve.snap(h * G), own)
                assert own.n == START_STEPS, own.n
                with dve.Fori(0, G - 1) as g:
                    own = Steps(dve, S["loop_steps"], dve.snap((h * (G - 1) + g) * LOOP_STEPS))
                    group(dve.snap(h * G + g), g, own, True)
                    assert own.n == LOOP_STEPS, own.n
                own = Steps(dve, S["last_steps"], dve.snap(h * LAST_STEPS))
                group(dve.snap(h * G + (G - 1)), G - 1, own, False)
                assert own.n == LAST_STEPS, own.n


def out_phase(nc, x, out_w, group_w, group_b, expert_w, expert_b, ydram, x1dram, xs, K):
    Q = 4
    NR = GROUPS + EXPERTS
    SLOTS = 4
    with ExitStack() as ctx:
        sb = lambda n, s, d=F32: ctx.enter_context(nc.sbuf_tensor(n, s, d))
        psum = lambda n: ctx.enter_context(nc.psum_tensor(n, [P, 512], F32))
        sem = semaphores(nc, ctx, "out_")
        ident, mod, a2 = K["ident"], K["mod"], K["a2"]
        wo = [sb(f"wo{i}", [P, KI, D], F32R) for i in range(2)]
        wraw = sb("wo_raw", [P, SLOTS, D])
        y4 = sb("y4", [P, Q, 512])
        yT = [sb(f"yT{i}", [P, Q, 512], F32R) for i in range(2)]
        rows = {n: sb("row_" + n, [P, D]) for n in ("gt1", "a2", "s2")}
        xr = sb("xr", [P, D])
        tmp = sb("tmp", [P, 2, 512])
        hf = sb("hf", [P, D])
        hfT = sb("hfT", [P, KD, P])
        wr = sb("wr", [P, KD, NR])
        rb = sb("rb", [P, NR])
        st = sb("st", [P, 4])
        minus_half, eps = sb("o_minus_half", [P, 1]), sb("o_eps", [P, 1])
        lg, el = sb("lg", [P, 8]), sb("el", [P, EXPERTS])
        gm8, em8 = sb("gm8", [P, 8]), sb("em8", [P, 8])
        gi8, ei8 = sb("gi8", [P, 8], U32), sb("ei8", [P, 8], U32)
        gif, eif, ngm = sb("gif", [P, 1]), sb("eif", [P, 2]), sb("ngm", [P, 1])
        ge, gsum, dif, ex = sb("ge", [P, 4]), sb("gsum", [P, 1]), sb("dif", [P, 1]), sb("ex", [P, 1])
        den, rec = sb("den", [P, 1]), sb("rec", [P, 1])
        ohg, pen = sb("ohg", [P, EXPERTS]), sb("pen", [P, EXPERTS])
        oh = [sb(f"oh{i}", [P, EXPERTS]) for i in range(2)]
        both = sb("both", [P, EXPERTS], BF16)
        pos, base, scr = sb("pos", [P, EXPERTS]), sb("base", [P, EXPERTS]), sb("scr", [P, 2, EXPERTS])
        df, dcur = sb("df", [P, 2]), sb("dcur", [P, 2], U32)
        ii = sb("ii", [P, 3, EXPERTS], I32)
        ff = sb("ff", [P, 3, EXPERTS])
        dest, gates = K["dest"], K["gates"]
        acc = [psum("acc0"), psum("acc1")]
        psT = [psum("oT0"), psum("oT1")]
        psH = [psum("oH0"), psum("oH1")]
        psR, psC = psum("psR"), psum("psC")
        NAMES = ("vec_loaded", "high", "low", "y_turned", "y_high", "y_low", "acc_done", "acc_read",
                 "half_added", "squared", "mean", "rstd", "hf_scaled", "hf_ready", "hf_turned", "hf_copied",
                 "logits", "gneg", "gexp", "edif", "eexp", "picked", "ranked", "placed", "scattered",
                 "x_loaded", "x1_stored", "vsteps", "setup", "consts", "rows_done", "rows_copied", "passed",
                 "table_steps", "y_order")
        S = {n: sem(n) for n in NAMES}
        raw_loaded = [sem(f"raw_loaded{i}") for i in range(SLOTS)]
        y_loaded = [sem(f"y_loaded{i}") for i in range(Q)]
        block = ctx.enter_context(nc.Block())

        @block.sync
        def _(sp):
            with nc.allow_non_contiguous_dma(reason="the router's weights are narrow"):
                sp.dma_start(wr[:, :, 0:GROUPS], group_w[0].rearrange("(k p) n -> p k n", p=P)).then_inc(S["vec_loaded"], 16)
                sp.dma_start(wr[:, :, GROUPS:NR], expert_w[0].rearrange("(k p) n -> p k n", p=P)).then_inc(S["vec_loaded"], 16)
            sp.dma_start(rb[:, 0:GROUPS], group_b.broadcast_to([P, GROUPS])).then_inc(S["vec_loaded"], 16)
            sp.dma_start(rb[:, GROUPS:NR], expert_b.broadcast_to([P, EXPERTS])).then_inc(S["vec_loaded"], 16)

            def load_y(t):
                for q in range(Q):
                    if not isinstance(t, int) or t:
                        sp.wait_ge(S["y_turned"], t * Q + (q - Q + 1))
                    sp.dma_start(y4[:, q, :], ydram[bass.ds(t * P, P), q * 512:(q + 1) * 512]
                                 ).then_inc(y_loaded[q], 16)

            def load_x(t):
                sp.dma_start(xr[:], x[0, bass.ds(t * P, P), :]).then_inc(S["x_loaded"], 16)

            def store_x1(t):
                sp.wait_ge(S["half_added"], t * 2 + 2)
                sp.dma_start(x1dram[bass.ds(t * P, P), :], xr[:]).then_inc(S["x1_stored"], 16)
                sp.wait_ge(S["x1_stored"], t * 16 + 16)
                sp.wait_ge(S["hf_scaled"], t + 1)

            load_y(0)
            load_x(0)
            for k in range(KI):
                if k >= SLOTS:
                    sp.wait_ge(S["low"], k - SLOTS + 1)
                sp.dma_start(wraw[:, k % SLOTS, :], out_w[0, k * P:(k + 1) * P, :]).then_inc(raw_loaded[k % SLOTS], 16)
            with sp.Fori(1, TILES) as t:
                load_y(t)
                store_x1(t - 1)
                load_x(t)
            store_x1(TILES - 1)

        @block.gpsimd
        def _(pool):
            own = Steps(pool, S["setup"])
            own.add(nc.gpsimd.memset(minus_half[:], -0.5))
            own.add(nc.gpsimd.memset(eps[:], EPS))
            own.add(nc.gpsimd.memset(lg[:, GROUPS:8], -BIG))
            own.add(nc.gpsimd.iota(ii[:, 0, :], pattern=[[1, EXPERTS]], base=0, channel_multiplier=0))
            own.add(nc.gpsimd.iota(ii[:, 1, :], pattern=[[1, GROUPS], [0, EPG]], base=0, channel_multiplier=0))
            own.add(nc.gpsimd.iota(ii[:, 2, :], pattern=[[REGION, EXPERTS]], base=0, channel_multiplier=0))
            own.settle()
            nc.gpsimd.tensor_copy(ff[:], ii[:]).then_inc(S["consts"], 1)

            def add_half(t, n):
                if n == 0:
                    pool.wait_ge(S["x_loaded"], t * 16 + 16)
                pool.wait_ge(S["acc_read"], t * 2 + (n + 1))
                h = slice(n * 512, (n + 1) * 512)
                nc.gpsimd.tensor_tensor(xr[:, h], xr[:, h], tmp[:, n, :], ALU.add).then_inc(S["half_added"], 1)

            def norm(t):
                pool.wait_ge(S["squared"], t + 1)
                nc.gpsimd.tensor_tensor(st[:, 1:2], st[:, 0:1], eps[:], ALU.add).then_inc(S["mean"], 1)
                pool.wait_ge(S["mean"], t + 1)
                nc.gpsimd.tensor_tensor(st[:, 2:3], st[:, 1:2], minus_half[:], ALU.pow).then_inc(S["rstd"], 1)
                pool.wait_ge(S["hf_scaled"], t + 1)
                nc.gpsimd.tensor_tensor(hf[:], hf[:], rows["s2"][:], ALU.add).then_inc(S["hf_ready"], 1)

            def scatter(t):
                pool.wait_ge(S["placed"], t + 1)
                pool.sem_inc(S["passed"], 1)
                for j in range(2):
                    nc.gpsimd.indirect_dma_start(xs, bass.IndirectOffsetOnAxis(ap=dcur[:, j:j + 1], axis=0), hf[:], None
                                                 ).then_inc(S["scattered"], 16)

            def tile(t, n):
                if n >= 2:
                    scatter(t - 2)
                if n >= 1:
                    add_half(t - 1, 1)
                    norm(t - 1)
                add_half(t, 0)

            tile(0, 0)
            tile(1, 1)
            with pool.Fori(2, TILES) as t:
                tile(t, 2)
            scatter(TILES - 2)
            add_half(TILES - 1, 1)
            norm(TILES - 1)
            scatter(TILES - 1)
            pool.wait_ge(S["scattered"], TILES * 32)

        @block.scalar
        def _(act):
            for k in range(KI):
                act.wait_ge(raw_loaded[k % SLOTS], 16 * (k // SLOTS + 1))
                nc.scalar.copy(wo[0][:, k, :], wraw[:, k % SLOTS, :]).then_inc(S["high"], 1)

            def high(t, q):
                act.wait_ge(S["y_turned"], t * Q + (q + 1))
                nc.scalar.copy(yT[0][:, q, :], psT[q % 2][:]).then_inc(S["y_high"], 1)

            def square(t):
                act.wait_ge(S["half_added"], t * 2 + 2)
                nc.scalar.activation(hf[:], xr[:], ACT.Square, scale=D ** -0.5, accum_out=st[:, 0:1]
                                     ).then_inc(S["squared"], 1)

            def copy_hf(t):
                act.wait_ge(S["hf_turned"], t + 1)
                for i in range(2):
                    last = nc.scalar.copy(hfT[:, i * 4:(i + 1) * 4, :].rearrange("p a b -> p (a b)"), psH[i][:])
                last.then_inc(S["hf_copied"], 1)

            def soft(t):
                act.wait_ge(S["gneg"], t + 1)
                nc.scalar.activation(ge[:], lg[:, 0:GROUPS], ACT.Exp, bias=ngm[:], accum_out=gsum[:]).then_inc(S["gexp"], 1)
                act.wait_ge(S["edif"], t + 1)
                nc.scalar.activation(ex[:], dif[:], ACT.Exp).then_inc(S["eexp"], 1)

            def tile(t, n):
                for q in range(Q):
                    high(t, q)
                if n >= 1:
                    if n >= 2:
                        act.wait_ge(S["scattered"], t * 32 - 32)
                    square(t - 1)
                    copy_hf(t - 1)
                    soft(t - 1)

            tile(0, 0)
            tile(1, 1)
            with act.Fori(2, TILES) as t:
                tile(t, 2)
            act.wait_ge(S["scattered"], (TILES - 1) * 32)
            square(TILES - 1)
            copy_hf(TILES - 1)
            soft(TILES - 1)

        @block.tensor
        def _(pe):
            for r, (src, off) in enumerate(((mod, 2 * KD), (a2, 0), (mod, 3 * KD))):
                for i in range(2):
                    if r:
                        pe.wait_ge(S["rows_copied"], 2 * r - 1 + i)
                    for k in range(4):
                        o = off + 4 * i + k
                        mm = nc.tensor.matmul(acc[i][:, k * P:(k + 1) * P], src[:, o:o + 1].broadcast_to([P, P]),
                                              ident[:], start=True, stop=True)
                    mm.then_inc(S["rows_done"], 1)

            def turn(t, q):
                pe.wait_ge(y_loaded[q], t * 16 + 16)
                if q >= 2:
                    pe.wait_ge(S["y_low"], t * Q + (q - 1))
                for k in range(4):
                    mm = nc.tensor.transpose(psT[q % 2][:, k * P:(k + 1) * P], y4[:, q, k * P:(k + 1) * P], ident[:])
                mm.then_inc(S["y_turned"], 1)

            def block_products(n, q, k):
                o = (k % 4) * P
                for i, j in ((1, 0), (0, 1), (0, 0)):
                    mm = nc.tensor.matmul(acc[n][:], yT[i][:, q, o:o + P], wo[j][:, k, n * 512:(n + 1) * 512],
                                          start=(k == 0 and i == 1), stop=(k == KI - 1 and i == 0 and j == 0))
                if k == KI - 1:
                    mm.then_inc(S["acc_done"], 1)

            def product(t, n, q):
                if n == 0:
                    pe.wait_ge(S["y_low"], t * Q + (q + 1))
                for k in range(4 * q, 4 * q + 4):
                    block_products(n, q, k)

            def first_tile():
                for k in range(KI):
                    if k % 4 == 0:
                        pe.wait_ge(S["y_low"], k // 4 + 1)
                    pe.wait_ge(S["low"], k + 1)
                    for n in range(2):
                        block_products(n, k // 4, k)

            def route_a(t):
                pe.wait_ge(S["hf_ready"], t + 1)
                for k in range(KD):
                    mm = nc.tensor.transpose(psH[k // 4][:, (k % 4) * P:(k % 4 + 1) * P], hf[:, k * P:(k + 1) * P], ident[:])
                mm.then_inc(S["hf_turned"], 1)

            def route_b(t):
                pe.wait_ge(S["hf_copied"], t + 1)
                for k in range(KD):
                    mm = nc.tensor.matmul(psR[:, 0:NR], hfT[:, k, :], wr[:, k, :], start=(k == 0), stop=(k == KD - 1))
                mm.then_inc(S["logits"], 1)

            def route_c(t):
                pe.wait_ge(S["picked"], t + 1)
                nc.tensor.matmul(psC[:, 0:EXPERTS], K["strictb"][:], both[:], start=True, stop=True)
                nc.tensor.matmul(psC[:, EXPERTS:2 * EXPERTS], K["onesb"][:], both[:], start=True, stop=True
                                 ).then_inc(S["ranked"], 1)

            def tile(t, n):
                for q in range(Q):
                    if n >= 2:
                        if q == 0:
                            pe.wait_ge(S["acc_read"], t * 2 - 2)
                        product(t - 1, 1, q)
                    turn(t, q)
                    if n >= 2 and q == 0:
                        route_b(t - 2)
                    if n >= 2 and q == 2:
                        route_c(t - 2)
                if n >= 1:
                    pe.wait_ge(S["acc_read"], t * 2 - 1)
                else:
                    pe.wait_ge(S["rows_copied"], 6)
                if n == 0:
                    first_tile()
                else:
                    for q in range(Q):
                        product(t, 0, q)
                    route_a(t - 1)

            pe.wait_ge(S["vec_loaded"], 4 * 16)
            tile(0, 0)
            tile(1, 1)
            with pe.Fori(2, TILES) as t:
                tile(t, 2)
            for q in range(Q):
                if q == 0:
                    pe.wait_ge(S["acc_read"], TILES * 2 - 2)
                product(TILES - 1, 1, q)
                if q == 0:
                    route_b(TILES - 2)
            route_c(TILES - 2)
            route_a(TILES - 1)
            route_b(TILES - 1)
            route_c(TILES - 1)

        @block.vector
        def _(dve):
            for r, name in enumerate(("gt1", "a2", "s2")):
                for i in range(2):
                    dve.wait_ge(S["rows_done"], 2 * r + i + 1)
                    nc.vector.tensor_copy(rows[name][:, i * 512:(i + 1) * 512], acc[i][:]).then_inc(S["rows_copied"], 1)
            for k in range(KI):
                dve.wait_ge(S["high"], k + 1)
                nc.vector.tensor_tensor(wo[1][:, k, :], wraw[:, k % SLOTS, :], wo[0][:, k, :].bitcast(F32), ALU.subtract
                                        ).then_inc(S["low"], 1)
            dve.wait_ge(S["consts"], 1)
            nc.vector.tensor_copy(base[:], ff[:, 2, :]).then_inc(S["y_order"], 1)
            dve.wait_ge(S["y_order"], 1)

            def low(t, q):
                dve.wait_ge(S["y_high"], t * Q + (q + 1))
                nc.vector.tensor_tensor(yT[1][:, q, :], psT[q % 2][:], yT[0][:, q, :].bitcast(F32), ALU.subtract
                                        ).then_inc(S["y_low"], 1)

            def gated(t, n):
                dve.wait_ge(S["acc_done"], t * 2 + (n + 1))
                nc.vector.tensor_tensor(tmp[:, n, :], acc[n][:], rows["gt1"][:, n * 512:(n + 1) * 512], ALU.mult
                                        ).then_inc(S["acc_read"], 1)

            def scaled(t):
                dve.wait_ge(S["rstd"], t + 1)
                nc.vector.scalar_tensor_tensor(hf[:], xr[:], st[:, 2:3], rows["a2"][:], ALU.mult, ALU.mult
                                               ).then_inc(S["hf_scaled"], 1)

            def pick(t, own):
                step = lambda ins: (own.add(ins), own.settle())
                dve.wait_ge(S["logits"], t + 1)
                own.add(nc.vector.tensor_tensor(lg[:, 0:GROUPS], psR[:, 0:GROUPS], rb[:, 0:GROUPS], ALU.add))
                own.add(nc.vector.tensor_tensor(el[:], psR[:, GROUPS:NR], rb[:, GROUPS:NR], ALU.add))
                own.settle()
                dve.sem_inc(S["passed"], 1)
                step(nc.vector.max(gm8[:], lg[:]))
                nc.vector.tensor_scalar(ngm[:], gm8[:, 0:1], -1.0, None, ALU.mult).then_inc(S["gneg"], 1)
                own.add(nc.vector.max_index(gi8[:], gm8[:], lg[:]))
                own.settle()
                step(nc.vector.tensor_copy(gif[:], gi8[:, 0:1]))
                step(nc.vector.tensor_scalar(ohg[:], ff[:, 1, :], gif[:], None, ALU.is_equal))
                own.add(nc.vector.tensor_scalar(pen[:], ohg[:], -1.0, BIG, ALU.add, ALU.mult))
                step(nc.vector.tensor_tensor(el[:], el[:], ohg[:], ALU.mult))
                step(nc.vector.tensor_tensor(el[:], el[:], pen[:], ALU.add))
                dve.sem_inc(S["passed"], 1)
                step(nc.vector.max(em8[:], el[:]))
                nc.vector.tensor_tensor(dif[:], em8[:, 1:2], em8[:, 0:1], ALU.subtract).then_inc(S["edif"], 1)
                own.add(nc.vector.max_index(ei8[:], em8[:], el[:]))
                own.settle()
                step(nc.vector.tensor_copy(eif[:], ei8[:, 0:2]))
                for j in range(2):
                    own.add(nc.vector.tensor_scalar(oh[j][:], ff[:, 0, :], eif[:, j:j + 1], None, ALU.is_equal))
                own.settle()
                nc.vector.tensor_tensor(both[:], oh[0][:], oh[1][:], ALU.add).then_inc(S["picked"], 1)
                dve.wait_ge(S["eexp"], t + 1)
                step(nc.vector.tensor_scalar(den[:], ex[:], 1.0, None, ALU.add))
                step(nc.vector.tensor_tensor(den[:], den[:], gsum[:], ALU.mult))
                step(nc.vector.reciprocal(rec[:], den[:]))
                dve.sem_inc(S["passed"], 1)
                gt = lambda j: gates[:, bass.ds(t * 2 + j, 1)]
                own.add(nc.vector.tensor_copy(gt(0), rec[:]))
                own.add(nc.vector.tensor_tensor(gt(1), rec[:], ex[:], ALU.mult))
                own.settle()

            def place(t, own):
                step = lambda ins: (own.add(ins), own.settle())
                dve.wait_ge(S["ranked"], t + 1)
                step(nc.vector.tensor_tensor(pos[:], base[:], psC[:, 0:EXPERTS], ALU.add))
                for j in range(2):
                    own.add(nc.vector.tensor_tensor_reduce(out=scr[:, j, :], in0=oh[j][:], in1=pos[:], scale=1.0,
                                                           scalar=0.0, op0=ALU.mult, op1=ALU.add,
                                                           accum_out=df[:, j:j + 1]))
                own.add(nc.vector.tensor_tensor(base[:], base[:], psC[:, EXPERTS:2 * EXPERTS], ALU.add))
                own.settle()
                if not isinstance(t, int) or t:
                    dve.wait_ge(S["scattered"], t * 32)
                nc.vector.tensor_copy(dcur[:], df[:]).then_inc(S["placed"], 1)
                own.add(nc.vector.tensor_copy(dest[:, bass.ds(t * 2, 2)], df[:]))
                own.settle()

            def tile(t, n, own):
                for q in range(Q):
                    low(t, q)
                    if q == 2 and n >= 2:
                        place(t - 2, own)
                if n >= 1:
                    gated(t - 1, 1)
                    scaled(t - 1)
                gated(t, 0)
                if n >= 1:
                    pick(t - 1, own)

            STEPS = 24
            own = Steps(dve, S["vsteps"])
            tile(0, 0, own)
            tile(1, 1, own)
            n1 = own.n
            with dve.Fori(2, TILES) as t:
                own = Steps(dve, S["vsteps"], dve.snap(t * STEPS + (n1 - 2 * STEPS)))
                tile(t, 2, own)
                assert own.n == STEPS, own.n
            own = Steps(dve, S["vsteps"], n1 + (TILES - 2) * STEPS)
            place(TILES - 2, own)
            gated(TILES - 1, 1)
            scaled(TILES - 1)
            pick(TILES - 1, own)
            place(TILES - 1, own)
            nc.vector.tensor_tensor(K["count"][:], base[:], ff[:, 2, :], ALU.subtract).then_inc(S["table_steps"], 1)


PEELED = 3
MAXB = 2 * SEQ // P + EXPERTS - 1


NP, NP2 = 8, 4


class ExpertWeights:

    def __init__(self, nc, ctx, sem, w1, w3, w2):
        self.w1, self.w3, self.w2 = w1, w3, w2
        self.raw = ctx.enter_context(nc.sbuf_tensor("e_raw", [P, NP, 2 * FF], F32))
        self.raw2 = ctx.enter_context(nc.sbuf_tensor("e_raw2", [P, NP2, D], F32))
        self.loaded = [sem(f"raw_loaded{i}") for i in range(NP // 2)]
        self.loaded2 = [sem(f"raw2_loaded{i}") for i in range(NP2 // 2)]

    def load(self, eng, e, i):
        w, r = (self.w1, i) if i < 2 else (self.w3, i - 2)
        src = w[0, bass.ds(e, 1), r * 4 * P:(r + 1) * 4 * P, :].rearrange("o (k p) f -> p (o k) f", p=P)
        eng.dma_start(self.raw[:, 2 * i:2 * i + 2, :].rearrange("p i (k f) -> p (i k) f", k=2), src
                      ).then_inc(self.loaded[i], 16)

    def load2(self, eng, e, i):
        src = self.w2[0, bass.ds(e, 1), i * 2 * P:(i + 1) * 2 * P, :].rearrange("o (k p) f -> p (o k) f", p=P)
        eng.dma_start(self.raw2[:, 2 * i:2 * i + 2, :], src).then_inc(self.loaded2[i], 16)


def plan_phase(nc, weights, K):
    with ExitStack() as ctx:
        sb = lambda n, s, d=F32: ctx.enter_context(nc.sbuf_tensor(n, s, d))
        sem = semaphores(nc, ctx, "plan_")
        count, ones, tab = K["count"], K["ones"], K["tab"]
        ii, ip = sb("p_ii", [P, EXPERTS], I32), sb("p_ip", [P, 1], I32)
        ex, bl = sb("p_expert", [P, EXPERTS]), sb("p_block", [P, 1])
        t0, ti = sb("p_t0", [P, EXPERTS]), sb("p_ti", [P, EXPERTS], I32)
        nb, inc, exc, last = (sb("p_" + n, [P, EXPERTS]) for n in ("nb", "inc", "exc", "last"))
        own_, scr = sb("p_own", [P, EXPERTS]), sb("p_scr", [P, 5, EXPERTS])
        of = sb("p_of", [P, 5])
        cols = sb("p_cols", [P, 4])
        start, shift = sb("p_start", [P, EXPERTS]), sb("p_shift", [P, EXPERTS])
        pe_, pf = sb("p_pe", [P, 2 * TILES], U32), sb("p_pf", [P, 2 * TILES])
        df, match = sb("p_df", [P, 2 * TILES]), sb("p_match", [P, 2 * TILES, EXPERTS])
        ps = ctx.enter_context(nc.psum_tensor("p_ps", [P, 512], F32))
        consts, steps, turned, cols_ready = sem("consts"), sem("steps"), sem("turned"), sem("cols_ready")
        block = ctx.enter_context(nc.Block())

        @block.sync
        def _(sp):
            for i in range(NP // 2):
                weights.load(sp, 0, i)
            for i in range(NP2 // 2):
                weights.load2(sp, 0, i)

        @block.gpsimd
        def _(pool):
            nc.gpsimd.iota(ii[:], pattern=[[1, EXPERTS]], base=0, channel_multiplier=0).then_inc(consts, 1)
            nc.gpsimd.iota(ip[:], pattern=[[0, 1]], base=0, channel_multiplier=1).then_inc(consts, 1)

        @block.tensor
        def _(pe):
            pe.wait_ge(cols_ready, 1)
            for j in range(4):
                mm = nc.tensor.matmul(ps[0:1, j * P:(j + 1) * P], cols[:, j:j + 1], K["ident"][:],
                                      start=True, stop=True)
            mm.then_inc(turned, 1)

        @block.vector
        def _(dve):
            own = Steps(dve, steps)
            step = lambda ins: (own.add(ins), own.settle())
            ts = nc.vector.tensor_scalar
            dve.wait_ge(consts, 2)
            own.add(nc.vector.tensor_copy(ex[:], ii[:]))
            own.add(nc.vector.tensor_copy(bl[:], ip[:]))
            own.add(ts(last[:], count[:], -float(P), 0.0, ALU.add, ALU.max))
            step(ts(t0[:], count[:], 1.0, float(P - 1), ALU.max, ALU.add))
            step(nc.vector.tensor_copy(ti[:], t0[:]))
            step(ts(ti[:], ti[:], 7, None, ALU.arith_shift_right))
            step(nc.vector.tensor_copy(nb[:], ti[:]))
            step(nc.vector.tensor_tensor_scan(inc[:], ones[:, 0:EXPERTS], nb[:], 0.0, ALU.mult, ALU.add))
            step(nc.vector.tensor_tensor(exc[:], inc[:], nb[:], ALU.subtract))
            own.add(ts(K["more"][:], inc[:, EXPERTS - 1:EXPERTS], -float(PEELED), None, ALU.add))
            own.add(ts(own_[:], exc[:], bl[:], None, ALU.is_le))
            step(ts(t0[:], inc[:], bl[:], None, ALU.is_le))
            step(nc.vector.tensor_tensor(own_[:], own_[:], t0[:], ALU.subtract))
            step(nc.vector.tensor_tensor_scan(start[:], ones[:, 0:EXPERTS], count[:], 0.0, ALU.mult, ALU.add))
            step(nc.vector.tensor_tensor(start[:], start[:], count[:], ALU.subtract))
            for j, v in enumerate((ex, exc, inc, last, start)):
                own.add(nc.vector.tensor_tensor_reduce(out=scr[:, j, :], in0=own_[:], in1=v[:], scale=1.0, scalar=0.0,
                                                       op0=ALU.mult, op1=ALU.add, accum_out=of[:, j:j + 1]))
            own.settle()
            own.add(nc.vector.tensor_copy(cols[:, 0:1], of[:, 0:1]))
            step(nc.vector.tensor_tensor(cols[:, 1:2], bl[:], of[:, 1:2], ALU.subtract))
            step(ts(cols[:, 1:2], cols[:, 1:2], float(P), of[:, 3:4], ALU.mult, ALU.min))
            own.add(nc.vector.tensor_tensor(cols[:, 3:4], cols[:, 1:2], of[:, 4:5], ALU.add))
            step(nc.vector.scalar_tensor_tensor(shift[:], ex[:], -float(REGION), start[:], ALU.mult, ALU.add))
            step(nc.vector.scalar_tensor_tensor(cols[:, 1:2], of[:, 0:1], float(REGION), cols[:, 1:2], ALU.mult, ALU.add))
            step(ts(of[:, 2:3], of[:, 2:3], -1.0, bl[:], ALU.add, ALU.is_equal))
            step(ts(cols[:, 2:3], of[:, 0:1], EXPERTS - 1.5, None, ALU.is_lt))
            step(nc.vector.tensor_tensor(cols[:, 2:3], cols[:, 2:3], of[:, 2:3], ALU.mult))
            nc.vector.memset(scr[:], 0.0).then_inc(cols_ready, 1)
            dve.wait_ge(turned, 1)
            own.add(nc.vector.tensor_copy(tab[:].rearrange("p q b -> p (q b)"), ps[0:1, :]))
            step(ts(pe_[:], K["dest"][:], REGION.bit_length() - 1, None, ALU.logical_shift_right))
            own.add(nc.vector.tensor_copy(pf[:], pe_[:]))
            step(nc.vector.tensor_copy(df[:], K["dest"][:]))
            wide = lambda a: a.unsqueeze(1).broadcast_to([P, 2 * TILES, EXPERTS])
            step(nc.vector.tensor_tensor(match[:], pf[:].unsqueeze(2).broadcast_to([P, 2 * TILES, EXPERTS]), wide(ex[:]),
                                         ALU.is_equal))
            step(nc.vector.tensor_tensor(match[:], match[:], wide(shift[:]), ALU.mult))
            step(nc.vector.tensor_reduce(pf[:], match[:], AX, ALU.add))
            step(nc.vector.tensor_tensor(df[:], df[:], pf[:], ALU.add))
            own.add(nc.vector.tensor_copy(K["dest"][:], df[:]))


def experts_phase(nc, weights, xs, ys, K):
    EXPERT, ROW, NEXT, OUT = range(4)
    with ExitStack() as ctx:
        sb = lambda n, s, d=F32: ctx.enter_context(nc.sbuf_tensor(n, s, d))
        psum = lambda n: ctx.enter_context(nc.psum_tensor(n, [P, 512], F32))
        sem = semaphores(nc, ctx, "experts_")
        ident, tab = K["ident"], K["tab"]
        wh = [sb(f"wh{i}", [P, NP, 2, FF], F32R) for i in range(2)]
        wy = [sb(f"wy{i}", [P, KF, D], F32R) for i in range(2)]
        wraw, wraw2, raw_loaded, raw2_loaded = weights.raw, weights.raw2, weights.loaded, weights.loaded2
        xb = sb("xb", [P, D])
        xT = [sb(f"xT{i}", [P, KD, P], F32R) for i in range(2)]
        sg, hb = sb("sg", [P, FF]), sb("hb", [P, FF])
        hT = [sb(f"e_hT{i}", [P, FF], F32R) for i in range(2)]
        ob = sb("ob", [P, D])
        flat = lambda a: a.rearrange("p a b -> p (a b)")
        psX = [psum("psX0"), psum("psX1")]
        ps1, ps3, psH = psum("ps1"), psum("ps3"), psum("psHt")
        psO = [psum("psO0"), psum("psO1")]
        NAMES = ("high", "low", "low2", "used", "used2", "x_loaded", "x_turned", "x_high", "x_low", "silu", "h_ready",
                 "h_turned", "h_high", "h_low", "out0", "out1", "out_stored", "high2", "passed")
        S = {n: sem(n) for n in NAMES}
        block = ctx.enter_context(nc.Block())

        def entry(eng, what, b, top=None):
            top = top or (EXPERTS - 1, (EXPERTS - 1) * REGION + SEQ - P, 1, 2 * SEQ)[what]
            return eng.value_load(tab[0:1, what, bass.ds(b, 1)], min_val=0, max_val=top)

        def blocks(eng, run):
            nb = eng.value_load(K["more"][0:1, 0:1], min_val=EXPERTS - PEELED, max_val=MAXB - PEELED) + PEELED
            for b in range(PEELED):
                run(b, b)
            with eng.Fori(PEELED, nb) as b:
                run(b, PEELED)
            return nb

        @block.sync
        def _(sp):
            def load_w(e):
                for i in range(NP // 2):
                    sp.wait_ge(S["low"], e * NP + (2 * i + 2 - NP))
                    sp.sem_inc(S["passed"], 1)
                    weights.load(sp, e, i)

            def load_w2(e):
                for i in range(NP2 // 2):
                    sp.wait_ge(S["low2"], e * NP2 + (2 * i + 2 - NP2))
                    sp.sem_inc(S["passed"], 1)
                    weights.load2(sp, e, i)

            load_w(1)
            with sp.Fori(1, EXPERTS - 1) as e:
                load_w(e + 1)
                load_w2(e)
            load_w2(EXPERTS - 1)

        @block.gpsimd
        def _(pool):
            def store(j, n):
                pool.wait_ge(S["out0"], j + 1)
                pool.wait_ge(S["out1"], j + 1)
                pool.sem_inc(S["passed"], 1)
                pool.dma_start(ys[bass.ds(entry(pool, OUT, j), P), :], ob[:]).then_inc(S["out_stored"], 16)

            def run(b, n):
                if n:
                    pool.wait_ge(S["x_turned"], b)
                    pool.sem_inc(S["passed"], 1)
                pool.dma_start(xb[:], xs[bass.ds(entry(pool, ROW, b), P), :]).then_inc(S["x_loaded"], 16)
                if n == 3:
                    store(b - 3, n)

            nb = blocks(pool, run)
            for j in range(3):
                store(nb + (j - 3), 3)
            pool.wait_ge(S["out_stored"], nb * 16)
            pool.sem_inc(S["passed"], 1)

        def following(eng, b):
            return entry(eng, NEXT, b), eng.snap(entry(eng, EXPERT, b) + 1)

        @block.scalar
        def _(act):
            def pieces(e, b=None):
                for i in range(NP):
                    act.wait_ge(raw_loaded[i // 2], e * 16 + 16)
                    if b is not None:
                        act.wait_ge(S["used"], b * NP + (i + 1))
                    nc.scalar.copy(flat(wh[0][:, i]), wraw[:, i, :]).then_inc(S["high"], 1)

            def pieces2(e):
                for i in range(NP2):
                    act.wait_ge(raw2_loaded[i // 2], e * 16 + 16)
                    nc.scalar.copy(wy[0][:, i, :], wraw2[:, i, :]).then_inc(S["high2"], 1)

            def out(j, n):
                act.wait_ge(S["used2"], j * NP2 + NP2)
                if n:
                    act.wait_ge(S["out_stored"], j * 16)
                nc.scalar.copy(ob[:, 0:512], psO[0][:]).then_inc(S["out0"], 1)

            def h_high(j):
                act.wait_ge(S["h_turned"], j + 1)
                nc.scalar.copy(hT[0][:], psH[:]).then_inc(S["h_high"], 1)

            def run(b, n):
                if n >= 2:
                    w2_is_last, w2_e = following(act, b - 2)
                act.wait_ge(S["x_turned"], b + 1)
                if n:
                    act.wait_ge(S["used"], b * NP)
                for i in range(2):
                    last = nc.scalar.copy(flat(xT[0][:, 4 * i:4 * i + 4]), psX[i][:])
                last.then_inc(S["x_high"], 1)
                if n >= 2:
                    out(b - 2, n - 2)
                if n >= 1:
                    h_high(b - 1)
                if n >= 2:
                    with act.If(w2_is_last == 1):
                        pieces2(w2_e)
                is_last, e = following(act, b)
                act.wait_ge(S["used"], b * NP + 4)
                if n:
                    act.wait_ge(S["h_ready"], b)
                nc.scalar.activation(sg[:], ps1[:], ACT.Silu).then_inc(S["silu"], 1)
                with act.If(is_last == 1):
                    pieces(e, b)

            pieces(0)
            pieces2(0)
            nb = blocks(act, run)
            out(nb - 2, 3)
            h_high(nb - 1)
            is_last, e = following(act, nb - 2)
            with act.If(is_last == 1):
                pieces2(e)
            out(nb - 1, 3)

        @block.tensor
        def _(pe):
            def turn(b, n):
                pe.wait_ge(S["x_loaded"], b * 16 + 16)
                if n:
                    pe.wait_ge(S["x_low"], b)
                for k in range(KD):
                    mm = nc.tensor.transpose(psX[k // 4][:, (k % 4) * P:(k % 4 + 1) * P], xb[:, k * P:(k + 1) * P], ident[:])
                mm.then_inc(S["x_turned"], 1)

            def first_products(b, n):
                e8 = pe.snap(entry(pe, EXPERT, b) * NP)
                pe.wait_ge(S["x_low"], b + 1)
                if n:
                    pe.wait_ge(S["h_ready"], b)
                for i in range(NP):
                    ps, r = (ps1, i) if i < 4 else (ps3, i - 4)
                    pe.wait_ge(S["low"], e8 + (i + 1))
                    for k in range(2):
                        for l, w in ((1, 0), (0, 1), (0, 0)):
                            mm = nc.tensor.matmul(ps[:], xT[l][:, 2 * r + k, :], wh[w][:, i, k, :],
                                                  start=(r == 0 and k == 0 and l == 1),
                                                  stop=(r == 3 and k == 1 and l == 0 and w == 0))
                    mm.then_inc(S["used"], 1)

            def second_product(j, n):
                e4 = pe.snap(entry(pe, EXPERT, j) * NP2)
                pe.wait_ge(S["h_low"], j + 1)
                if n:
                    pe.wait_ge(S["out0"], j)
                    pe.wait_ge(S["out1"], j)
                for k in range(KF):
                    pe.wait_ge(S["low2"], e4 + (k + 1))
                    for o in range(2):
                        for l, w in ((1, 0), (0, 1), (0, 0)):
                            mm = nc.tensor.matmul(psO[o][:], hT[l][:, k * P:(k + 1) * P], wy[w][:, k, o * 512:(o + 1) * 512],
                                                  start=(k == 0 and l == 1), stop=(k == KF - 1 and l == 0 and w == 0))
                    mm.then_inc(S["used2"], 1)

            def turn_h(j):
                pe.wait_ge(S["h_ready"], j + 1)
                for k in range(KF):
                    mm = nc.tensor.transpose(psH[:, k * P:(k + 1) * P], hb[:, k * P:(k + 1) * P], ident[:])
                mm.then_inc(S["h_turned"], 1)

            def run(b, n):
                turn(b, n)
                if n >= 2:
                    second_product(b - 2, n - 2)
                if n >= 1:
                    turn_h(b - 1)
                first_products(b, n)

            nb = blocks(pe, run)
            second_product(nb - 2, 3)
            turn_h(nb - 1)
            second_product(nb - 1, 3)

        @block.vector
        def _(dve):
            def pieces(e, which):
                for i in which:
                    dve.wait_ge(S["high"], e * NP + (i + 1))
                    nc.vector.tensor_tensor(flat(wh[1][:, i]), wraw[:, i, :], flat(wh[0][:, i]).bitcast(F32), ALU.subtract
                                            ).then_inc(S["low"], 1)

            def pieces2(e):
                for i in range(NP2):
                    dve.wait_ge(S["high2"], e * NP2 + (i + 1))
                    nc.vector.tensor_tensor(wy[1][:, i, :], wraw2[:, i, :], wy[0][:, i, :].bitcast(F32), ALU.subtract
                                            ).then_inc(S["low2"], 1)

            def out(j, n):
                dve.wait_ge(S["used2"], j * NP2 + NP2)
                if n:
                    dve.wait_ge(S["out_stored"], j * 16)
                nc.vector.tensor_copy(ob[:, 512:1024], psO[1][:]).then_inc(S["out1"], 1)

            def h_low(j):
                dve.wait_ge(S["h_high"], j + 1)
                nc.vector.tensor_tensor(hT[1][:], psH[:], hT[0][:].bitcast(F32), ALU.subtract).then_inc(S["h_low"], 1)

            def run(b, n):
                if n >= 2:
                    w2_is_last, w2_e = following(dve, b - 2)
                dve.wait_ge(S["x_high"], b + 1)
                for i in range(2):
                    last = nc.vector.tensor_tensor(flat(xT[1][:, 4 * i:4 * i + 4]), psX[i][:],
                                                   flat(xT[0][:, 4 * i:4 * i + 4]).bitcast(F32), ALU.subtract)
                last.then_inc(S["x_low"], 1)
                if n >= 2:
                    out(b - 2, n - 2)
                if n >= 1:
                    h_low(b - 1)
                if n >= 2:
                    with dve.If(w2_is_last == 1):
                        pieces2(w2_e)
                is_last, e = following(dve, b)
                with dve.If(is_last == 1):
                    pieces(e, range(NP // 2))
                dve.wait_ge(S["silu"], b + 1)
                dve.wait_ge(S["used"], b * NP + NP)
                if n:
                    dve.wait_ge(S["h_turned"], b)
                nc.vector.tensor_tensor(hb[:], sg[:], ps3[:], ALU.mult).then_inc(S["h_ready"], 1)
                with dve.If(is_last == 1):
                    pieces(e, range(NP // 2, NP))

            pieces(0, range(NP))
            pieces2(0)
            nb = blocks(dve, run)
            out(nb - 2, 3)
            h_low(nb - 1)
            is_last, e = following(dve, nb - 2)
            with dve.If(is_last == 1):
                pieces2(e)
            out(nb - 1, 3)


def final_phase(nc, final_w, x1dram, ys, outd, K):
    NS = 4
    PER = 16 // NS
    with ExitStack() as ctx:
        sb = lambda n, s, d=F32: ctx.enter_context(nc.sbuf_tensor(n, s, d))
        sem = semaphores(nc, ctx, "final_")
        dest, gates = K["dest"], K["gates"]
        r = [[sb(f"r{i}{j}", [P, D]) for j in range(2)] for i in range(NS)]
        x1 = [sb(f"fx{i}", [P, D]) for i in range(NS)]
        sq = [sb(f"fsq{i}", [P, D]) for i in range(NS)]
        fo = [sb(f"fo{i}", [P, D]) for i in range(NS)]
        g2row, fw = sb("g2row", [P, D]), sb("fw", [P, D])
        di = [sb(f"di{i}", [P, 2], U32) for i in range(NS)]
        gi = [sb(f"gi{i}", [P, 2]) for i in range(NS)]
        st = [sb(f"fst{i}", [P, 4]) for i in range(NS)]
        minus_half, eps = sb("f_minus_half", [P, 1]), sb("f_eps", [P, 1])
        ps = [ctx.enter_context(nc.psum_tensor(f"f_ps{i}", [P, 512], F32)) for i in range(2)]
        NAMES = ("rows_done", "rows_copied", "w_loaded", "index", "scaled", "mixed", "gated", "added", "squared", "mean",
                 "rstd", "normed", "consts", "passed")
        S = {n: sem(n) for n in NAMES}
        gathered = [sem(f"gathered{i}") for i in range(NS)]
        x_loaded = [sem(f"x_loaded{i}") for i in range(NS)]
        stored = [sem(f"stored{i}") for i in range(NS)]
        block = ctx.enter_context(nc.Block())

        def tiles(eng, run):
            for i in range(NS):
                run(i, i, i - 1 if i else None, 0, True)
            with eng.Fori(1, TILES // NS - 1) as p:
                for i in range(NS):
                    run(p * NS + i, i, (i - 1) % NS, 1, True)
            for i in range(NS):
                run(TILES - NS + i, i, (i - 1) % NS, 1, False)

        @block.sync
        def _(sp):
            sp.dma_start(fw[:], final_w.rearrange("(o d) -> o d", o=1).broadcast_to([P, D])).then_inc(S["w_loaded"], 16)

            def load(t, i, before, n, more):
                if n:
                    sp.wait_ge(S["normed"], t - NS + 1)
                sp.dma_start(x1[i][:], x1dram[bass.ds(t * P, P), :]).then_inc(x_loaded[i], 16)

            tiles(sp, load)

        @block.gpsimd
        def _(pool):
            nc.gpsimd.memset(minus_half[:], -0.5).then_inc(S["consts"], 1)
            nc.gpsimd.memset(eps[:], EPS).then_inc(S["consts"], 1)
            pool.wait_ge(S["consts"], 2)

            def gather(t, i, n):
                pool.wait_ge(S["index"], t + 1)
                if n:
                    pool.wait_ge(S["added"], t - NS + 1)
                pool.sem_inc(S["passed"], 1)
                for j in range(2):
                    nc.gpsimd.indirect_dma_start(r[i][j][:], None, ys[0:2 * SEQ, :],
                                                 bass.IndirectOffsetOnAxis(ap=di[i][:, j:j + 1], axis=0)).then_inc(gathered[i], 16)

            def add(t, i):
                pool.wait_ge(x_loaded[i], (t - i) * PER + 16)
                pool.wait_ge(S["gated"], t + 1)
                nc.gpsimd.tensor_tensor(x1[i][:], x1[i][:], r[i][0][:], ALU.add).then_inc(S["added"], 1)

            def rstd(t, i):
                pool.wait_ge(S["squared"], t + 1)
                nc.gpsimd.tensor_tensor(st[i][:, 1:2], st[i][:, 0:1], eps[:], ALU.add).then_inc(S["mean"], 1)
                pool.wait_ge(S["mean"], t + 1)
                nc.gpsimd.tensor_tensor(st[i][:, 2:3], st[i][:, 1:2], minus_half[:], ALU.pow).then_inc(S["rstd"], 1)

            def run(t, i, before, n, more):
                if before is not None:
                    rstd(t - 1, before)
                add(t, i)
                if more:
                    gather(t + NS, i, 1)

            for i in range(NS):
                gather(i, i, 0)
            tiles(pool, run)
            rstd(TILES - 1, NS - 1)

        @block.scalar
        def _(act):
            def scale(t, i):
                act.wait_ge(gathered[i], (t - i) * 2 * PER + 32)
                nc.scalar.activation(r[i][0][:], r[i][0][:], ACT.Copy, scale=gi[i][:, 0:1]).then_inc(S["scaled"], 1)

            def square(t, i):
                act.wait_ge(S["added"], t + 1)
                nc.scalar.activation(sq[i][:], x1[i][:], ACT.Square, scale=D ** -0.5, accum_out=st[i][:, 0:1]
                                     ).then_inc(S["squared"], 1)

            def store(t, i):
                act.wait_ge(S["normed"], t + 1)
                act.sem_inc(S["passed"], 1)
                act.dma_start(outd[0, bass.ds(t * P, P), :], fo[i][:]).then_inc(stored[i], 16)

            def run(t, i, before, n, more):
                scale(t, i)
                if before is not None:
                    square(t - 1, before)
                if n or i >= 2:
                    store(t - 2, (i - 2) % NS)

            tiles(act, run)
            square(TILES - 1, NS - 1)
            store(TILES - 2, NS - 2)
            store(TILES - 1, NS - 1)
            for i in range(NS):
                act.wait_ge(stored[i], TILES * PER)

        @block.tensor
        def _(pe):
            for i in range(2):
                for k in range(4):
                    o = 5 * KD + 4 * i + k
                    mm = nc.tensor.matmul(ps[i][:, k * P:(k + 1) * P], K["mod"][:, o:o + 1].broadcast_to([P, P]),
                                          K["ident"][:], start=True, stop=True)
                mm.then_inc(S["rows_done"], 1)

        @block.vector
        def _(dve):
            def index(t, i, n):
                if n:
                    dve.wait_ge(S["mixed"], t - NS + 1)
                    dve.wait_ge(gathered[i], (t - i) * 2 * PER)
                    dve.sem_inc(S["passed"], 1)
                nc.vector.tensor_copy(gi[i][:], gates[:, bass.ds(t * 2, 2)])
                nc.vector.tensor_copy(di[i][:], dest[:, bass.ds(t * 2, 2)]).then_inc(S["index"], 1)

            def mix(t, i):
                dve.wait_ge(S["scaled"], t + 1)
                nc.vector.scalar_tensor_tensor(r[i][0][:], r[i][1][:], gi[i][:, 1:2], r[i][0][:], ALU.mult, ALU.add
                                               ).then_inc(S["mixed"], 1)
                dve.wait_ge(S["mixed"], t + 1)
                nc.vector.tensor_tensor(r[i][0][:], r[i][0][:], g2row[:], ALU.mult).then_inc(S["gated"], 1)

            def norm(t, i, n):
                dve.wait_ge(S["rstd"], t + 1)
                if n:
                    dve.wait_ge(stored[i], (t - i) * PER)
                nc.vector.scalar_tensor_tensor(fo[i][:], x1[i][:], st[i][:, 2:3], fw[:], ALU.mult, ALU.mult
                                               ).then_inc(S["normed"], 1)

            def run(t, i, before, n, more):
                mix(t, i)
                if more:
                    index(t + NS, i, 1)
                if before is not None:
                    norm(t - 1, before, n)

            for i in range(NS):
                index(i, i, 0)
            for i in range(2):
                dve.wait_ge(S["rows_done"], i + 1)
                nc.vector.tensor_copy(g2row[:, i * 512:(i + 1) * 512], ps[i][:]).then_inc(S["rows_copied"], 1)
            dve.wait_ge(S["rows_copied"], 2)
            dve.wait_ge(S["w_loaded"], 16)
            tiles(dve, run)
            norm(TILES - 1, NS - 1, 1)


def build(nc, a, out, xs, ydram, x1dram, ys):
    with ExitStack() as ctx:
        sb = lambda n, s, d=F32: ctx.enter_context(nc.sbuf_tensor(n, s, d))
        keep = lambda *which: {n: sb("k_" + n, s, d) for n, s, d in which}
        K = keep(
            ("ident", [P, P], F32), ("upper", [P, P], F32), ("ones", [P, P], F32), ("mask", [P, P], F32),
            ("identb", [P, P], BF16), ("maskb", [P, P], BF16), ("strictb", [P, P], BF16), ("onesb", [P, P], BF16),
            ("mod", [P, 6 * KD], F32), ("a1", [P, KD], F32), ("a2", [P, KD], F32),
            ("conv", [P, TAPS + 1, CB], F32))
        mod_phase(nc, a["c"], a["ada_w"], a["ada_b"], a["norm_mix_w"], a["norm_ffn_w"], a["ssm_conv_w"],
                  a["ssm_conv_b"], K)
        mixer_phase(nc, a["x"], a["ssm_in_w"], a["ssm_dt_bias"], a["ssm_a_log"], a["ssm_d"], a["ssm_norm_w"], ydram,
                    xs, K)
        K.update(keep(
            ("dest", [P, 2 * TILES], U32), ("gates", [P, 2 * TILES], F32), ("count", [P, EXPERTS], F32),
            ("tab", [1, 4, P], I32), ("more", [P, 1], I32)))
        out_phase(nc, a["x"], a["ssm_out_w"], a["moe_group_w"], a["moe_group_b"], a["moe_expert_w"],
                  a["moe_expert_b"], ydram, x1dram, xs, K)
        with ExitStack() as both:
            weights = ExpertWeights(nc, both, semaphores(nc, both, "weights_"), a["moe_w1"], a["moe_w3"], a["moe_w2"])
            plan_phase(nc, weights, K)
            experts_phase(nc, weights, xs, ys, K)
        final_phase(nc, a["final_norm_w"], x1dram, ys, out, K)


USED = ("x", "c", "ada_w", "ada_b", "norm_mix_w", "norm_ffn_w", "ssm_in_w", "ssm_conv_w", "ssm_conv_b", "ssm_dt_bias",
        "ssm_a_log", "ssm_d", "ssm_norm_w", "ssm_out_w", "moe_group_w", "moe_group_b", "moe_expert_w", "moe_expert_b",
        "moe_w1", "moe_w3", "moe_w2", "final_norm_w")


def kernel(**inputs):
    import numpy as np
    import concourse.bacc as bacc
    from concourse.bass_utils import run_bass_kernel_spmd

    nc = bacc.Bacc("TRN2", target_bir_lowering=False, num_devices=1)
    arrays, args = {}, {}
    for name in USED:
        arrays[f"in_{name}"] = np.ascontiguousarray(inputs[name])
        args[name] = nc.dram_tensor(f"in_{name}", arrays[f"in_{name}"].shape, F32, kind="ExternalInput").ap()
    out = nc.dram_tensor("out", (1, SEQ, D), F32, kind="ExternalOutput").ap()
    scratch = lambda name, shape: nc.dram_tensor(name, shape, F32, kind="Internal").ap()
    build(nc, args, out, scratch("xs", (EXPERTS * REGION, D)), scratch("y_inner", (SEQ, DI)),
          scratch("x1", (SEQ, D)), scratch("ys", (2 * SEQ + P, D)))
    r = run_bass_kernel_spmd(nc, [arrays], core_ids=[0])
    return r.results[0]["out"]
```
